# Optimizing a Trainium2 kernel written in Bass

```python
import jax, jax.numpy as jnp
from jax import lax
import numpy as np
import jax
import jax.numpy as jnp

D_MODEL = 1024
BATCH = 1
SEQ = 256
DEPTH = 2

CHUNK = 64
HEAD_DIM = 64
SWA_HEADS = 8
SWA_KV_HEADS = 2
SWA_GROUP = SWA_HEADS // SWA_KV_HEADS
SWA_WINDOW = 128
SWA_WIN_CHUNKS = (SWA_WINDOW + CHUNK - 1) // CHUNK
RWKV_HEADS = 4
RWKV_W_RANK = 64
RWKV_A_RANK = 64
RWKV_G_RANK = 128
RWKV_GN_EPS = 64e-5
FOX_HEADS = 4
FOX_BLOCK = 128
DSA_HEADS = 4
IDX_HEADS = 4
IDX_DIM = 64
DSA_TOPK_MAX = 256
DSA_BLOCK = 128
D_FF = 2816
N_EXPERTS = 8
TOP_K = 2
D_FF_EXPERT = 1408
N_DENSE = (DEPTH + 1) // 2
N_MOE = DEPTH // 2
N_BRANCHES = 4
DN_ALPHA = (2 * DEPTH) ** 0.25
DN_BETA = (8 * DEPTH) ** -0.25
LN_EPS = 1e-5
ATTN_SCALE = HEAD_DIM ** -0.5
IDX_SCALE = IDX_DIM ** -0.5
IDX_W_SCALE = IDX_HEADS ** -0.5

SWA_Q = SWA_HEADS * HEAD_DIM
SWA_KV = SWA_KV_HEADS * HEAD_DIM
RWKV_W = RWKV_HEADS * HEAD_DIM
FOX_W = FOX_HEADS * HEAD_DIM
DSA_W = DSA_HEADS * HEAD_DIM
MIX_WIDTHS = (SWA_Q, RWKV_W, FOX_W, DSA_W)
MIX_WIDTH = SWA_Q + RWKV_W + FOX_W + DSA_W
SWA_SPLITS = (SWA_Q, SWA_KV, SWA_KV)
RWKV_SPLITS = (RWKV_W, RWKV_W, RWKV_W, RWKV_W_RANK, RWKV_A_RANK, RWKV_G_RANK)
FOX_SPLITS = (FOX_W, FOX_W, FOX_W, FOX_HEADS)
DSA_SPLITS = (DSA_W, HEAD_DIM, HEAD_DIM, IDX_HEADS * IDX_DIM, IDX_DIM, IDX_HEADS)
RWKV_IN = sum(RWKV_SPLITS)
GATE_COLS = N_BRANCHES * D_MODEL
IN_GROUPS = (sum(SWA_SPLITS), RWKV_IN, sum(FOX_SPLITS), sum(DSA_SPLITS), GATE_COLS)
D_IN = sum(IN_GROUPS)


def split_cols(t, sizes, axis=-1):
    idx = [int(i) for i in np.cumsum(sizes)[:-1]]
    return jnp.split(t, idx, axis=axis)

def layer_norm(x, g, b):
    xf = x.astype(jnp.float32)
    mu = jnp.mean(xf, axis=-1, keepdims=True)
    var = jnp.mean(jnp.square(xf - mu), axis=-1, keepdims=True)
    return ((xf - mu) * lax.rsqrt(var + LN_EPS) * g + b).astype(x.dtype)

def swa_branch(q, k, v, sinks):
    B, S, _ = q.shape
    nc = S // CHUNK
    W = SWA_WIN_CHUNKS
    q = q.reshape(B, nc, CHUNK, SWA_KV_HEADS, SWA_GROUP, HEAD_DIM)
    pad = ((0, 0), (W, 0), (0, 0), (0, 0), (0, 0))
    kp = jnp.pad(k.reshape(B, nc, CHUNK, SWA_KV_HEADS, HEAD_DIM), pad)
    vp = jnp.pad(v.reshape(B, nc, CHUNK, SWA_KV_HEADS, HEAD_DIM), pad)
    kb = jnp.concatenate([kp[:, j:j + nc] for j in range(W + 1)], axis=2)
    vb = jnp.concatenate([vp[:, j:j + nc] for j in range(W + 1)], axis=2)
    key_chunk = jnp.arange(nc)[:, None] - W + jnp.arange(W + 1)[None, :]
    valid = jnp.repeat(key_chunk >= 0, CHUNK, axis=1)
    logits = jnp.einsum('bcqhgd,bckhd->bchgqk', q, kb).astype(jnp.float32) * ATTN_SCALE
    logits = jnp.where(valid[None, :, None, None, None, :], logits, -jnp.inf)
    sink = sinks.astype(jnp.float32).reshape(1, 1, SWA_KV_HEADS, SWA_GROUP, 1, 1)
    m = jnp.maximum(jnp.max(logits, axis=-1, keepdims=True), sink)
    e = jnp.exp(logits - m)
    p = e / (jnp.sum(e, axis=-1, keepdims=True) + jnp.exp(sink - m))
    o = jnp.einsum('bchgqk,bckhd->bcqhgd', p.astype(v.dtype), vb)
    return o.reshape(B, S, SWA_Q)

def rwkv7_branch(p, mu, w0, w_up, a0, a_up, g_up, k_k, k_a, r_k, gn_g, gn_b):
    B, S, _ = p.shape
    p_prev = jnp.pad(p[:, :-1], ((0, 0), (1, 0), (0, 0)))
    p = p + mu * (p_prev - p)
    r, k, v, w_lo, a_lo, g_lo = split_cols(p, RWKV_SPLITS)
    log_w = -jnp.exp(-jax.nn.softplus(-(w0 + jnp.tanh(w_lo) @ w_up).astype(jnp.float32)) - 0.5)
    a = jax.nn.sigmoid(a0 + a_lo @ a_up)
    g = jax.nn.sigmoid(g_lo) @ g_up
    hd = lambda t: t.reshape(B, S, RWKV_HEADS, HEAD_DIM).astype(jnp.float32)
    kk = hd(k * k_k)
    kk = kk * lax.rsqrt(jnp.sum(kk * kk, axis=-1, keepdims=True) + 1e-12)
    k = k * (1.0 + (a - 1.0) * k_a)
    r_h, k_h, v_h, a_h, w_h = hd(r), hd(k), hd(v), hd(a), hd(jnp.exp(log_w))
    seq = tuple(jnp.moveaxis(t, 1, 0) for t in (r_h, w_h, k_h, v_h, kk, a_h))

    def step(state, inp):
        r_t, w_t, k_t, v_t, kk_t, a_t = inp
        sa = jnp.einsum('bhvk,bhk->bhv', state, -kk_t)
        state = (state * w_t[:, :, None, :]
                 + sa[..., None] * (kk_t * a_t)[:, :, None, :]
                 + v_t[..., None] * k_t[:, :, None, :])
        return state, jnp.einsum('bhvk,bhk->bhv', state, r_t)

    s0 = jnp.zeros((B, RWKV_HEADS, HEAD_DIM, HEAD_DIM), jnp.float32)
    _, y = lax.scan(step, s0, seq)
    y = jnp.moveaxis(y, 0, 1)
    ym = jnp.mean(y, axis=-1, keepdims=True)
    yv = jnp.mean(jnp.square(y - ym), axis=-1, keepdims=True)
    y = ((y - ym) * lax.rsqrt(yv + RWKV_GN_EPS)).reshape(B, S, RWKV_W) * gn_g + gn_b
    bonus = (jnp.sum(r_h * k_h * r_k, axis=-1, keepdims=True) * v_h).reshape(B, S, RWKV_W)
    return ((y + bonus) * g).astype(p.dtype)

def fox_branch(q, k, v, f_logit, f_bias):
    B, S, _ = q.shape
    q = q.reshape(B, S, FOX_HEADS, HEAD_DIM)
    k = k.reshape(B, S, FOX_HEADS, HEAD_DIM)
    v = v.reshape(B, S, FOX_HEADS, HEAD_DIM)
    log_f = jax.nn.log_sigmoid(f_logit.astype(jnp.float32) + f_bias)
    c = jnp.cumsum(log_f, axis=1).transpose(0, 2, 1)
    outs = []
    for blk in range(S // FOX_BLOCK):
        lo, hi = blk * FOX_BLOCK, (blk + 1) * FOX_BLOCK
        logits = jnp.einsum('bqhd,bkhd->bhqk', q[:, lo:hi], k[:, :hi]).astype(jnp.float32) * ATTN_SCALE
        logits = logits + c[:, :, lo:hi, None] - c[:, :, None, :hi]
        causal = jnp.arange(lo, hi)[:, None] >= jnp.arange(hi)[None, :]
        logits = jnp.where(causal, logits, -jnp.inf)
        p = jax.nn.softmax(logits, axis=-1)
        outs.append(jnp.einsum('bhqk,bkhd->bqhd', p.astype(v.dtype), v[:, :hi]))
    return jnp.concatenate(outs, axis=1).reshape(B, S, FOX_W)

def dsa_branch(q, k, v, q_idx, k_idx, w_idx):
    B, S, _ = q.shape
    topk = min(DSA_TOPK_MAX, S // 4)
    nb = S // DSA_BLOCK
    qT = jnp.moveaxis(q.reshape(B, nb, DSA_BLOCK, DSA_HEADS, HEAD_DIM), 1, 0)
    qiT = jnp.moveaxis(q_idx.reshape(B, nb, DSA_BLOCK, IDX_HEADS, IDX_DIM), 1, 0)
    wiT = jnp.moveaxis(w_idx.reshape(B, nb, DSA_BLOCK, IDX_HEADS), 1, 0)
    key_chunk = jnp.arange(S) // CHUNK

    def block(args):
        blk, qb, qib, wib = args
        t = blk * DSA_BLOCK + jnp.arange(DSA_BLOCK)
        admissible = key_chunk[None, :] <= (t // CHUNK)[:, None]
        rel = jax.nn.relu(jnp.einsum('bqhd,bsd->bqhs', qib, k_idx) * IDX_SCALE)
        score = jnp.einsum('bqhs,bqh->bqs', rel, wib * IDX_W_SCALE).astype(jnp.float32)
        score = jnp.where(admissible[None], score, -jnp.inf)
        top_val, top_idx = lax.top_k(score, topk)
        valid = jnp.isfinite(top_val)
        k_sel = jax.vmap(lambda kk, ii: kk[ii])(k, top_idx)
        v_sel = jax.vmap(lambda vv, ii: vv[ii])(v, top_idx)
        logits = jnp.einsum('bqhd,bqkd->bqhk', qb, k_sel).astype(jnp.float32) * ATTN_SCALE
        logits = jnp.where(valid[:, :, None, :], logits, -jnp.inf)
        p = jax.nn.softmax(logits, axis=-1)
        return jnp.einsum('bqhk,bqkd->bqhd', p.astype(v.dtype), v_sel)

    outs = lax.map(block, (jnp.arange(nb), qT, qiT, wiT))
    return jnp.moveaxis(outs, 0, 1).reshape(B, S, DSA_W)

def mixer_block(x, w_in, sinks, mu, w0, w_up, a0, a_up, g_up, k_k, k_a, r_k, gn_g, gn_b,
                f_bias, gate_bias, w_branch, w_out):
    B, S, _ = x.shape
    p_swa, p_rwkv, p_fox, p_dsa, p_gate = split_cols(x @ w_in, IN_GROUPS)
    o_swa = swa_branch(*split_cols(p_swa, SWA_SPLITS), sinks)
    o_rwkv = rwkv7_branch(p_rwkv, mu, w0, w_up, a0, a_up, g_up, k_k, k_a, r_k, gn_g, gn_b)
    o_fox = fox_branch(*split_cols(p_fox, FOX_SPLITS), f_bias)
    o_dsa = dsa_branch(*split_cols(p_dsa, DSA_SPLITS))
    gates = jax.nn.sigmoid(p_gate.reshape(B, S, N_BRANCHES, D_MODEL) + gate_bias)
    w_rows = split_cols(w_branch, MIX_WIDTHS, axis=0)
    merged = jnp.zeros_like(x)
    for i, (o, w) in enumerate(zip((o_swa, o_rwkv, o_fox, o_dsa), w_rows)):
        merged = merged + gates[:, :, i] * (o @ w)
    return merged @ w_out

def swiglu(x, w1, w3, w2):
    return (jax.nn.silu(x @ w1) * (x @ w3)) @ w2

def moe_ffn(x, router_w, router_b, w1, w3, w2):
    logits = (x @ router_w).astype(jnp.float32) + router_b
    top_val, top_idx = lax.top_k(logits, TOP_K)
    weights = jax.nn.softmax(top_val, axis=-1)
    combine = jnp.sum(jax.nn.one_hot(top_idx, N_EXPERTS, dtype=jnp.float32) * weights[..., None], axis=-2)
    y = jnp.zeros_like(x)
    for e in range(N_EXPERTS):
        y = y + combine[..., e:e + 1].astype(x.dtype) * swiglu(x, w1[e], w3[e], w2[e])
    return y

def first_inputs(seed: int = 0) -> dict:
    key = jax.random.key(seed)
    ks = iter(jax.random.split(key, 32))
    nrm = lambda shape, scale: scale * jax.random.normal(next(ks), shape, jnp.float32)
    unif = lambda shape, lo, hi: jax.random.uniform(next(ks), shape, jnp.float32, lo, hi)
    L = DEPTH
    return {
        'x': nrm((BATCH, SEQ, D_MODEL), 1.0),
        'w_in': nrm((L, D_MODEL, D_IN), D_MODEL ** -0.5),
        'swa_sinks': nrm((L, SWA_HEADS), 0.5),
        'rwkv_mu': unif((L, RWKV_IN), 0.0, 1.0),
        'rwkv_w0': unif((L, RWKV_W), -6.0, 1.0),
        'rwkv_w_up': nrm((L, RWKV_W_RANK, RWKV_W), 0.1),
        'rwkv_a0': nrm((L, RWKV_W), 0.1),
        'rwkv_a_up': nrm((L, RWKV_A_RANK, RWKV_W), RWKV_A_RANK ** -0.5),
        'rwkv_g_up': nrm((L, RWKV_G_RANK, RWKV_W), RWKV_G_RANK ** -0.5),
        'rwkv_k_k': 0.85 + nrm((L, RWKV_W), 0.05),
        'rwkv_k_a': 1.0 + nrm((L, RWKV_W), 0.05),
        'rwkv_r_k': nrm((L, RWKV_HEADS, HEAD_DIM), 0.1),
        'rwkv_gn_g': 1.0 + nrm((L, RWKV_W), 0.05),
        'rwkv_gn_b': nrm((L, RWKV_W), 0.02),
        'fox_f_bias': 2.0 + nrm((L, FOX_HEADS), 0.5),
        'gate_bias': nrm((L, N_BRANCHES, D_MODEL), 0.1),
        'w_branch': nrm((L, MIX_WIDTH, D_MODEL), (4 * HEAD_DIM) ** -0.5),
        'w_out': nrm((L, D_MODEL, D_MODEL), DN_BETA * D_MODEL ** -0.5),
        'ln_g': 1.0 + nrm((L, 2, D_MODEL), 0.05),
        'ln_b': nrm((L, 2, D_MODEL), 0.02),
        'ffn_w1': nrm((N_DENSE, D_MODEL, D_FF), D_MODEL ** -0.5),
        'ffn_w3': nrm((N_DENSE, D_MODEL, D_FF), D_MODEL ** -0.5),
        'ffn_w2': nrm((N_DENSE, D_FF, D_MODEL), DN_BETA * D_FF ** -0.5),
        'router_w': nrm((N_MOE, D_MODEL, N_EXPERTS), D_MODEL ** -0.5),
        'router_b': nrm((N_MOE, N_EXPERTS), 0.01),
        'exp_w1': nrm((N_MOE, N_EXPERTS, D_MODEL, D_FF_EXPERT), D_MODEL ** -0.5),
        'exp_w3': nrm((N_MOE, N_EXPERTS, D_MODEL, D_FF_EXPERT), D_MODEL ** -0.5),
        'exp_w2': nrm((N_MOE, N_EXPERTS, D_FF_EXPERT, D_MODEL), DN_BETA * D_FF_EXPERT ** -0.5),
    }

def first_block(x, w_in, swa_sinks, rwkv_mu, rwkv_w0, rwkv_w_up, rwkv_a0, rwkv_a_up, rwkv_g_up,
              rwkv_k_k, rwkv_k_a, rwkv_r_k, rwkv_gn_g, rwkv_gn_b, fox_f_bias, gate_bias, w_branch,
              w_out, ln_g, ln_b, ffn_w1, ffn_w3, ffn_w2, router_w, router_b, exp_w1, exp_w3, exp_w2):
    for layer in range(DEPTH):
        y = mixer_block(x, w_in[layer], swa_sinks[layer], rwkv_mu[layer], rwkv_w0[layer],
                        rwkv_w_up[layer], rwkv_a0[layer], rwkv_a_up[layer], rwkv_g_up[layer],
                        rwkv_k_k[layer], rwkv_k_a[layer], rwkv_r_k[layer], rwkv_gn_g[layer],
                        rwkv_gn_b[layer], fox_f_bias[layer], gate_bias[layer], w_branch[layer],
                        w_out[layer])
        x = layer_norm(DN_ALPHA * x + y, ln_g[layer, 0], ln_b[layer, 0])
        j = layer // 2
        if layer % 2 == 0:
            y = swiglu(x, ffn_w1[j], ffn_w3[j], ffn_w2[j])
        else:
            y = moe_ffn(x, router_w[j], router_b[j], exp_w1[j], exp_w3[j], exp_w2[j])
        x = layer_norm(DN_ALPHA * x + y, ln_g[layer, 1], ln_b[layer, 1])
    return x


N_MEM = 256
EPS = 1e-6
NEG_INF = -1e30

ROPE_DIM = HEAD_DIM // 4
ROPE_THETA = 500000.0

A_HEADS = 8
A_WIDTH = A_HEADS * HEAD_DIM
MOBA_BLOCK = 256
MOBA_TOPK = 3
MOBA_QCHUNK = 32

B_GROUPS = 8
B_WIDTH = B_GROUPS * HEAD_DIM
GMLP_CHUNK = 128

GLA_HEADS = 4
GLA_DK = (D_MODEL // 2) // GLA_HEADS
GLA_DV = D_MODEL // GLA_HEADS
GLA_LOWRANK = 16
GLA_TAU = 16.0
GLA_CHUNK = 64

X_HEADS = 4
X_HEAD_DIM = D_MODEL // X_HEADS

D_FF_2 = -(-8 * D_MODEL // (3 * 256)) * 256

EV_IN = 3 * A_WIDTH + 2 * B_WIDTH
OD_IN = 2 * GLA_HEADS * GLA_DK + 2 * GLA_HEADS * GLA_DV


def rmsnorm(x, g):
    xf = x.astype(jnp.float32)
    y = xf * lax.rsqrt(jnp.mean(xf * xf, axis=-1, keepdims=True) + EPS)
    return (y * g.astype(jnp.float32)).astype(x.dtype)

def layernorm(x, g, b):
    xf = x.astype(jnp.float32)
    mu = jnp.mean(xf, axis=-1, keepdims=True)
    var = jnp.mean(jnp.square(xf - mu), axis=-1, keepdims=True)
    y = (xf - mu) * lax.rsqrt(var + EPS) * g.astype(jnp.float32) + b.astype(jnp.float32)
    return y.astype(x.dtype)

def partial_rope(x, positions):
    half = ROPE_DIM // 2
    inv_freq = ROPE_THETA ** (-jnp.arange(half, dtype=jnp.float32) * 2.0 / ROPE_DIM)
    ang = positions.astype(jnp.float32)[:, None, :, None] * inv_freq
    cos, sin = jnp.cos(ang), jnp.sin(ang)
    xf = x.astype(jnp.float32)
    x1, x2 = xf[..., :half], xf[..., half:ROPE_DIM]
    out = jnp.concatenate([x1 * cos - x2 * sin, x2 * cos + x1 * sin, xf[..., ROPE_DIM:]], axis=-1)
    return out.astype(x.dtype)

def moba_attention(q, k, v):
    Bn, H, S, Dh = q.shape
    S_pad = -(-S // MOBA_BLOCK) * MOBA_BLOCK
    pad = [(0, 0), (0, 0), (0, S_pad - S), (0, 0)]
    q, k, v = jnp.pad(q, pad), jnp.pad(k, pad), jnp.pad(v, pad)
    nb = S_pad // MOBA_BLOCK
    topk = min(MOBA_TOPK, nb)
    scale = Dh ** -0.5
    kb = k.reshape(Bn, H, nb, MOBA_BLOCK, Dh)
    vb = v.reshape(Bn, H, nb, MOBA_BLOCK, Dh)
    k_mean = jnp.mean(kb.astype(jnp.float32), axis=3)
    gate = jnp.einsum('bhsd,bhnd->bhsn', q.astype(jnp.float32), k_mean)
    own = jnp.arange(S_pad) // MOBA_BLOCK
    past = jnp.arange(nb)[None, :] < own[:, None]
    gate = jnp.where(past[None, None], gate, NEG_INF)
    _, sel = lax.top_k(gate, topk)
    valid = sel < own[None, None, :, None]

    nq = S_pad // MOBA_QCHUNK
    q_c = q.reshape(Bn, H, nq, MOBA_QCHUNK, Dh).transpose(2, 0, 1, 3, 4)
    sel_c = sel.reshape(Bn, H, nq, MOBA_QCHUNK, topk).transpose(2, 0, 1, 3, 4)
    valid_c = valid.reshape(Bn, H, nq, MOBA_QCHUNK, topk).transpose(2, 0, 1, 3, 4)
    chunk_ids = jnp.arange(nq, dtype=jnp.int32)
    bi = jnp.arange(Bn)[:, None, None, None]
    hi = jnp.arange(H)[None, :, None, None]
    key_idx = jnp.arange(MOBA_BLOCK)

    def one_chunk(args):
        qc, selc, validc, ci = args
        blk = (ci * MOBA_QCHUNK) // MOBA_BLOCK
        k_own = lax.dynamic_index_in_dim(kb, blk, axis=2, keepdims=False)
        v_own = lax.dynamic_index_in_dim(vb, blk, axis=2, keepdims=False)
        qpos = (ci * MOBA_QCHUNK) % MOBA_BLOCK + jnp.arange(MOBA_QCHUNK)
        causal = key_idx[None, :] <= qpos[:, None]
        s_own = jnp.einsum('bhqd,bhkd->bhqk', qc, k_own, preferred_element_type=jnp.float32) * scale
        s_own = jnp.where(causal[None, None], s_own, NEG_INF)
        k_sel = kb[bi, hi, selc]
        v_sel = vb[bi, hi, selc]
        s_sel = jnp.einsum('bhqd,bhqnkd->bhqnk', qc, k_sel, preferred_element_type=jnp.float32) * scale
        s_sel = jnp.where(validc[..., None], s_sel, NEG_INF)
        logits = jnp.concatenate([s_own, s_sel.reshape(Bn, H, MOBA_QCHUNK, topk * MOBA_BLOCK)], axis=-1)
        p = jax.nn.softmax(logits, axis=-1)
        p_own = p[..., :MOBA_BLOCK].astype(v.dtype)
        p_sel = p[..., MOBA_BLOCK:].reshape(Bn, H, MOBA_QCHUNK, topk, MOBA_BLOCK).astype(v.dtype)
        out = (jnp.einsum('bhqk,bhkd->bhqd', p_own, v_own, preferred_element_type=jnp.float32)
               + jnp.einsum('bhqnk,bhqnkd->bhqd', p_sel, v_sel, preferred_element_type=jnp.float32))
        return out.astype(q.dtype)

    out = lax.map(one_chunk, (q_c, sel_c, valid_c, chunk_ids))
    out = out.transpose(1, 2, 0, 3, 4).reshape(Bn, H, S_pad, Dh)
    return out[:, :, :S]

def chunked_spatial_gating(u, v, w_s, b_s, ln_g, ln_b):
    Bn, S, G, Dg = v.shape
    nc = S // GMLP_CHUNK
    vn = layernorm(v, ln_g, ln_b).reshape(Bn, nc, GMLP_CHUNK, G, Dg)
    mask = jnp.tril(jnp.ones((GMLP_CHUNK, GMLP_CHUNK), dtype=w_s.dtype))
    ws = w_s * mask[None]
    mixed = jnp.einsum('gij,bcjgd->bcigd', ws, vn) + b_s.T[None, None, :, :, None]
    return u * mixed.reshape(Bn, S, G, Dg).astype(u.dtype)

def even_mixer(h, positions, w_in, q_gain, k_gain, w_s, b_s, ln_g, ln_b, w_out):
    Bn, S, _ = h.shape
    proj = h @ w_in
    q, k, v, pu, pv = jnp.split(proj, [A_WIDTH, 2 * A_WIDTH, 3 * A_WIDTH, 3 * A_WIDTH + B_WIDTH], axis=-1)

    def heads(t):
        return t.reshape(Bn, S, A_HEADS, HEAD_DIM).transpose(0, 2, 1, 3)

    q = partial_rope(rmsnorm(heads(q), q_gain), positions)
    k = partial_rope(rmsnorm(heads(k), k_gain), positions)
    a = moba_attention(q, k, heads(v)).transpose(0, 2, 1, 3).reshape(Bn, S, A_WIDTH)
    u = jax.nn.gelu(pu, approximate=False).reshape(Bn, S, B_GROUPS, HEAD_DIM)
    vg = jax.nn.gelu(pv, approximate=False).reshape(Bn, S, B_GROUPS, HEAD_DIM)
    g = chunked_spatial_gating(u, vg, w_s, b_s, ln_g, ln_b).reshape(Bn, S, B_WIDTH)
    return jnp.concatenate([a, g], axis=-1) @ w_out

def gla_chunked(q, k, v, log_a):
    Bn, H, S, dk = q.shape
    dv = v.shape[-1]
    nc = S // GLA_CHUNK
    f32 = jnp.float32
    qc = q.astype(f32).reshape(Bn, H, nc, GLA_CHUNK, dk)
    kc = k.astype(f32).reshape(Bn, H, nc, GLA_CHUNK, dk)
    vc = v.astype(f32).reshape(Bn, H, nc, GLA_CHUNK, dv)
    b = jnp.cumsum(log_a.astype(f32).reshape(Bn, H, nc, GLA_CHUNK, dk), axis=3)
    b_last = b[:, :, :, -1:, :]
    q_in = qc * jnp.exp(b)
    k_in = kc * jnp.exp(-b)
    causal = jnp.tril(jnp.ones((GLA_CHUNK, GLA_CHUNK), dtype=bool))
    att = jnp.where(causal, jnp.einsum('bhnid,bhnjd->bhnij', q_in, k_in), 0.0)
    o_intra = jnp.einsum('bhnij,bhnjv->bhniv', att, vc)
    k_state = kc * jnp.exp(b_last - b)
    d_state = jnp.einsum('bhnjd,bhnjv->bhndv', k_state, vc)
    decay = jnp.exp(b_last[:, :, :, 0, :])

    def step(s_prev, xs):
        ds_n, dec_n = xs
        return dec_n[..., None] * s_prev + ds_n, s_prev

    _, s_before = lax.scan(step, jnp.zeros((Bn, H, dk, dv), f32),
                           (jnp.moveaxis(d_state, 2, 0), jnp.moveaxis(decay, 2, 0)))
    s_before = jnp.moveaxis(s_before, 0, 2)
    o_inter = jnp.einsum('bhnid,bhndv->bhniv', q_in, s_before)
    return (o_intra + o_inter).reshape(Bn, H, S, dv).astype(v.dtype)

def gla_mixer(h, w_in, w_g1, w_g2, b_g, o_gain, w_out):
    Bn, S, _ = h.shape
    qk_w = GLA_HEADS * GLA_DK
    v_w = GLA_HEADS * GLA_DV
    proj = h @ w_in
    q, k, v, r = jnp.split(proj, [qk_w, 2 * qk_w, 2 * qk_w + v_w], axis=-1)
    log_a = jax.nn.log_sigmoid(((h @ w_g1) @ w_g2 + b_g).astype(jnp.float32)) / GLA_TAU

    def heads(t, d):
        return t.reshape(Bn, S, GLA_HEADS, d).transpose(0, 2, 1, 3)

    o = gla_chunked(heads(q, GLA_DK) * (GLA_DK ** -0.5), heads(k, GLA_DK),
                    heads(v, GLA_DV), heads(log_a, GLA_DK))
    o = rmsnorm(o, o_gain[:, None, :])
    o = o.transpose(0, 2, 1, 3).reshape(Bn, S, v_w) * jax.nn.silu(r)
    return o @ w_out

def mem_cross_attention(h, mem_n, w_q, w_kv, q_gain, k_gain, w_out):
    Bn, S, _ = h.shape
    M = mem_n.shape[1]
    q = rmsnorm((h @ w_q).reshape(Bn, S, X_HEADS, X_HEAD_DIM), q_gain)
    k, v = jnp.split(mem_n @ w_kv, 2, axis=-1)
    k = rmsnorm(k.reshape(Bn, M, X_HEADS, X_HEAD_DIM), k_gain)
    v = v.reshape(Bn, M, X_HEADS, X_HEAD_DIM)
    s = jnp.einsum('bqhd,bkhd->bhqk', q, k, preferred_element_type=jnp.float32) * (X_HEAD_DIM ** -0.5)
    p = jax.nn.softmax(s, axis=-1).astype(v.dtype)
    o = jnp.einsum('bhqk,bkhd->bqhd', p, v).reshape(Bn, S, D_MODEL)
    return o @ w_out

def swiglu_2(h, w_gu, w_down):
    g, u = jnp.split(h @ w_gu, 2, axis=-1)
    return (jax.nn.silu(g) * u) @ w_down

def second_inputs(seed: int = 0) -> dict:
    key = jax.random.key(seed)
    ks = iter(jax.random.split(key, 32))
    f32 = jnp.float32
    n_ev = (DEPTH + 1) // 2
    n_od = DEPTH // 2

    def nrm(shape, scale):
        return jax.random.normal(next(ks), shape, f32) * scale

    def gain(shape):
        return 1.0 + 0.05 * jax.random.normal(next(ks), shape, f32)

    x = nrm((BATCH, SEQ, D_MODEL), 1.0)
    mem = nrm((BATCH, N_MEM, D_MODEL), 1.0)
    positions = (jnp.arange(SEQ, dtype=jnp.int32)[None, :]
                 + jax.random.randint(next(ks), (BATCH, 1), 0, 4096, dtype=jnp.int32))
    return {
        'x': x,
        'mem': mem,
        'positions': positions,
        'norm_mix': gain((DEPTH, D_MODEL)),
        'norm_mem_q': gain((DEPTH, D_MODEL)),
        'norm_mem_kv': gain((DEPTH, D_MODEL)),
        'norm_ffn': gain((DEPTH, D_MODEL)),
        'ev_w_in': nrm((n_ev, D_MODEL, EV_IN), D_MODEL ** -0.5),
        'ev_q_gain': gain((n_ev, HEAD_DIM)),
        'ev_k_gain': gain((n_ev, HEAD_DIM)),
        'ev_w_s': nrm((n_ev, B_GROUPS, GMLP_CHUNK, GMLP_CHUNK), GMLP_CHUNK ** -0.5),
        'ev_b_s': gain((n_ev, B_GROUPS, GMLP_CHUNK)),
        'ev_ln_g': gain((n_ev, B_GROUPS, HEAD_DIM)),
        'ev_ln_b': nrm((n_ev, B_GROUPS, HEAD_DIM), 0.02),
        'ev_w_out': nrm((n_ev, A_WIDTH + B_WIDTH, D_MODEL), 0.5 * (A_WIDTH + B_WIDTH) ** -0.5),
        'od_w_in': nrm((n_od, D_MODEL, OD_IN), D_MODEL ** -0.5),
        'od_w_g1': nrm((n_od, D_MODEL, GLA_LOWRANK), D_MODEL ** -0.5),
        'od_w_g2': nrm((n_od, GLA_LOWRANK, GLA_HEADS * GLA_DK), GLA_LOWRANK ** -0.5),
        'od_b_g': nrm((n_od, GLA_HEADS * GLA_DK), 0.02),
        'od_o_gain': gain((n_od, GLA_HEADS, GLA_DV)),
        'od_w_out': nrm((n_od, GLA_HEADS * GLA_DV, D_MODEL), 0.5 * (GLA_HEADS * GLA_DV) ** -0.5),
        'xa_w_q': nrm((DEPTH, D_MODEL, D_MODEL), D_MODEL ** -0.5),
        'xa_w_kv': nrm((DEPTH, D_MODEL, 2 * D_MODEL), D_MODEL ** -0.5),
        'xa_q_gain': gain((DEPTH, X_HEAD_DIM)),
        'xa_k_gain': gain((DEPTH, X_HEAD_DIM)),
        'xa_w_out': nrm((DEPTH, D_MODEL, D_MODEL), 0.5 * D_MODEL ** -0.5),
        'ffn_w_gu': nrm((DEPTH, D_MODEL, 2 * D_FF_2), D_MODEL ** -0.5),
        'ffn_w_down': nrm((DEPTH, D_FF_2, D_MODEL), 0.5 * D_FF_2 ** -0.5),
    }

def second_block(x, mem, positions, norm_mix, norm_mem_q, norm_mem_kv, norm_ffn,
              ev_w_in, ev_q_gain, ev_k_gain, ev_w_s, ev_b_s, ev_ln_g, ev_ln_b, ev_w_out,
              od_w_in, od_w_g1, od_w_g2, od_b_g, od_o_gain, od_w_out,
              xa_w_q, xa_w_kv, xa_q_gain, xa_k_gain, xa_w_out,
              ffn_w_gu, ffn_w_down):
    for l in range(DEPTH):
        i = l // 2
        h = rmsnorm(x, norm_mix[l])
        if l % 2 == 0:
            x = x + even_mixer(h, positions, ev_w_in[i], ev_q_gain[i], ev_k_gain[i],
                               ev_w_s[i], ev_b_s[i], ev_ln_g[i], ev_ln_b[i], ev_w_out[i])
        else:
            x = x + gla_mixer(h, od_w_in[i], od_w_g1[i], od_w_g2[i], od_b_g[i],
                              od_o_gain[i], od_w_out[i])
        x = x + mem_cross_attention(rmsnorm(x, norm_mem_q[l]), rmsnorm(mem, norm_mem_kv[l]),
                                    xa_w_q[l], xa_w_kv[l], xa_q_gain[l], xa_k_gain[l], xa_w_out[l])
        x = x + swiglu_2(rmsnorm(x, norm_ffn[l]), ffn_w_gu[l], ffn_w_down[l])
    return x


def setup_inputs(seed=0):
    out = dict(first_inputs(seed))
    for name, value in second_inputs(seed + 1).items():
        if name != "x":
            out[name + "_2"] = value
    return out


def reference(
    x, w_in, swa_sinks, rwkv_mu, rwkv_w0, rwkv_w_up, rwkv_a0, rwkv_a_up, rwkv_g_up, rwkv_k_k,
    rwkv_k_a, rwkv_r_k, rwkv_gn_g, rwkv_gn_b, fox_f_bias, gate_bias, w_branch, w_out, ln_g,
    ln_b, ffn_w1, ffn_w3, ffn_w2, router_w, router_b, exp_w1, exp_w3, exp_w2, mem_2,
    positions_2, norm_mix_2, norm_mem_q_2, norm_mem_kv_2, norm_ffn_2, ev_w_in_2, ev_q_gain_2,
    ev_k_gain_2, ev_w_s_2, ev_b_s_2, ev_ln_g_2, ev_ln_b_2, ev_w_out_2, od_w_in_2, od_w_g1_2,
    od_w_g2_2, od_b_g_2, od_o_gain_2, od_w_out_2, xa_w_q_2, xa_w_kv_2, xa_q_gain_2, xa_k_gain_2,
    xa_w_out_2, ffn_w_gu_2, ffn_w_down_2,
):
    x = first_block(
        x, w_in, swa_sinks, rwkv_mu, rwkv_w0, rwkv_w_up, rwkv_a0, rwkv_a_up, rwkv_g_up,
        rwkv_k_k, rwkv_k_a, rwkv_r_k, rwkv_gn_g, rwkv_gn_b, fox_f_bias, gate_bias, w_branch,
        w_out, ln_g, ln_b, ffn_w1, ffn_w3, ffn_w2, router_w, router_b, exp_w1, exp_w3, exp_w2,
    )
    return second_block(
        x, mem_2, positions_2, norm_mix_2, norm_mem_q_2, norm_mem_kv_2, norm_ffn_2, ev_w_in_2,
        ev_q_gain_2, ev_k_gain_2, ev_w_s_2, ev_b_s_2, ev_ln_g_2, ev_ln_b_2, ev_w_out_2,
        od_w_in_2, od_w_g1_2, od_w_g2_2, od_b_g_2, od_o_gain_2, od_w_out_2, xa_w_q_2, xa_w_kv_2,
        xa_q_gain_2, xa_k_gain_2, xa_w_out_2, ffn_w_gu_2, ffn_w_down_2,
    )


_drawn_inputs = setup_inputs


def setup_inputs(seed=0):
    import zlib

    import numpy as np

    out = dict(_drawn_inputs(seed))
    spreads = {}
    factors = {'swa_sinks': 8.0,
     'rwkv_w_up': 7.309,
     'rwkv_a0': 6.648,
     'rwkv_k_k': 7.495,
     'rwkv_k_a': 3.299,
     'rwkv_gn_g': 4.112,
     'rwkv_gn_b': 6.802,
     'gate_bias': 3.128,
     'router_b': 3.87,
     'norm_mem_q_2': 8.0,
     'norm_mem_kv_2': 8.0,
     'ev_q_gain_2': 8.0,
     'ev_k_gain_2': 8.0,
     'ev_b_s_2': 4.086,
     'ev_ln_g_2': 5.612,
     'ev_ln_b_2': 8.0,
     'od_b_g_2': 8.0,
     'od_o_gain_2': 3.782,
     'xa_q_gain_2': 8.0,
     'xa_k_gain_2': 8.0}
    for name, (base, spread) in spreads.items():
        noise = np.random.default_rng([zlib.crc32(name.encode()), seed]).standard_normal(out[name].shape)
        drawn = base * np.exp(spread * noise) if base else spread * noise
        out[name] = jnp.asarray(drawn.astype(out[name].dtype))
    for name, factor in factors.items():
        out[name] = (out[name] * factor).astype(out[name].dtype)
    return out
```

```python
import numpy as np
import concourse.bass as bass
from concourse import mybir
from contextlib import ExitStack

P = 128
S = 256
NT = S // P
D = 1024
KT = D // P
HD = 64
DEPTH = 2
CH = 64
NCH = S // CH
DFF = 2816
FT = DFF // P
NEXP = 8
DFE = 1408
ET = DFE // P
ALPHA = float((2 * DEPTH) ** 0.25)
LN_EPS = 1e-5
RMS_EPS = 1e-6
GN_EPS = 64e-5
TOPK = min(256, S // 4)
NEG = -1e30
TAKEN = -3e38
SLOT = 4096
RING = 3

TM_SWA_V, TM_FOX_V, TM_FOX_F, TM_DSA_V, TM_DSA_W, TM_COLS = 0, 128, 384, 388, 452, 456
F_SWA_Q, F_SWA_K, F_R, F_K, F_V, F_LO, F_FOX_Q, F_FOX_K, F_DSA_Q, F_DSA_K, F_IDX_Q, F_IDX_K, F_TILES = \
    0, 4, 6, 8, 10, 12, 14, 16, 18, 20, 21, 23, 24

_AT = {}
NCOLS = 0


def _columns(name, n):
    global NCOLS
    _AT[name] = NCOLS
    NCOLS += n


for _l in range(DEPTH):
    for _name, _n in (("mu", 8), ("w0", 2), ("a0", 2), ("k_k", 2), ("k_a", 2), ("r_k", 2), ("gn_g", 2), ("gn_b", 2),
                      ("gate", 32), ("norm_mix", 8), ("norm_q", 8), ("norm_kv", 8), ("norm_ffn", 8),
                      ("xq_gain", 2), ("xk_gain", 2)):
        _columns(f"{_name}{_l}", _n)
for _name, _n in (("q_gain", 1), ("k_gain", 1), ("b_g", 4), ("o_gain", 8), ("inv_freq", 1),
                  ("eps_ln", 1), ("eps_rms", 1), ("eps_gn", 1), ("eps_kk", 1), ("half_pi", 1)):
    _columns(_name, _n)

CONST_SPEC = [("ident", P), ("bones", P), ("ones", P), ("rot", P), ("causal", S * NT), ("window", S * NT),
              ("admit", S * NT), ("prefix", S * NT), ("strict_incl", 2 * P), ("levels", 6 * P),
              ("chunk_keep", S * 4), ("sel4", 4 * S), ("tril", P)]
CONST_AT = {}
NCONST = 0
for _name, _n in CONST_SPEC:
    CONST_AT[_name] = (NCONST, _n)
    NCONST += _n


def shape_constants():
    c = np.zeros((P, NCONST), np.float32)

    def put(name, a):
        at, n = CONST_AT[name]
        c[:a.shape[0], at:at + n] = a.reshape(a.shape[0], n)

    i = np.arange(P)
    s = np.arange(S)
    put("ident", np.eye(P))
    put("bones", (i[:, None] // HD == i[None, :] // HD).astype(np.float32))
    put("ones", np.ones((P, P)))
    rot = np.zeros((P, P))
    for base in (0, HD):
        for a in range(8):
            rot[base + 8 + a, base + a] = -1.0
            rot[base + a, base + 8 + a] = 1.0
    put("rot", rot)
    q = np.arange(NT)[None, :, None] * P + i[:, None, None]
    k = s[None, None, :]
    put("causal", np.where(k <= q, 0.0, NEG))
    put("window", np.where((k // CH <= q // CH) & (k // CH >= q // CH - 2), 0.0, NEG))
    put("admit", np.where(k // CH <= q // CH, 0.0, NEG))
    put("prefix", (q <= k).astype(np.float32))
    same = (i[:, None] // CH == i[None, :] // CH)
    put("strict_incl", np.stack([same & (i[:, None] < i[None, :]), same & (i[:, None] <= i[None, :])], 1).astype(np.float32))
    put("levels", np.stack([((i[:, None] // m) % 2 == 0) & (i[None, :] // m == i[:, None] // m + 1)
                            for m in (1, 2, 4, 8, 16, 32)], 1).astype(np.float32))
    put("chunk_keep", np.broadcast_to((np.arange(4 * S) % CH != 0).astype(np.float32), (P, 4 * S)))
    sel = np.zeros((4, 4, S))
    for h in range(4):
        sel[h, h, :P] = 1.0
        sel[h, h, P:] = -1.0
    put("sel4", sel)
    put("tril", (i[:, None] <= i[None, :]).astype(np.float32))
    return c


MIX_JOBS = {}
MIX_SLOTS = [("rk", 768, 512, 2), ("vlo", 1280, 512, 2), ("dsa", 2564, 384, 3), ("idx", 2948, 324, 3),
             ("foxqk", 1792, 512, 2), ("foxv", 2304, 260, 2), ("swaq", 0, 512, 2), ("swakv", 512, 256, 2)] \
    + [(f"gate{g}", 3272 + 512 * g, 512, 2) for g in range(8)]
_n = 0
for _name, _, _, _jobs in MIX_SLOTS:
    MIX_JOBS[_name] = _n
    _n += _jobs
MIX_JOBS["brA"] = _n
MIX_JOBS["brB"] = _n + 4
MIX_JOBS["brC"] = _n + 12
MIX_JOBS["out"] = _n + 16
MIX_TOTAL = _n + 18
FFN_DOWN = 6
FFN_TOTAL = FT + FFN_DOWN
EXP_JOBS = ET + 3
MOE_TOTAL = NEXP * EXP_JOBS
EV_TOTAL = 2 + 2 + 2 + 2 + 2 + 2
XA_TOTAL = 2 * 2 + 2 * 2 + 2 * 2 + 2
GLA_TOTAL = 2 + 2 + 4 + 4 + 2
STAGES = [("mix0", MIX_TOTAL), ("ffn0", FFN_TOTAL), ("mix1", MIX_TOTAL), ("moe", MOE_TOTAL), ("ev", EV_TOTAL),
          ("xa0", XA_TOTAL), ("ffn1", FFN_TOTAL), ("gla", GLA_TOTAL), ("xa1", XA_TOTAL), ("ffn2", FFN_TOTAL)]
JOB0 = {}
_n = 0
for _name, _jobs in STAGES:
    JOB0[_name] = _n
    _n += _jobs
SLOTS_OF = {"mix0": 21, "ffn0": 17, "mix1": 21, "moe": 9 * NEXP, "ev": 7, "xa0": 8, "ffn1": 17, "gla": 8, "xa1": 8,
            "ffn2": 17}
SLOT0 = {}
_n = 0
for _name, _ in STAGES:
    SLOT0[_name] = _n
    _n += SLOTS_OF[_name]


def attention_units():
    out = {}
    n = 0
    for stage, kinds in (("mix0", (("swa", 8), ("fox", 4), ("dsa", 4))), ("mix1", (("swa", 8), ("fox", 4), ("dsa", 4))),
                         ("ev", (("moba", 8),)), ("xa0", (("cross", 4),)), ("xa1", (("cross", 4),))):
        units = [(kind, h, t) for kind, heads in kinds for h in range(heads) for t in range(NT)]
        out[stage] = (n, units)
        n += len(units)
    return out


UNITS = attention_units()

MIX_PLAN = [("rk", "feat", 0, F_R), ("rk", "feat", 256, F_K), ("vlo", "feat", 0, F_V), ("vlo", "feat", 256, F_LO),
            ("dsa", "feat", 0, F_DSA_Q), ("dsa", "dup64", 256, F_DSA_K), ("dsa", "tok", (320, 64), TM_DSA_V),
            ("idx", "feat", 0, F_IDX_Q), ("idx", "dup64", 256, F_IDX_K), ("idx", "tok", (320, 4), TM_DSA_W),
            ("foxqk", "feat", 0, F_FOX_Q), ("foxqk", "feat", 256, F_FOX_K),
            ("foxv", "tok1", (0, 0, 260), TM_FOX_V), ("foxv", "tok1", (1, 0, 260), TM_FOX_V),
            ("swaq", "feat", 0, F_SWA_Q), ("swaq", "feat", 256, F_SWA_Q + 2),
            ("swakv", "dup128", 0, F_SWA_K), ("swakv", "tok", (128, 128), TM_SWA_V)]
N_PROJ = len(MIX_PLAN)
SLOT_NO = {name: n for n, (name, _, _, _) in enumerate(MIX_SLOTS)}
TAKEN_BY_ACT = {"mix0": N_PROJ + 16, "ffn0": 0, "mix1": N_PROJ + 16, "moe": 0, "ev": 10, "xa0": 12, "ffn1": 0, "gla": 12,
                "xa1": 12, "ffn2": 0}
ACT0 = {}
_n = 0
for _name, _ in STAGES:
    ACT0[_name] = _n
    _n += TAKEN_BY_ACT[_name]
H0 = {"ffn0": 0, "moe": FT, "ffn1": FT + NEXP * ET, "ffn2": 2 * FT + NEXP * ET}
NORMS = ["mix0", "ffn0", "mix1", "moe", "ev", "xq0", "xkv0", "ffn1", "gla", "xq1", "xkv1", "ffn2"]
NORM_NO = {name: n for n, name in enumerate(NORMS)}


def slot_table():
    t = []
    for name, _ in STAGES:
        if name.startswith("mix"):
            t += [(1, jobs) for _, _, _, jobs in MIX_SLOTS] + [(1, 4), (1, 8), (1, 4), (1, 1), (1, 1)]
        elif name.startswith("ffn"):
            t += [(2, 2)] * (FT // 2) + [(1, 1)] * FFN_DOWN
        elif name == "moe":
            t += ([(2, 2)] * (ET // 2) + [(2, 1)] + [(1, 1)] * 3) * NEXP
        elif name == "ev":
            t += [(1, 2)] * 5 + [(1, 1)] * 2
        else:
            t += [(1, 2)] * 6 + [(1, 1)] * 2
    return t


SLOTS = slot_table()


def loaded_value(slot):
    return 16 * sum(SLOTS[g][0] for g in range(slot % RING, slot + 1, RING))


def used_value(slot):
    return sum(j for _, j in SLOTS[:slot + 1])


def program(nc, a, out):
    fp32, i32 = mybir.dt.float32, mybir.dt.int32
    ALU, ACT = mybir.AluOpType, mybir.ActivationFunctionType
    AX = mybir.AxisListType.X

    ctx = ExitStack()
    with ctx:
        def sb(name, shape, dt=fp32):
            return ctx.enter_context(nc.sbuf_tensor(name, shape, dt))

        sems = {}

        def sem(name):
            if name not in sems:
                sems[name] = ctx.enter_context(nc.semaphore(name))
            return sems[name]

        ring = sb("ring", [P, RING, SLOT])
        X = sb("X", [P, NT, D])
        XT = sb("XT", [P, KT, S])
        CST = sb("CST", [P, NCONST])
        COL = sb("COL", [P, NCOLS])
        LORA = sb("LORA", [P, 512])
        SROW = sb("SROW", [P, 32])
        RW = sb("RW", [P, KT, NEXP])
        G1 = sb("G1", [P, KT, 16])
        F = sb("F", [P, F_TILES, S])
        TM = sb("TM", [P, NT, TM_COLS])
        G = sb("G", [P, 32, S])
        OT = sb("OT", [P, 10, S])
        WK = sb("WK", [P, 9728])
        SMX = sb("SMX", [P, 4, S])
        PT = sb("PT", [P, 2, S])
        SEL = sb("SEL", [P, NT, S])
        TINY = sb("TINY", [P, 256])

        def const(name):
            at, n = CONST_AT[name]
            return CST[:, at:at + n]

        def col(name, n=0):
            return COL[:, _AT[name] + n:_AT[name] + n + 1]

        ident = const("ident")
        bones = const("bones")
        ones = const("ones")
        rot = const("rot")
        causal = const("causal").rearrange("p (t k) -> p t k", t=NT)
        window = const("window").rearrange("p (t k) -> p t k", t=NT)
        admit = const("admit").rearrange("p (t k) -> p t k", t=NT)
        prefix = const("prefix").rearrange("p (t k) -> p t k", t=NT)
        strict_incl = const("strict_incl")
        levels = const("levels").rearrange("p (l k) -> p l k", l=6)
        keep4 = const("chunk_keep")
        sel4 = const("sel4").rearrange("p (h k) -> p h k", h=4)
        tril = const("tril")

        def wk(at, n):
            return WK[:, at:at + n]

        ROWS = wk(0, 2048)
        AR = wk(0, 1024).rearrange("p (f t a n) -> p f t a n", f=2, t=NT, a=2)
        ARF = wk(0, 1024).rearrange("p (f t x) -> p f t x", f=2, t=NT)
        BKT = wk(1024, 1024).rearrange("p (w f n) -> p w f n", w=2, f=2)
        TOK = wk(2048, 1536).rearrange("p (w t n) -> p w t n", w=3, t=NT)
        XI = wk(3584, 1024).rearrange("p (i n) -> p i n", i=8)
        XIT = wk(4608, 1024).rearrange("p (i n) -> p i n", i=8)
        T1 = wk(5632, 1024).rearrange("p (i n) -> p i n", i=8)
        LM = wk(6656, 1024).rearrange("p (i n) -> p i n", i=8)
        ST = wk(7680, 128).rearrange("p (f n) -> p f n", f=2)
        R1 = wk(7808, 256)
        SA = wk(8064, 256)
        YT = wk(8320, 512).rearrange("p (f n) -> p f n", f=2)
        GG = wk(8832, 512).rearrange("p (f n) -> p f n", f=2)
        MB = G[:, 16:24, :].rearrange("p i (w n) -> p i w n", w=2)
        MK = G[:, 24:32, :].rearrange("p i (w n) -> p i w n", w=2)
        DT = G[:, 16:24, :]
        E = [wk(3584 + 512 * n, 512) for n in range(8)]
        REL = OT[:, 0:4, :]
        SCORE = OT[:, 8:10, :]
        C8 = wk(9344, 256)

        XN = wk(4096, 2048).rearrange("p (t n) -> p t n", t=NT)
        MEM = wk(7680, 2048).rearrange("p (t n) -> p t n", t=NT)
        MT = wk(0, 2048).rearrange("p (k n) -> p k n", k=KT)
        BS = wk(0, 1024).rearrange("p (g i) -> p g i", g=8)
        GLN = wk(1024, 1024).rearrange("p (w n) -> p w n", w=2)
        WS = wk(2048, 1024).rearrange("p (g j) -> p g j", g=8)
        WST = F[:, 12:16, :].rearrange("p a b -> p (a b)").rearrange("p (g i) -> p g i", g=8)
        POSI = wk(3072, 256).bitcast(i32)
        COS, SIN = wk(6144, 256), wk(6400, 256)
        GL1 = wk(6144, 256)[0:16, :]
        SIL = wk(6656, 512).rearrange("p (b n) -> p b n", b=2)
        NQ = wk(6656, 1024)
        flat = lambda lo, hi: G[:, lo:hi, :].rearrange("p a b -> p (a b)")
        GB, GE, KS = flat(8, 12), flat(12, 16), flat(16, 20)
        ATT = flat(20, 24).rearrange("p (h t n) -> p h t n", h=4, t=NT)
        KSM = flat(24, 28).rearrange("p (t n) -> p t n", t=NT)
        GS = flat(28, 32).rearrange("p (h n) -> p h n", h=4)

        bank = [ctx.enter_context(nc.psum_tensor(f"bank{n}", [P, 512], fp32)) for n in range(8)]

        def half(b):
            return bank[b][:, :].rearrange("p (h n) -> p h n", h=2)

        def ring8(slot):
            return ring[:, slot % RING, :].rearrange("p (k n) -> p k n", k=KT)

        def ring4(slot):
            return ring[:, slot % RING, :].rearrange("p (k n) -> p k n", k=4)

        V2 = G[:, 0:8, :].rearrange("p (t x) n -> p t (x n)", t=NT)

        def unit_at(kind, h, t):
            hb = HD * (h % 2)
            nk = NT if kind == "cross" or t > 0 else 1
            keys = slice(0, nk * P)
            tq = slice(t * P, (t + 1) * P)
            if kind == "cross":
                qk = [(F[:, 2 * h + e, tq], F[:, 8 + 2 * h + e, keys]) for e in range(2)]
                return nk, qk, [[V2[:, kt, h * S + e * P:h * S + (e + 1) * P] for e in range(2)] for kt in range(nk)], \
                    (slice(0, P), slice(2 * h, 2 * h + 2))
            fq, fk, v0, o0 = {"swa": (F_SWA_Q + h // 2, F_SWA_K + h // 4, TM_SWA_V + HD * (h // 4), h // 2),
                              "fox": (F_FOX_Q + h // 2, F_FOX_K + h // 2, TM_FOX_V + HD * h, 6 + h // 2),
                              "dsa": (F_DSA_Q + h // 2, F_DSA_K, TM_DSA_V, 8 + h // 2),
                              "moba": (h // 2, 4 + h // 2, HD * h, h // 2)}[kind]
            vv = V2 if kind == "moba" else TM
            return nk, [(F[hb:hb + HD, fq, tq], F[hb:hb + HD, fk, keys])], \
                [[vv[:, kt, v0:v0 + HD]] for kt in range(nk)], (slice(hb, hb + HD), slice(o0, o0 + 1))

        SCORE_SCALE = {"swa": HD ** -0.5, "fox": HD ** -0.5, "dsa": HD ** -0.5, "moba": HD ** -0.5, "cross": 256 ** -0.5}

        block = ctx.enter_context(nc.Block())

        @block.sync
        def _(sp):
            sp.dma_start(X[:, :, :], a["x"].rearrange("(t p) n -> p t n", p=P)).then_inc(sem("x_in"), 16)
            sp.dma_start(CST[:, :], a["consts"]).then_inc(sem("params_in"), 16)
            sp.dma_start(COL[:, :], a["cols"]).then_inc(sem("params_in"), 16)
            sp.dma_start(SROW[:, :], a["srow"].partition_broadcast(P)).then_inc(sem("params_in"), 16)
            sp.dma_start(RW[:, :, :], a["router_w"][0].rearrange("(k p) n -> p k n", p=P))\
                .then_inc(sem("params_in"), 16)
            sp.dma_start(G1[:, :, :], a["od_w_g1_2"][0].rearrange("(k p) n -> p k n", p=P))\
                .then_inc(sem("params_in"), 16)

            def free(slot):
                if slot >= RING:
                    sp.wait_ge(sem("gemm_done"), used_value(slot - RING))

            def put(slot, dst, src):
                sp.dma_start(dst, src).then_inc(sem(f"slot_loaded{slot % RING}"), 16)

            def cols(w, c0, n):
                return w.rearrange("(k p) n -> p k n", p=P)[:, :, c0:c0 + n]

            def rows4(w, r0, kn):
                return w[r0 * P:(r0 + kn) * P, :].rearrange("(k p) n -> p k n", p=P)

            def mix(L):
                slot = SLOT0[f"mix{L}"]
                for _, c0, n, _ in MIX_SLOTS:
                    free(slot)
                    put(slot, ring8(slot)[:, :, 0:n], cols(a["w_in"][L], c0, n))
                    slot += 1
                for w, r0, kn in ((a["w_branch"][L], 0, 4), (a["w_branch"][L], 4, 4), (a["w_branch"][L], 8, 2),
                                  (a["w_out"][L], 0, 4), (a["w_out"][L], 4, 4)):
                    free(slot)
                    put(slot, ring4(slot)[:, 0:kn, :], rows4(w, r0, kn))
                    slot += 1

            def ffn(stage, w1, c1, w3, c3, w2):
                s0 = SLOT0[stage]

                def up(slot, at):
                    put(slot, ring8(slot)[:, :, 0:S], w1.rearrange("(k p) n -> p k n", p=P)[:, :, bass.ds(at + c1, S)])
                    put(slot, ring8(slot)[:, :, S:2 * S],
                        w3.rearrange("(k p) n -> p k n", p=P)[:, :, bass.ds(at + c3, S)])

                for i in range(RING):
                    free(s0 + i)
                    up(s0 + i, S * i)
                with sp.Fori(1, 3) as r:
                    for i in range(RING):
                        sp.wait_ge(sem("gemm_done"), JOB0[stage] + 2 * (i + 1) + 6 * (r - 1))
                        up(s0 + i, S * RING * r + S * i)
                for i in range(3 * RING, FT // 2):
                    free(s0 + i)
                    up(s0 + i, S * i)
                for i in range(FFN_DOWN):
                    slot = s0 + FT // 2 + i
                    kn = min(4, FT - 4 * i)
                    free(slot)
                    put(slot, ring4(slot)[:, 0:kn, :], rows4(w2, 4 * i, kn))

            def expert(e, first):
                s0 = SLOT0["moe"]
                job = JOB0["moe"]
                w1, w3 = ([a[n][0, bass.ds(e, 1), :, :].rearrange("e (k p) n -> p (e k) n", p=P) for n in
                           ("exp_w1", "exp_w3")])
                w2 = a["exp_w2"][0, bass.ds(e, 1), :, :].rearrange("e (k p) n -> p (e k) n", p=P)
                for i in range(9):
                    slot = s0 + i
                    if first:
                        free(slot)
                    elif i < RING:
                        sp.wait_ge(sem("gemm_done"), job + ET + i + 1 + EXP_JOBS * (e - 1))
                    else:
                        sp.wait_ge(sem("gemm_done"), used_value(slot - RING) + EXP_JOBS * e)
                    if i < 6:
                        n = min(S, DFE - S * i)
                        put(slot, ring8(slot)[:, :, 0:n], w1[:, :, S * i:S * i + n])
                        put(slot, ring8(slot)[:, :, S:S + n], w3[:, :, S * i:S * i + n])
                    else:
                        k0 = 4 * (i - 6)
                        kn = min(4, ET - k0)
                        put(slot, ring4(slot)[:, 0:kn, :], w2[:, k0:k0 + kn, :])

            def simple(stage, col_slots, w_out):
                slot = SLOT0[stage]
                for w, c0 in col_slots:
                    free(slot)
                    put(slot, ring8(slot), cols(w, c0, 512))
                    slot += 1
                for r0 in (0, 4):
                    free(slot)
                    put(slot, ring4(slot), rows4(w_out, r0, 4))
                    slot += 1

            mix(0)
            ffn("ffn0", a["ffn_w1"][0], 0, a["ffn_w3"][0], 0, a["ffn_w2"][0])
            mix(1)
            expert(0, True)
            with sp.Fori(1, NEXP) as e:
                expert(e, False)
            simple("ev", [(a["ev_w_in_2"][0], 512 * i) for i in range(5)], a["ev_w_out_2"][0])
            for L in range(DEPTH):
                if L == 1:
                    simple("gla", [(a["od_w_in_2"][0], 512 * i) for i in range(6)], a["od_w_out_2"][0])
                simple(f"xa{L}", [(a["xa_w_q_2"][L], 0), (a["xa_w_q_2"][L], 512)]
                       + [(a["xa_w_kv_2"][L], 512 * i) for i in range(4)], a["xa_w_out_2"][L])
                ffn(f"ffn{L + 1}", a["ffn_w_gu_2"][L], 0, a["ffn_w_gu_2"][L], DFF, a["ffn_w_down_2"][L])
            sp.wait_ge(sem("x_final"), 1)
            sp.dma_start(out.rearrange("(t p) n -> p t n", p=P), X[:, :, :]).then_inc(sem("x_out"), 16)
            sp.wait_ge(sem("x_out"), 16)

        @block.gpsimd
        def _(pool):

            def lora(L):
                if L:
                    pool.wait_ge(sem("lora_out"), 3 * L)
                pool.dma_start(LORA[0:64, 0:256], a["rwkv_w_up"][L]).then_inc(sem("lora_loaded"), 16)
                pool.dma_start(LORA[64:128, 0:256], a["rwkv_a_up"][L]).then_inc(sem("lora_loaded"), 16)
                pool.dma_start(LORA[:, 256:512], a["rwkv_g_up"][L]).then_inc(sem("lora_loaded"), 16)

            def rows(name, L, k):
                pool.dma_start(ROWS[:, 0:D], a["ln_g"][L, k:k + 1, :].rearrange("a n -> (a n)").partition_broadcast(P))\
                    .then_inc(sem("rows_loaded"), 16)
                pool.dma_start(ROWS[:, D:2 * D],
                               a["ln_b"][L, k:k + 1, :].rearrange("a n -> (a n)").partition_broadcast(P))\
                    .then_inc(sem("rows_loaded"), 16)

            for L in range(DEPTH):
                lora(L)
                pool.wait_ge(sem("shift_done"), L + 1)
                nc.gpsimd.memset(G[:, 16:32, :], 0.0).then_inc(sem("grams_cleared"), 1)
                pool.wait_ge(sem("rwkv_done"), L + 1)
                rows("mix", L, 0)
                pool.wait_ge(sem("ln_done"), 2 * L + 1)
                rows("ffn", L, 1)
            pool.wait_ge(sem("ln_done"), 4)
            for dst, src in ((ROWS[:, 0:1024], a["ev_b_s_2"][0]), (ROWS[:, 1024:1536], a["ev_ln_g_2"][0]),
                             (ROWS[:, 1536:2048], a["ev_ln_b_2"][0])):
                pool.dma_start(dst, src.rearrange("g n -> (g n)").partition_broadcast(P))\
                    .then_inc(sem("gm_loaded"), 16)
            pool.dma_start(wk(2048, 1024).rearrange("p (g j) -> p g j", g=8),
                           a["ev_w_s_2"][0].rearrange("g i j -> i g j")).then_inc(sem("gm_loaded"), 16)
            pool.dma_start(wk(3072, 256).bitcast(i32), a["positions_2"].rearrange("b n -> (b n)").partition_broadcast(P))\
                .then_inc(sem("gm_loaded"), 16)
            pool.dma_start(LORA[0:16, :], a["od_w_g2_2"][0]).then_inc(sem("gm_loaded"), 16)
            pool.dma_start(MEM[:, :, :], a["mem_2"].rearrange("(t p) n -> p t n", p=P)).then_inc(sem("mem_loaded"), 16)

        @block.tensor
        def _(pe):
            mm = nc.tensor.matmul
            waited = [-1]
            fences = [0]

            def fence(ins):
                fences[0] += 1
                ins.then_inc(sem("row_tile_fence"), 1)
                pe.wait_ge(sem("row_tile_fence"), fences[0])

            def slot_in(slot):
                if slot != waited[0]:
                    pe.wait_ge(sem(f"slot_loaded{slot % RING}"), loaded_value(slot))
                    waited[0] = slot

            def transposed(name, src):
                n = NORM_NO[name]
                for j in range(4):
                    for i in range(2):
                        for t in range(NT):
                            last = nc.tensor.transpose(half(2 + j)[:, i, t * P:(t + 1) * P],
                                                       src[:, t, (2 * j + i) * P:(2 * j + i + 1) * P], ident)
                    last.then_inc(sem("xt_psum"), 1)
                pe.wait_ge(sem("xt_ready"), 4 * n + 4)

            def bank_free(stage, i):
                if ACT0[stage] + i - 1 > 0:
                    pe.wait_ge(sem("proj_taken"), ACT0[stage] + i - 1)

            def feat(stage, slot, i, c0, tiles=2, width=P, src=XT):
                slot_in(slot)
                bank_free(stage, i)
                for t in range(tiles):
                    for k in range(KT):
                        last = mm(half(i % 2)[0:width, t, :], ring8(slot)[:, k, c0 + t * P:c0 + t * P + width],
                                  src[:, k, :], start=(k == 0), stop=(k == KT - 1))
                last.then_inc(sem("gemm_done"), 1)

            def tok(stage, slot, i, c0, width, tiles, src=XT):
                slot_in(slot)
                bank_free(stage, i)
                for n, t in enumerate(tiles):
                    for k in range(KT):
                        last = mm(bank[i % 2][:, n * width:(n + 1) * width], src[:, k, t * P:(t + 1) * P],
                                  ring8(slot)[:, k, c0:c0 + width], start=(k == 0), stop=(k == KT - 1))
                last.then_inc(sem("gemm_done"), 1)

            def down(slot, src, k0, kn, first, last_slot):
                slot_in(slot)
                for k in range(kn):
                    for t in range(NT):
                        for h in range(2):
                            last = mm(bank[2 + 2 * t + h][:, :], src[:, k0 + k, t * P:(t + 1) * P],
                                      ring4(slot)[:, k, h * 512:(h + 1) * 512],
                                      start=(first and k == 0), stop=(last_slot and k == kn - 1))
                last.then_inc(sem("gemm_done"), 1)

            def scores(n, unit):
                kind, h, t = unit
                nk, qk, _, _ = unit_at(kind, h, t)
                if n >= 2:
                    pe.wait_ge(sem("scores_taken"), n - 1)
                dst = bank[2 + n % 2][:, 0:nk * P]
                for i, (lhsT, rhs) in enumerate(qk):
                    last = mm(dst, lhsT, rhs, start=(i == 0), stop=(i == len(qk) - 1 and kind != "fox"),
                              skip_group_check=kind == "fox")
                if kind == "fox":
                    mm(half(2 + n % 2)[:, 0, 0:P], C8[0:4, t * P:(t + 1) * P], sel4[0:4, h, 0:P],
                       start=False, stop=False, skip_group_check=True)
                    if nk == 2:
                        mm(half(2 + n % 2)[:, 0, P:2 * P], C8[0:4, t * P:(t + 1) * P], sel4[0:4, h, 0:P],
                           start=False, stop=False, skip_group_check=True)
                    last = mm(dst, sel4[0:4, h, P:2 * P], C8[0:4, 0:nk * P], start=False, stop=True,
                              skip_group_check=True)
                last.then_inc(sem("scores_ready"), 1)

            def turn(n, unit):
                kind, h, t = unit
                nk = unit_at(kind, h, t)[0]
                pe.wait_ge(sem("probs_ready"), n + 1)
                if n >= 2:
                    pe.wait_ge(sem("pt_ready"), n - 1)
                for kt in range(nk):
                    last = nc.tensor.transpose(half(4 + n % 2)[:, 0, kt * P:(kt + 1) * P],
                                               SMX[:, n % 4, kt * P:(kt + 1) * P], ident)
                last.then_inc(sem("pt_psum"), 1)

            def context(n, unit):
                kind, h, t = unit
                nk, _, vs, (parts, outs) = unit_at(kind, h, t)
                pe.wait_ge(sem("pt_ready"), n + 1)
                if n >= 2:
                    pe.wait_ge(sem("ctx_taken"), n - 1)
                for e in range(outs.stop - outs.start):
                    for kt in range(nk):
                        last = mm(bank[6 + n % 2][parts, e * P:(e + 1) * P], vs[kt][e], PT[:, n % 2, kt * P:(kt + 1) * P],
                                  start=(kt == 0), stop=(kt == nk - 1))
                last.then_inc(sem("ctx_psum"), 1)

            def attention(stage, filler=None):
                n0, units = UNITS[stage]
                for i in range(len(units) + 3):
                    if i < len(units):
                        scores(n0 + i, units[i])
                    if filler is not None:
                        filler(i)
                    if 2 <= i < len(units) + 2:
                        turn(n0 + i - 2, units[i - 2])
                    if i >= 3:
                        context(n0 + i - 3, units[i - 3])
                pe.wait_ge(sem("ctx_taken"), n0 + len(units))

            def mix(L):
                stage = f"mix{L}"
                s0 = SLOT0[stage]
                if L == 0:
                    pe.wait_ge(sem("x_in"), 16)
                    pe.wait_ge(sem("params_in"), 80)
                else:
                    pe.wait_ge(sem("ln_done"), 2)
                transposed(stage, X)
                for i, (name, kind, c, dest) in enumerate(MIX_PLAN):
                    slot = s0 + SLOT_NO[name]
                    if kind == "feat":
                        feat(stage, slot, i, c)
                    elif kind == "dup64":
                        feat(stage, slot, i, c, 1, 64)
                    elif kind == "dup128":
                        feat(stage, slot, i, c, 1)
                    elif kind == "tok":
                        tok(stage, slot, i, c[0], c[1], range(NT))
                    else:
                        tok(stage, slot, i, c[1], c[2], [c[0]])

                def gate(j):
                    feat(stage, s0 + SLOT_NO["gate0"] + j // 2, N_PROJ + j, (j % 2) * 2 * P)

                pe.wait_ge(sem("lora_loaded"), 48 * (L + 1))
                pe.wait_ge(sem("lora_in"), L + 1)
                for m in range(2):
                    last = mm(half(2)[:, m, :], LORA[0:64, m * P:(m + 1) * P], F[0:64, F_LO, :], start=True, stop=True)
                last.then_inc(sem("lora_out"), 1)
                for m in range(2):
                    last = mm(half(3)[:, m, :], LORA[64:128, m * P:(m + 1) * P], F[64:128, F_LO, :],
                              start=True, stop=True)
                last.then_inc(sem("lora_out"), 1)
                for m in range(2):
                    last = mm(half(4)[:, m, :], LORA[:, 256 + m * P:256 + (m + 1) * P], F[:, F_LO + 1, :],
                              start=True, stop=True)
                last.then_inc(sem("lora_out"), 1)
                pe.wait_ge(sem("proj_taken"), ACT0[stage] + N_PROJ)
                for t in range(NT):
                    if t:
                        pe.wait_ge(sem("idx_relu"), 2 * L + 1)
                    for h in range(4):
                        hb = HD * (h % 2)
                        last = mm(half(6 + h % 2)[:, h // 2, :], F[hb:hb + HD, F_IDX_Q + h // 2, t * P:(t + 1) * P],
                                  F[hb:hb + HD, F_IDX_K, :], start=True, stop=True)
                    last.then_inc(sem("idx_scores"), 1)
                    gate(t)
                pe.wait_ge(sem("logf_ready"), L + 1)
                for t in range(NT):
                    last = mm(bank[5][0:4, 0:S], TM[:, t, TM_FOX_F:TM_FOX_F + 4], prefix[:, t, :],
                              start=(t == 0), stop=(t == NT - 1))
                last.then_inc(sem("foxc_psum"), 1)
                gate(2)
                pe.wait_ge(sem("kk_square"), L + 1)
                pe.wait_ge(sem("lora_taken"), 3 * (L + 1))
                mm(bank[2][:, :], bones, E[5], start=True, stop=True).then_inc(sem("kk_sum"), 1)
                gate(3)
                pe.wait_ge(sem("rkr_ready"), L + 1)
                mm(bank[3][:, :], bones, E[5], start=True, stop=True).then_inc(sem("rkr_sum"), 1)
                pe.wait_ge(sem("rwkv_factors"), L + 1)
                pe.wait_ge(sem("c8_ready"), L + 1)
                pe.wait_ge(sem("idx_relu"), 2 * L + 2)
                for w, src in enumerate((BKT[:, 0, :, :], BKT[:, 1, :, :], F[:, F_V:F_V + 2, :])):
                    for t in range(NT):
                        for f in range(2):
                            last = nc.tensor.transpose(half(4 + w)[:, t, f * P:(f + 1) * P],
                                                       src[:, f, t * P:(t + 1) * P], ident)
                    last.then_inc(sem("tok_psum"), 1)
                pe.wait_ge(sem("tok_ready"), 3 * (L + 1))
                pe.wait_ge(sem("bonus_taken"), L + 1)
                for w in range(2):
                    for i in range(8):
                        h, t = i // 2, i % 2
                        hb = HD * (h % 2)
                        if w and t == 0:
                            pe.wait_ge(sem("gram_taken"), 8 * L + i // 2 + 1)
                        last = mm(half(2 + i // 2)[:, t, :], BKT[hb:hb + HD, w, h // 2, t * P:(t + 1) * P],
                                  ARF[hb:hb + HD, h // 2, t, :], start=True, stop=True)
                        if t:
                            last.then_inc(sem("gram_psum"), 1)
                gate(4)
                pe.wait_ge(sem("gram_taken"), 8 * L + 8)
                for lv in range(6):
                    n = 6 * L + lv
                    pe.wait_ge(sem("lm_ready"), n + 1)
                    for i in range(8):
                        last = mm(bank[2 + i // 4][:, (i % 4) * P:(i % 4 + 1) * P], LM[:, i, :],
                                  ident if lv == 0 else XI[:, i, :], start=True, stop=True)
                    last.then_inc(sem("t1_psum"), 1)
                    if lv in (1, 3, 4):
                        gate(5 + (lv > 1) + (lv > 3))
                    if lv:
                        pe.wait_ge(sem("t1_ready"), 5 * L + lv)
                        if lv < 5:
                            for i in range(8):
                                last = mm(bank[4 + i // 4][:, (i % 4) * P:(i % 4 + 1) * P], XIT[:, i, :], T1[:, i, :],
                                          start=True, stop=True)
                        for i in range(8):
                            last = mm(bank[6 + i // 4][:, (i % 4) * P:(i % 4 + 1) * P], T1[:, i, :], XIT[:, i, :],
                                      start=True, stop=True)
                        last.then_inc(sem("xu_psum"), 1)
                pe.wait_ge(sem("inverse_ready"), L + 1)
                for c in range(NCH):
                    n = NCH * L + c
                    t, tb = c // 2, CH * (c % 2)
                    tc = slice(tb, tb + CH)
                    pe.wait_ge(sem("state_ready"), (NCH + 1) * L + c + 1)
                    other = 1 - c % 2
                    for h in (other, other + 2, 1 - other, 3 - other):
                        hb, f = HD * (h % 2), h // 2
                        hc = slice(h * HD, (h + 1) * HD)
                        last = mm(bank[2][tc, hc], AR[hb:hb + HD, f, t, 0, tc], ST[hb:hb + HD, f, :],
                                  start=(h == other), stop=False, skip_group_check=True)
                        if h == other + 2:
                            fence(last)
                    for h in range(4):
                        hc = slice(h * HD, (h + 1) * HD)
                        last = mm(bank[2][tc, hc], MK[tc, 2 * h + t, 0, tc], TOK[tc, 2, t, hc],
                                  start=False, stop=True, skip_group_check=True)
                    last.then_inc(sem("r1_psum"), 1)
                    pe.wait_ge(sem("r1_ready"), n + 1)
                    for h in range(4):
                        i = 2 * h + t
                        hc = slice(h * HD, (h + 1) * HD)
                        last = mm(bank[3][tc, hc], XIT[tc, i, tc], R1[tc, hc], start=True, stop=True)
                    last.then_inc(sem("sa_psum"), 1)
                    pe.wait_ge(sem("sa_ready"), n + 1)
                    if c:
                        pe.wait_ge(sem("y_taken"), n)
                    for h in range(4):
                        hb, f = HD * (h % 2), h // 2
                        i = 2 * h + t
                        hc = slice(h * HD, (h + 1) * HD)
                        dst = bank[5][hb:hb + HD, f * HD:(f + 1) * HD]
                        mm(dst, TOK[tc, 0, t, hc], SA[tc, hc], start=True, stop=False)
                        last = mm(dst, TOK[tc, 1, t, hc], TOK[tc, 2, t, hc], start=False, stop=True)
                    last.then_inc(sem("st_psum"), 1)
                    for h in (other, other + 2, 1 - other, 3 - other):
                        hb, f = HD * (h % 2), h // 2
                        last = mm(bank[4][hb:hb + HD, f * CH:(f + 1) * CH], ST[hb:hb + HD, f, :],
                                  AR[hb:hb + HD, f, t, 1, tc], start=(f == 0), stop=False, skip_group_check=True)
                        if h == other + 2:
                            fence(last)
                    for h in range(4):
                        hb, f = HD * (h % 2), h // 2
                        i = 2 * h + t
                        hc = slice(h * HD, (h + 1) * HD)
                        dst = bank[4][hb:hb + HD, f * CH:(f + 1) * CH]
                        mm(dst, SA[tc, hc], MB[tc, i, 1, tc], start=False, stop=False, skip_group_check=True)
                        last = mm(dst, TOK[tc, 2, t, hc], MK[tc, i, 1, tc], start=False, stop=True, skip_group_check=True)
                    last.then_inc(sem("y_psum"), 1)
                pe.wait_ge(sem("y_taken"), NCH * (L + 1))
                mm(bank[2][:, :], bones, YT.rearrange("p f n -> p (f n)"), start=True, stop=True)\
                    .then_inc(sem("gn_sum"), 1)
                pe.wait_ge(sem("gn_square"), L + 1)
                mm(bank[3][:, :], bones, E[0], start=True, stop=True).then_inc(sem("gn_var"), 1)
                gate(8)
                pe.wait_ge(sem("dsa_mask"), L + 1)
                pe.wait_ge(sem("rwkv_done"), L + 1)
                attention(stage, lambda i: gate(9 + i // 4) if i % 4 == 0 and i // 4 < 7 else None)
                pe.wait_ge(sem("proj_taken"), ACT0[stage] + N_PROJ + 16)
                j = 16 * L
                for slot, parts in ((s0 + 16, ((0, 0, 4),)), (s0 + 17, ((4, 0, 2), (6, 2, 2))), (s0 + 18, ((8, 0, 2),))):
                    slot_in(slot)
                    for o0, k0, kn in parts:
                        for fp in range(4):
                            if j >= 2 and not (L and j < 16 * L + 2):
                                pe.wait_ge(sem("merge_taken"), j - 1)
                            for e in range(2):
                                for k in range(kn):
                                    last = mm(half(j % 2)[:, e, :],
                                              ring4(slot)[:, k0 + k, (2 * fp + e) * P:(2 * fp + e + 1) * P],
                                              OT[:, o0 + k, :], start=(k == 0), stop=(k == kn - 1))
                            last.then_inc(sem("gemm_done"), 1)
                            j += 1
                pe.wait_ge(sem("merged"), L + 1)
                for i in range(2):
                    down(s0 + 19 + i, XT, 4 * i, 4, i == 0, i == 1)

            def up(slot, c, n, bk, hoff, cw=S):
                for e in range(2):
                    for k in range(KT):
                        last = mm(half(bk)[:, e, :], ring8(slot)[:, k, e * cw + c * P:e * cw + (c + 1) * P], XT[:, k, :],
                                  start=(k == 0), stop=(k == KT - 1))
                last.then_inc(sem("gemm_done"), 1)

            def ffn(stage):
                s0, h0 = SLOT0[stage], H0[stage]
                with pe.Fori(0, 3) as r:
                    for i in range(RING):
                        base = loaded_value(s0 + i)
                        pe.wait_ge(sem(f"slot_loaded{(s0 + i) % RING}"), base + 32 * r)
                        for c in range(2):
                            n = 2 * i + c
                            pe.wait_ge(sem("hidden_ready"), h0 + 6 * r + max(n, 1))
                            up(s0 + i, c, n, n % 2, h0)
                for i in range(3 * RING, FT // 2):
                    slot_in(s0 + i)
                    for c in range(2):
                        pe.wait_ge(sem("hidden_ready"), h0 + 2 * i + c)
                        up(s0 + i, c, 2 * i + c, c, h0)
                pe.wait_ge(sem("hidden_ready"), h0 + FT + 1)
                for i in range(FFN_DOWN):
                    down(s0 + FT // 2 + i, F, 4 * i, min(4, FT - 4 * i), i == 0, i == FFN_DOWN - 1)

            def moe():
                s0, h0 = SLOT0["moe"], H0["moe"]
                for t in range(NT):
                    for k in range(KT):
                        last = mm(bank[6][:, t * NEXP:(t + 1) * NEXP], XT[:, k, t * P:(t + 1) * P], RW[:, k, :],
                                  start=(k == 0), stop=(k == KT - 1))
                last.then_inc(sem("router_psum"), 1)
                with pe.Fori(0, NEXP) as e:
                    for i in range(6):
                        pe.wait_ge(sem(f"slot_loaded{(s0 + i) % RING}"), loaded_value(s0 + i) + 80 * e)
                        for c in range(min(2, ET - 2 * i)):
                            n = 2 * i + c
                            pe.wait_ge(sem("hidden_ready"), h0 + ET * e + max(n, 1))
                            up(s0 + i, c, n, n % 2, h0)
                    pe.wait_ge(sem("hidden_ready"), h0 + ET * e + ET + 1)
                    pe.wait_ge(sem("expert_taken"), 4 * e + 1)
                    for i in range(3):
                        slot = s0 + 6 + i
                        pe.wait_ge(sem(f"slot_loaded{slot % RING}"), loaded_value(slot) + 80 * e)
                        waited[0] = slot
                        down(slot, F, 4 * i, min(4, ET - 4 * i), i == 0, i == 2)

            def head_norm(n0, groups, group):
                for i in groups:
                    pe.wait_ge(sem("hn_square"), n0 + i + 1)
                    if i >= 2:
                        pe.wait_ge(sem("hn_done"), n0 + i - 1)
                    if group == 1:
                        last = mm(bank[2 + i % 2][:, :], bones, NQ[:, (i % 2) * 512:(i % 2 + 1) * 512], start=True, stop=True)
                    else:
                        for e in range(2):
                            last = mm(bank[2 + i % 2][:, 0:S], ones, NQ[:, (i % 2) * 512 + e * S:(i % 2) * 512 + (e + 1) * S],
                                      start=(e == 0), stop=(e == 1))
                    last.then_inc(sem("hn_sum"), 1)

            def ev():
                s0 = SLOT0["ev"]
                pe.wait_ge(sem("xn_ready"), NORM_NO["ev"] - 3)
                transposed("ev", XN)
                for i in range(4):
                    feat("ev", s0 + i // 2, i, (i % 2) * 2 * P)
                for t in range(NT):
                    tok("ev", s0 + 2, 4 + t, 0, 512, [t])
                    head_norm(0, [t], 1)
                for i in range(2):
                    feat("ev", s0 + 3, 6 + i, i * 2 * P)
                    head_norm(0, [2 + i], 1)
                for t in range(NT):
                    tok("ev", s0 + 4, 8 + t, 0, 512, [t])
                for i in range(4):
                    pe.wait_ge(sem("hn_done"), i + 1)
                    if i >= 2:
                        pe.wait_ge(sem("rope_done"), i - 1)
                    mm(bank[4 + i % 2][:, :], rot, F[:, 2 * i:2 * i + 2, :], start=True, stop=True)\
                        .then_inc(sem("rot_psum"), 1)
                pe.wait_ge(sem("gm_loaded"), 96)
                for g in range(8):
                    last = nc.tensor.transpose(bank[6 + g // 4][:, (g % 4) * P:(g % 4 + 1) * P], WS[:, g, :], ident)
                last.then_inc(sem("wst_psum"), 1)
                pe.wait_ge(sem("rope_done"), 4)
                pe.wait_ge(sem("vn_ready"), 1)
                for g in range(8):
                    hb = HD * (g % 2)
                    for t in range(NT):
                        last = mm(half(6 + g // 4)[hb:hb + HD, (g // 2) % 2, t * P:(t + 1) * P],
                                  V2[:, t, 512 + g * HD:512 + (g + 1) * HD], WST[:, g, :], start=True, stop=True)
                last.then_inc(sem("mixed_psum"), 1)
                pe.wait_ge(sem("gmlp_done"), 1)
                attention("ev")
                for i in range(2):
                    down(s0 + 5 + i, OT, 4 * i, 4, i == 0, i == 1)

            def xa(L):
                stage = f"xa{L}"
                s0 = SLOT0[stage]
                pe.wait_ge(sem("xn_ready"), NORM_NO[f"xq{L}"] - 3)
                transposed(f"xq{L}", XN)
                pe.wait_ge(sem("xn_ready"), NORM_NO[f"xkv{L}"] - 3)
                transposed(f"xkv{L}", XN)
                for i in range(4):
                    feat(stage, s0 + i // 2, i, (i % 2) * 2 * P)
                for i in range(4):
                    feat(stage, s0 + 2 + i // 2, 4 + i, (i % 2) * 2 * P, src=MT)
                for i in range(4):
                    tok(stage, s0 + 4 + i // 2, 8 + i, 0, 512, [i % 2], src=MT)
                    head_norm(4 + 12 * L, [2 * i, 2 * i + 1], 2)
                pe.wait_ge(sem("hn_done"), 12 + 12 * L)
                pe.wait_ge(sem("proj_taken"), ACT0[stage] + 12)
                attention(stage)
                for i in range(2):
                    down(s0 + 6 + i, OT, 4 * i, 4, i == 0, i == 1)

            def gla():
                s0 = SLOT0["gla"]
                pe.wait_ge(sem("xn_ready"), NORM_NO["gla"] - 3)
                transposed("gla", XN)
                for k in range(KT):
                    last = mm(bank[6][0:16, 0:S], G1[:, k, :], XT[:, k, :], start=(k == 0), stop=(k == KT - 1))
                last.then_inc(sem("g1_psum"), 1)
                for i in range(4):
                    feat("gla", s0 + i // 2, i, (i % 2) * 2 * P)
                pe.wait_ge(sem("g1_ready"), 1)
                for h in range(4):
                    last = mm(half(2 + h // 2)[:, h % 2, :], LORA[0:16, h * P:(h + 1) * P], GL1, start=True, stop=True)
                last.then_inc(sem("g2_psum"), 1)
                for i in range(4):
                    tok("gla", s0 + 2 + i // 2, 4 + i, 0, 512, [i % 2])
                for i in range(4):
                    feat("gla", s0 + 4 + i // 2, 8 + i, (i % 2) * 2 * P)
                pe.wait_ge(sem("gla_factors"), 1)
                pe.wait_ge(sem("proj_taken"), ACT0["gla"] + 12)
                for t in range(NT):
                    for h in range(4):
                        last = nc.tensor.transpose(bank[2 + t][:, h * P:(h + 1) * P],
                                                   KS[:, h * S + t * P:h * S + (t + 1) * P], ident)
                last.then_inc(sem("ksm_psum"), 1)
                for h in range(4):
                    for t in range(NT):
                        last = mm(bank[4 + h // 2][:, ((h % 2) * 2 + t) * P:((h % 2) * 2 + t + 1) * P],
                                  F[:, 4 + h, t * P:(t + 1) * P], F[:, h, t * P:(t + 1) * P], start=True, stop=True)
                last.then_inc(sem("att_psum"), 1)
                pe.wait_ge(sem("ksm_ready"), 1)
                pe.wait_ge(sem("att_ready"), 1)
                for c in range(NCH):
                    t, tb = c // 2, CH * (c % 2)
                    tc = slice(tb, tb + CH)
                    pe.wait_ge(sem("gs_ready"), c + 1)
                    if c:
                        pe.wait_ge(sem("go_taken"), c)
                    for h in range(4):
                        for e in range(2):
                            dst = bank[6][:, (2 * h + e) * CH:(2 * h + e + 1) * CH]
                            vc = slice(h * S + e * P, h * S + (e + 1) * P)
                            mm(dst, V2[tc, t, vc], ATT[tc, h, t, tc], start=True, stop=False)
                            last = mm(dst, GS[:, h, e * P:(e + 1) * P], F[:, h, c * CH:(c + 1) * CH],
                                      start=False, stop=True)
                    last.then_inc(sem("go_psum"), 1)
                    for h in range(4):
                        last = mm(half(2 + h // 2)[:, h % 2, :], KSM[tc, t, h * P:(h + 1) * P],
                                  V2[tc, t, h * S:(h + 1) * S], start=True, stop=True)
                    last.then_inc(sem("ds_psum"), 1)
                pe.wait_ge(sem("gs_ready"), NCH + 1)
                head_norm(12, range(4), 2)
                pe.wait_ge(sem("gla_done"), 1)
                for i in range(2):
                    down(s0 + 6 + i, OT, 4 * i, 4, i == 0, i == 1)

            def normed(name, src):
                pe.wait_ge(sem("xn_ready"), NORM_NO[name] - 3)
                transposed(name, src)

            mix(0)
            pe.wait_ge(sem("ln_done"), 1)
            transposed("ffn0", X)
            ffn("ffn0")
            mix(1)
            pe.wait_ge(sem("ln_done"), 3)
            transposed("moe", X)
            moe()
            ev()
            xa(0)
            normed("ffn1", XN)
            ffn("ffn1")
            gla()
            xa(1)
            normed("ffn2", XN)
            ffn("ffn2")

        @block.scalar
        def _(act):
            av = nc.scalar.activation
            chain = [0]

            def step(ins):
                chain[0] += 1
                ins.then_inc(sem("act_step"), 1)
                act.wait_ge(sem("act_step"), chain[0])

            def xt_out(name, dst, gain=None):
                n = NORM_NO[name]
                for j in range(4):
                    act.wait_ge(sem("xt_psum"), 4 * n + j + 1)
                    if gain is None:
                        last = av(dst[:, 2 * j:2 * j + 2, :], half(2 + j), ACT.Copy)
                    else:
                        for i in range(2):
                            last = av(dst[:, 2 * j + i, :], half(2 + j)[:, i, :], ACT.Copy, scale=col(gain, 2 * j + i))
                    last.then_inc(sem("xt_ready"), 1)

            def proj(stage, i, outs):
                act.wait_ge(sem("gemm_done"), JOB0[stage] + i + 1)
                for dst, src, fn, bias in outs:
                    last = av(dst, src, fn) if bias is None else av(dst, src, fn, bias=bias)
                last.then_inc(sem("proj_taken"), 1)

            def feat_out(stage, i, dest, fn=ACT.Copy):
                proj(stage, i, [(F[:, dest:dest + 2, :], half(i % 2), fn, None)])

            def exps(n, unit):
                kind, h, t = unit
                nk = unit_at(kind, h, t)[0]
                c0 = 8 * (n % 4)
                act.wait_ge(sem("nmax_ready"), n + 1)
                if kind == "swa":
                    av(TINY[:, c0 + 2:c0 + 3], SROW[:, SINK[0] + h:SINK[0] + h + 1], ACT.Exp, bias=TINY[:, c0:c0 + 1])
                av(SMX[:, n % 4, 0:nk * P], SMX[:, n % 4, 0:nk * P], ACT.Exp, bias=TINY[:, c0:c0 + 1],
                   accum_out=TINY[:, c0 + 1:c0 + 2]).then_inc(sem("exp_done"), 1)

            def pt_out(n, unit):
                kind, h, t = unit
                nk = unit_at(kind, h, t)[0]
                act.wait_ge(sem("pt_psum"), n + 1)
                if n >= 2:
                    act.wait_ge(sem("ctx_psum"), n - 1)
                av(PT[:, n % 2, 0:nk * P], half(4 + n % 2)[:, 0, 0:nk * P], ACT.Copy).then_inc(sem("pt_ready"), 1)

            def ctx_out(n, unit):
                kind, h, t = unit
                _, _, _, (parts, outs) = unit_at(kind, h, t)
                ne = outs.stop - outs.start
                act.wait_ge(sem("ctx_psum"), n + 1)
                av(OT[parts, outs, t * P:(t + 1) * P],
                   bank[6 + n % 2][parts, 0:ne * P].rearrange("p (e n) -> p e n", e=ne), ACT.Copy)\
                    .then_inc(sem("ctx_taken"), 1)

            SINK = [0]

            def attention(stage, filler=None):
                n0, units = UNITS[stage]
                for i in range(len(units) + 3):
                    if i < len(units):
                        exps(n0 + i, units[i])
                    if filler is not None:
                        filler(i)
                    if 2 <= i < len(units) + 2:
                        pt_out(n0 + i - 2, units[i - 2])
                    if i >= 3:
                        ctx_out(n0 + i - 3, units[i - 3])

            def mix(L):
                stage = f"mix{L}"
                SINK[0] = 8 * L
                if L == 0:
                    act.wait_ge(sem("params_in"), 80)
                xt_out(stage, XT)
                for i, (name, kind, c, dest) in enumerate(MIX_PLAN):
                    b = bank[i % 2]
                    if kind == "feat":
                        feat_out(stage, i, dest)
                    elif kind == "dup64":
                        proj(stage, i, [(F[o:o + HD, dest, :], b[0:HD, 0:S], ACT.Copy, None) for o in (0, HD)])
                    elif kind == "dup128":
                        proj(stage, i, [(F[o:o + HD, dest + g, :], b[g * HD:(g + 1) * HD, 0:S], ACT.Copy, None)
                                        for g in range(2) for o in (0, HD)])
                    elif kind == "tok":
                        w = c[1]
                        proj(stage, i, [(TM[:, :, dest:dest + w], b[:, 0:NT * w].rearrange("p (t n) -> p t n", t=NT),
                                         ACT.Copy, None)])
                    else:
                        proj(stage, i, [(TM[:, c[0], dest:dest + c[2]], b[:, 0:c[2]], ACT.Copy, None)])
                    if i == 7:
                        act.wait_ge(sem("shift_done"), L + 1)
                        av(F[0:64, F_LO, :], F[0:64, F_LO, :], ACT.Tanh)
                        av(F[:, F_LO + 1, :], F[:, F_LO + 1, :], ACT.Sigmoid).then_inc(sem("lora_in"), 1)

                def gate(j):
                    i = N_PROJ + j
                    proj(stage, i, [(G[:, 2 * j + e, :], half(i % 2)[:, e, :], ACT.Sigmoid, col(f"gate{L}", 2 * j + e))
                                    for e in range(2)])

                act.wait_ge(sem("lora_out"), 3 * L + 1)
                for m in range(2):
                    last = av(E[0][:, m * S:(m + 1) * S], half(2)[:, m, :], ACT.Sigmoid, bias=col(f"w0{L}", m))
                last.then_inc(sem("lora_taken"), 1)
                act.wait_ge(sem("lora_out"), 3 * L + 2)
                for m in range(2):
                    last = av(E[2][:, m * S:(m + 1) * S], half(3)[:, m, :], ACT.Sigmoid, bias=col(f"a0{L}", m))
                last.then_inc(sem("lora_taken"), 1)
                act.wait_ge(sem("lora_out"), 3 * L + 3)
                av(GG, half(4), ACT.Copy).then_inc(sem("lora_taken"), 1)
                for t in range(NT):
                    act.wait_ge(sem("idx_scores"), 2 * L + t + 1)
                    if t:
                        act.wait_ge(sem("idx_acc"), 2 * L + 1)
                    av(REL[:, 0:2, :], half(6), ACT.Relu, scale=HD ** -0.5)
                    av(REL[:, 2:4, :], half(7), ACT.Relu, scale=HD ** -0.5).then_inc(sem("idx_relu"), 1)
                    gate(t)
                act.wait_ge(sem("foxz_ready"), L + 1)
                z = TINY[:, 40:48]
                step(av(TINY[:, 48:56], z, ACT.Abs))
                step(av(TINY[:, 48:56], TINY[:, 48:56], ACT.Exp, scale=-1.0))
                av(TINY[:, 48:56], TINY[:, 48:56], ACT.Ln, bias=1.0).then_inc(sem("foxl_ready"), 1)
                gate(2)
                act.wait_ge(sem("scan_ready"), L + 1)
                av(E[3], E[1], ACT.Exp)
                av(E[4], E[1], ACT.Exp, scale=-1.0)
                av(E[6], E[6], ACT.Exp).then_inc(sem("exps_ready"), 1)
                act.wait_ge(sem("kk_sum"), L + 1)
                av(E[5], bank[2][:, :], ACT.Sqrt, bias=col("eps_kk")).then_inc(sem("kk_root"), 1)
                gate(3)
                for w in range(3):
                    act.wait_ge(sem("tok_psum"), 3 * L + w + 1)
                    av(TOK[:, w, :, :], half(4 + w), ACT.Copy).then_inc(sem("tok_ready"), 1)
                gate(4)
                for lv in range(1, 6):
                    act.wait_ge(sem("t1_psum"), 6 * L + lv + 1)
                    if lv > 1:
                        act.wait_ge(sem("xu_psum"), 5 * L + lv - 1)
                    av(T1[:, 0:4, :], bank[2][:, :].rearrange("p (i n) -> p i n", i=4), ACT.Copy)
                    av(T1[:, 4:8, :], bank[3][:, :].rearrange("p (i n) -> p i n", i=4), ACT.Copy)\
                        .then_inc(sem("t1_ready"), 1)
                    if lv in (1, 3, 4):
                        gate(5 + (lv > 1) + (lv > 3))
                for c in range(NCH):
                    act.wait_ge(sem("y_psum"), NCH * L + c + 1)
                    av(YT[:, :, c * CH:(c + 1) * CH], bank[4][:, 0:2 * CH].rearrange("p (f n) -> p f n", f=2), ACT.Copy)\
                        .then_inc(sem("y_taken"), 1)
                act.wait_ge(sem("gn_var"), L + 1)
                av(E[1], bank[3][:, :], ACT.Sqrt, scale=1.0 / HD, bias=col("eps_gn")).then_inc(sem("gn_root"), 1)
                act.wait_ge(sem("rwkv_done"), L + 1)
                gate(8)
                attention(stage, lambda i: gate(9 + i // 4) if i % 4 == 0 and i // 4 < 7 else None)

            def root(count, scale, eps):
                act.wait_ge(sem("ms_ready"), count)
                av(TINY[:, 66:68], TINY[:, 64:66], ACT.Sqrt, scale=scale, bias=col(eps)).then_inc(sem("root_ready"), 1)

            def silu(n, bk):
                av(SIL[:, bk, :], half(bk)[:, 0, :], ACT.Silu).then_inc(sem("silu_ready"), 1)

            def ffn(stage):
                job = JOB0[stage]
                with act.Fori(0, 3) as r:
                    for n in range(6):
                        act.wait_ge(sem("gemm_done"), job + 6 * r + n + 1)
                        silu(n, n % 2)
                for n in range(18, FT):
                    act.wait_ge(sem("gemm_done"), job + n + 1)
                    silu(n, n % 2)

            def moe():
                job = JOB0["moe"]
                act.wait_ge(sem("router_top"), 1)
                av(TINY[:, 70:72], TINY[:, 68:70], ACT.Exp).then_inc(sem("router_exp"), 1)
                with act.Fori(0, NEXP) as e:
                    for n in range(ET):
                        act.wait_ge(sem("gemm_done"), job + EXP_JOBS * e + n + 1)
                        silu(n, n % 2)

            def head_root(n0, groups, width):
                for i in groups:
                    act.wait_ge(sem("hn_sum"), n0 + i + 1)
                    w = 512 if width == HD else S
                    av(NQ[:, (i % 2) * 512:(i % 2) * 512 + w], bank[2 + i % 2][:, 0:w], ACT.Sqrt, scale=1.0 / width,
                       bias=col("eps_rms")).then_inc(sem("hn_root"), 1)

            def tok_out(stage, i, t, c0, fn=ACT.Copy):
                proj(stage, i, [(V2[:, t, c0:c0 + 512], bank[i % 2][:, :], fn, None)])

            def ev():
                root(5, 1.0 / D, "eps_rms")
                xt_out("ev", XT, "norm_mix0")
                for i in range(4):
                    feat_out("ev", i, 2 * i)
                for t in range(NT):
                    tok_out("ev", 4 + t, t, 0)
                    head_root(0, [t], HD)
                for i in range(2):
                    feat_out("ev", 6 + i, 8 + 2 * i, ACT.Gelu)
                    head_root(0, [2 + i], HD)
                for t in range(NT):
                    tok_out("ev", 8 + t, t, 512, ACT.Gelu)
                act.wait_ge(sem("angle_ready"), 1)
                av(SIN, COS, ACT.Sin)
                step(av(COS, COS, ACT.Abs))
                av(COS, COS, ACT.Sin, scale=-1.0, bias=col("half_pi")).then_inc(sem("rope_table"), 1)
                act.wait_ge(sem("gvar_ready"), 1)
                av(TINY[:, 96:112], TINY[:, 80:96], ACT.Sqrt, scale=1.0 / HD, bias=col("eps_rms"))\
                    .then_inc(sem("groot_ready"), 1)
                attention("ev")

            def xa(L):
                stage = f"xa{L}"
                root(6 + 4 * L, 1.0 / D, "eps_rms")
                xt_out(f"xq{L}", XT, f"norm_q{L}")
                root(7 + 4 * L, 1.0 / D, "eps_rms")
                xt_out(f"xkv{L}", MT, f"norm_kv{L}")
                for i in range(8):
                    feat_out(stage, i, 2 * i)
                for i in range(4):
                    tok_out(stage, 8 + i, i % 2, 512 * (i // 2))
                    head_root(4 + 12 * L, [2 * i, 2 * i + 1], S)
                attention(stage)

            def gla():
                root(9, 1.0 / D, "eps_rms")
                xt_out("gla", XT, "norm_mix1")
                act.wait_ge(sem("g1_psum"), 1)
                av(GL1, bank[6][0:16, 0:S], ACT.Copy).then_inc(sem("g1_ready"), 1)
                for i in range(4):
                    feat_out("gla", i, 2 * i)
                act.wait_ge(sem("g2_psum"), 1)
                for h in range(4):
                    last = av(GB[:, h * S:(h + 1) * S], half(2 + h // 2)[:, h % 2, :], ACT.Identity, bias=col("b_g", h))
                step(last)
                step(av(GE, GB, ACT.Abs))
                step(av(GE, GE, ACT.Exp, scale=-1.0))
                av(GE, GE, ACT.Ln, bias=1.0).then_inc(sem("gl_ready"), 1)
                for i in range(4):
                    tok_out("gla", 4 + i, i % 2, 512 * (i // 2))
                for i in range(4):
                    feat_out("gla", 8 + i, 8 + 2 * i, ACT.Silu)
                act.wait_ge(sem("gscan_ready"), 1)
                av(GE, GB, ACT.Exp).then_inc(sem("gexp_ready"), 1)
                act.wait_ge(sem("gexp_used"), 1)
                av(GE, GB, ACT.Exp, scale=-1.0).then_inc(sem("gexp_ready"), 1)
                act.wait_ge(sem("glast_ready"), 1)
                av(KS, KS, ACT.Exp).then_inc(sem("gexp_ready"), 1)
                act.wait_ge(sem("ksm_psum"), 1)
                for t in range(NT):
                    last = av(KSM[:, t, :], bank[2 + t][:, :], ACT.Copy)
                last.then_inc(sem("ksm_ready"), 1)
                for c in range(NCH):
                    act.wait_ge(sem("go_psum"), c + 1)
                    av(OT[:, 0:8, c * CH:(c + 1) * CH], bank[6][:, :].rearrange("p (e n) -> p e n", e=8), ACT.Copy)\
                        .then_inc(sem("go_taken"), 1)
                head_root(12, range(4), S)

            mix(0)
            root(1, 1.0, "eps_ln")
            xt_out("ffn0", XT)
            ffn("ffn0")
            root(2, 1.0, "eps_ln")
            mix(1)
            root(3, 1.0, "eps_ln")
            xt_out("moe", XT)
            moe()
            root(4, 1.0, "eps_ln")
            ev()
            xa(0)
            root(8, 1.0 / D, "eps_rms")
            xt_out("ffn1", XT, "norm_ffn0")
            ffn("ffn1")
            gla()
            xa(1)
            root(12, 1.0 / D, "eps_rms")
            xt_out("ffn2", XT, "norm_ffn1")
            ffn("ffn2")

        @block.vector
        def _(dve):
            v = nc.vector
            chain = [0]
            made = {}

            def step(ins):
                chain[0] += 1
                ins.then_inc(sem("dve_step"), 1)
                dve.wait_ge(sem("dve_step"), chain[0])

            def signal(ins, name):
                made[name] = made.get(name, 0) + 1
                ins.then_inc(sem(name), 1)
                dve.wait_ge(sem(name), made[name])

            def cols(t, lo, n):
                return t[:, lo:lo + n]

            def stt(out, in0, scalar, in1, op0, op1, **kw):
                return v.scalar_tensor_tensor(out=out, in0=in0, scalar=scalar, in1=in1, op0=op0, op1=op1, **kw)

            MASK = {"swa": window, "fox": causal, "moba": causal, "dsa": SEL}
            LAYER = [0]

            def scaled(n, unit):
                kind, h, t = unit
                w = unit_at(kind, h, t)[0] * P
                c0 = 8 * (n % 4)
                dve.wait_ge(sem("scores_ready"), n + 1)
                if n >= 4:
                    dve.wait_ge(sem("pt_psum"), n - 3)
                src, dst = bank[2 + n % 2][:, 0:w], SMX[:, n % 4, 0:w]
                if kind == "cross":
                    signal(v.tensor_scalar(dst, src, SCORE_SCALE[kind], None, ALU.mult), "scores_taken")
                else:
                    signal(stt(dst, src, SCORE_SCALE[kind], MASK[kind][:, t, 0:w], ALU.mult, ALU.add), "scores_taken")
                nm = TINY[:, c0:c0 + 1]
                red = v.tensor_reduce(nm, dst, axis=AX, op=ALU.max, negate=True)
                if kind == "swa":
                    step(red)
                    s0 = 8 * LAYER[0] + h
                    red = stt(nm, SROW[:, s0:s0 + 1], -1.0, nm, ALU.mult, ALU.min)
                signal(red, "nmax_ready")

            def normalised(n, unit):
                kind, h, t = unit
                w = unit_at(kind, h, t)[0] * P
                c0 = 8 * (n % 4)
                dve.wait_ge(sem("exp_done"), n + 1)
                rs, es, ri = (TINY[:, c0 + e:c0 + e + 1] for e in (1, 2, 3))
                if kind == "swa":
                    step(v.tensor_tensor(rs, rs, es, ALU.add))
                step(v.reciprocal(ri, rs))
                signal(v.tensor_scalar(SMX[:, n % 4, 0:w], SMX[:, n % 4, 0:w], ri, None, ALU.mult), "probs_ready")

            def attention(stage):
                n0, units = UNITS[stage]
                for i in range(len(units) + 1):
                    if i < len(units):
                        scaled(n0 + i, units[i])
                    if i:
                        normalised(n0 + i - 1, units[i - 1])

            def mix(L):
                stage = f"mix{L}"
                LAYER[0] = L
                a0 = ACT0[stage]
                if L == 0:
                    dve.wait_ge(sem("params_in"), 80)
                dve.wait_ge(sem("proj_taken"), a0 + 4)
                R8 = F[:, F_R:F_R + 8, :]
                v.tensor_tensor(DT[:, :, 1:S], R8[:, :, 0:S - 1], R8[:, :, 1:S], ALU.subtract)
                step(v.tensor_scalar(DT[:, :, 0:1], R8[:, :, 0:1], -1.0, None, ALU.mult))
                for m in range(8):
                    last = stt(F[:, F_R + m, :], DT[:, m, :], col(f"mu{L}", m), F[:, F_R + m, :], ALU.mult, ALU.add)
                signal(last, "shift_done")
                for m in range(2):
                    last = v.tensor_scalar(cols(E[7], m * S, S), F[:, F_K + m, :], col(f"k_k{L}", m), None, ALU.mult)
                step(last)
                signal(v.tensor_tensor(E[5], E[7], E[7], ALU.mult), "kk_square")
                dve.wait_ge(sem("lora_taken"), 3 * L + 1)
                step(v.tensor_scalar(E[0], E[0], -float(np.exp(-0.5)), None, ALU.mult))
                step(v.tensor_tensor_scan(E[1], keep4[:, 0:512], E[0], 0.0, ALU.mult, ALU.add))
                signal(v.tensor_tensor(E[6], E[1], E[0], ALU.subtract), "scan_ready")
                dve.wait_ge(sem("idx_relu"), 2 * L + 1)
                iw = TINY[:, 56:64].rearrange("p (t h) -> p t h", t=NT)
                step(v.tensor_scalar(iw, TM[:, :, TM_DSA_W:TM_DSA_W + 4], 0.5, None, ALU.mult))
                for t in range(NT):
                    dve.wait_ge(sem("idx_relu"), 2 * L + t + 1)
                    step(v.tensor_scalar(SCORE[:, t, :], REL[:, 0, :], iw[:, t, 0:1], None, ALU.mult))
                    for h in range(1, 4):
                        ins = stt(SCORE[:, t, :], REL[:, 2 * (h % 2) + h // 2, :], iw[:, t, h:h + 1], SCORE[:, t, :], ALU.mult, ALU.add)
                        if h < 3:
                            step(ins)
                    signal(ins, "idx_acc")
                z = TINY[:, 40:48].rearrange("p (t h) -> p t h", t=NT)
                fb = SROW[:, 16 + 4 * L:20 + 4 * L].unsqueeze(1).to_broadcast([P, NT, 4])
                signal(v.tensor_tensor(z, TM[:, :, TM_FOX_F:TM_FOX_F + 4], fb, ALU.add), "foxz_ready")
                step(v.tensor_tensor(SCORE, SCORE, admit, ALU.add))
                dve.wait_ge(sem("foxl_ready"), L + 1)
                signal(stt(TM[:, :, TM_FOX_F:TM_FOX_F + 4], z, 0.0, TINY[:, 48:56].rearrange("p (t h) -> p t h", t=NT),
                           ALU.min, ALU.subtract), "logf_ready")
                dve.wait_ge(sem("lora_taken"), 3 * L + 2)
                for m in range(2):
                    last = v.tensor_scalar(cols(E[0], m * S, S), cols(E[2], m * S, S), -1.0, col(f"k_a{L}", m),
                                           ALU.add, ALU.mult)
                step(last)
                for m in range(2):
                    last = stt(F[:, F_K + m, :], cols(E[0], m * S, S), 1.0, F[:, F_K + m, :], ALU.add, ALU.mult)
                step(last)
                dve.wait_ge(sem("foxc_psum"), L + 1)
                signal(v.tensor_scalar(C8[0:4, :], bank[5][0:4, 0:S], 1.0 / SCORE_SCALE["fox"], None, ALU.mult), "c8_ready")
                dve.wait_ge(sem("kk_root"), L + 1)
                step(v.reciprocal(E[5], E[5]))
                step(v.tensor_tensor(E[7], E[7], E[5], ALU.mult))
                for m in range(2):
                    last = stt(cols(E[5], m * S, S), F[:, F_R + m, :], col(f"r_k{L}", m), F[:, F_K + m, :],
                               ALU.mult, ALU.mult)
                signal(last, "rkr_ready")
                dve.wait_ge(sem("exps_ready"), L + 1)

                def tiles(x):
                    return x.rearrange("p (t n) -> p t n", t=NT)

                for f in range(2):
                    stt(AR[:, f, :, 0, :], tiles(cols(E[7], f * S, S)), -1.0, tiles(cols(E[6], f * S, S)), ALU.mult, ALU.mult)
                    v.tensor_tensor(AR[:, f, :, 1, :], tiles(F[:, F_R + f, :]), tiles(cols(E[3], f * S, S)), ALU.mult)
                v.tensor_copy(TINY[:, 112:120].rearrange("p (x o) -> p x o", o=1),
                              E[3].rearrange("p (x n) -> p x n", n=CH)[:, :, CH - 1:CH])
                two = lambda x: x.rearrange("p (f n) -> p f n", f=2)
                v.tensor_tensor(BKT[:, 1, :, :], F[:, F_K:F_K + 2, :], two(E[4]), ALU.mult)
                step(v.tensor_tensor(E[1], E[7], E[2], ALU.mult))
                signal(v.tensor_tensor(BKT[:, 0, :, :], two(E[1]), two(E[4]), ALU.mult), "rwkv_factors")
                dve.wait_ge(sem("rkr_sum"), L + 1)
                signal(v.tensor_tensor(OT[:, 6:8, :], half(3), F[:, F_V:F_V + 2, :], ALU.mult), "bonus_taken")
                signal(v.memset(ST, 0.0), "state_ready")
                dve.wait_ge(sem("grams_cleared"), L + 1)
                mask = strict_incl.bitcast(i32).unsqueeze(1).to_broadcast([P, 2, 2 * P])
                for n in range(8):
                    dve.wait_ge(sem("gram_psum"), 8 * L + n + 1)
                    lo = 16 + 8 * (n // 4) + 2 * (n % 4)
                    signal(v.copy_predicated(G[:, lo:lo + 2, :], mask, half(2 + n % 4)), "gram_taken")

                def select(r):
                    t = r // (TOPK // 8)
                    best = TINY[:, 72:80]
                    step(v.max(out=best, in_=SCORE[:, t, :]))
                    step(v.match_replace(out=SCORE[:, t, :], in_to_replace=best, in_values=SCORE[:, t, :],
                                         imm_value=TAKEN))

                eight = lambda x: x.unsqueeze(1).to_broadcast([P, 8, P])
                four = lambda x: x.unsqueeze(1).to_broadcast([P, 4, P])
                quad = lambda b: bank[b][:, :].rearrange("p (i n) -> p i n", i=4)
                signal(v.tensor_tensor(LM, MB[:, :, 0, :], eight(levels[:, 0, :]), ALU.mult), "lm_ready")
                step(v.tensor_tensor(XIT, LM, eight(ident), ALU.add))
                dve.wait_ge(sem("t1_psum"), 6 * L + 1)
                v.tensor_tensor(XI[:, 0:4, :], quad(2), four(ident), ALU.add)
                step(v.tensor_tensor(XI[:, 4:8, :], quad(3), four(ident), ALU.add))
                for lv in range(1, 6):
                    dve.wait_ge(sem("t1_psum"), 6 * L + lv)
                    ins = v.tensor_tensor(LM, MB[:, :, 0, :], eight(levels[:, lv, :]), ALU.mult)
                    if lv > 1:
                        step(ins)
                        dve.wait_ge(sem("xu_psum"), 5 * L + lv - 1)
                        v.tensor_tensor(XI[:, 0:4, :], quad(4), XI[:, 0:4, :], ALU.add)
                        v.tensor_tensor(XI[:, 4:8, :], quad(5), XI[:, 4:8, :], ALU.add)
                        v.tensor_tensor(XIT[:, 0:4, :], quad(6), XIT[:, 0:4, :], ALU.add)
                        ins = v.tensor_tensor(XIT[:, 4:8, :], quad(7), XIT[:, 4:8, :], ALU.add)
                    signal(ins, "lm_ready")
                    for r in range(2 * lv - 2, 2 * lv):
                        select(r)
                dve.wait_ge(sem("xu_psum"), 5 * L + 5)
                v.tensor_tensor(XIT[:, 0:4, :], quad(6), XIT[:, 0:4, :], ALU.add)
                signal(v.tensor_tensor(XIT[:, 4:8, :], quad(7), XIT[:, 4:8, :], ALU.add), "inverse_ready")
                for c in range(NCH):
                    n = NCH * L + c
                    tc = slice(CH * (c % 2), CH * (c % 2) + CH)
                    dve.wait_ge(sem("r1_psum"), n + 1)
                    signal(v.tensor_copy(R1[tc, :], bank[2][tc, 0:256]), "r1_ready")
                    dve.wait_ge(sem("sa_psum"), n + 1)
                    signal(v.tensor_copy(SA[tc, :], bank[3][tc, 0:256]), "sa_ready")
                    dve.wait_ge(sem("y_psum"), n + 1)
                    step(v.tensor_tensor(ST, bank[5][:, 0:2 * HD].rearrange("p (f n) -> p f n", f=2), ST, ALU.add))
                    for f in range(2):
                        last = v.tensor_scalar(ST[:, f, :], ST[:, f, :], TINY[:, 112 + 4 * f + c:113 + 4 * f + c],
                                               None, ALU.mult)
                    signal(last, "state_ready")
                    select(10 + c)
                dve.wait_ge(sem("gn_sum"), L + 1)
                dve.wait_ge(sem("y_taken"), NCH * (L + 1))
                yt = YT.rearrange("p f n -> p (f n)")
                step(stt(yt, bank[2][:, :], -1.0 / HD, yt, ALU.mult, ALU.add))
                signal(v.tensor_tensor(E[0], yt, yt, ALU.mult), "gn_square")
                for r in (14, 15):
                    select(r)
                signal(v.tensor_scalar(SEL[:, :, :], SCORE, -2e30, NEG, ALU.is_ge, ALU.mult), "dsa_mask")
                dve.wait_ge(sem("gn_root"), L + 1)
                step(v.reciprocal(E[1], E[1]))
                step(v.tensor_tensor(yt, yt, E[1], ALU.mult))
                for f in range(2):
                    last = v.tensor_scalar(YT[:, f, :], YT[:, f, :], col(f"gn_g{L}", f), col(f"gn_b{L}", f),
                                           ALU.mult, ALU.add)
                step(last)
                step(v.tensor_tensor(YT, YT, OT[:, 6:8, :], ALU.add))
                signal(v.tensor_tensor(OT[:, 4:6, :], YT, GG, ALU.mult), "rwkv_done")
                attention(stage)
                tmp = wk(3584, 1024).rearrange("p (b h n) -> p b h n", b=2, h=2)
                job = JOB0[stage] + MIX_JOBS["brA"]
                for j in range(16):
                    fp = j % 4
                    dve.wait_ge(sem("gemm_done"), job + j + 1)
                    g = G[:, 2 * j:2 * j + 2, :]
                    acc = XT[:, 2 * fp:2 * fp + 2, :]
                    if j < 4:
                        signal(v.tensor_tensor(acc, g, half(j % 2), ALU.mult), "merge_taken")
                    else:
                        signal(v.tensor_tensor(tmp[:, j % 2, :, :], g, half(j % 2), ALU.mult), "merge_taken")
                        ins = v.tensor_tensor(acc, tmp[:, j % 2, :, :], acc, ALU.add)
                        if j == 15:
                            signal(ins, "merged")
                        else:
                            step(ins)

            def layer_norm(k, stage):
                if stage != "moe":
                    dve.wait_ge(sem("gemm_done"), used_value(SLOT0[stage] + SLOTS_OF[stage] - 1))
                for t in range(NT):
                    for h in range(2):
                        hc = slice(h * 512, (h + 1) * 512)
                        y = V2[:, t, hc] if stage == "moe" else bank[2 + 2 * t + h][:, :]
                        ins = stt(X[:, t, hc], X[:, t, hc], ALPHA, y, ALU.mult, ALU.add)
                step(ins)
                stats = TINY[:, 120:144].rearrange("p (t h n) -> p t h n", t=NT, h=2)
                for t in range(NT):
                    for h in range(2):
                        ins = v.bn_stats(stats[:, t, h, :], X[:, t, h * 512:(h + 1) * 512])
                step(ins)
                mv = TINY[:, 144:148].rearrange("p (t n) -> p t n", t=NT)
                for t in range(NT):
                    ins = v.bn_aggr(mv[:, t, :], stats[:, t, :, :])
                step(ins)
                signal(v.tensor_copy(TINY[:, 64:66].rearrange("p (t n) -> p t n", t=NT), mv[:, :, 1:2]), "ms_ready")
                dve.wait_ge(sem("root_ready"), made["ms_ready"])
                step(v.reciprocal(TINY[:, 68:70], TINY[:, 66:68]))
                dve.wait_ge(sem("rows_loaded"), 32 * (k + 1))
                for t in range(NT):
                    ins = stt(X[:, t, :], X[:, t, :], mv[:, t, 0:1], ROWS[:, 0:D], ALU.subtract, ALU.mult)
                step(ins)
                for t in range(NT):
                    ins = stt(X[:, t, :], X[:, t, :], TINY[:, 68 + t:69 + t], ROWS[:, D:2 * D], ALU.mult, ALU.add)
                signal(ins, "ln_done")

            def residual(stage):
                dve.wait_ge(sem("gemm_done"), used_value(SLOT0[stage] + SLOTS_OF[stage] - 1))
                for t in range(NT):
                    for h in range(2):
                        hc = slice(h * 512, (h + 1) * 512)
                        ins = v.tensor_tensor(X[:, t, hc], bank[2 + 2 * t + h][:, :], X[:, t, hc], ALU.add)
                return ins

            def rms_norm(name, src):
                dve.wait_ge(sem("xt_psum"), 4 * NORM_NO[name])
                for t in range(NT):
                    ins = stt(XN[:, t, :], src[:, t, :], 1.0, src[:, t, :], ALU.mult, ALU.mult,
                              accum_out=TINY[:, 64 + t:65 + t])
                signal(ins, "ms_ready")
                dve.wait_ge(sem("root_ready"), made["ms_ready"])
                step(v.reciprocal(TINY[:, 68:70], TINY[:, 66:68]))
                for t in range(NT):
                    ins = v.tensor_scalar(XN[:, t, :], src[:, t, :], TINY[:, 68 + t:69 + t], None, ALU.mult)
                signal(ins, "xn_ready")

            def hidden(n, bk, dst):
                dve.wait_ge(sem("silu_ready"), n + 1)
                v.tensor_tensor(dst, SIL[:, bk, :].unsqueeze(1), half(bk)[:, 1:2, :], ALU.mult).then_inc(sem("hidden_ready"), 1)

            def ffn(stage):
                h0 = H0[stage]
                with dve.Fori(0, 3) as r:
                    for n in range(6):
                        hidden(h0 + 6 * r + n, n % 2, F[:, bass.ds(6 * r + n, 1), :])
                for n in range(18, FT):
                    hidden(h0 + n, n % 2, F[:, n:n + 1, :])

            def moe():
                h0 = H0["moe"]
                lg, eq, cum, lg2 = (TINY[:, c:c + 16].rearrange("p (t e) -> p t e", t=NT) for c in (128, 176, 192, 240))
                comb, one1, one2 = (TINY[:, c:c + 16].rearrange("p (t e) -> p t e", t=NT) for c in (160, 208, 224))
                dve.wait_ge(sem("router_psum"), 1)
                rb = SROW[:, 24:32].unsqueeze(1).to_broadcast([P, NT, NEXP])
                step(v.tensor_tensor(lg, bank[6][:, 0:16].rearrange("p (t e) -> p t e", t=NT), rb, ALU.add))

                def best(src, m, one):
                    mt = TINY[:, m:m + 2].rearrange("p (t n) -> p t n", t=NT)
                    step(v.tensor_reduce(TINY[:, m:m + 2], src, axis=AX, op=ALU.max))
                    step(v.tensor_tensor(eq, src, mt.to_broadcast([P, NT, NEXP]), ALU.is_equal))
                    for t in range(NT):
                        ins = v.tensor_tensor_scan(cum[:, t, :], ones[:, 0:NEXP], eq[:, t, :], 0.0, ALU.mult, ALU.add)
                    step(ins)
                    step(stt(one, cum, 1.0, eq, ALU.is_equal, ALU.mult))

                best(lg, 148, one1)
                step(stt(lg2, one1, TAKEN, lg, ALU.mult, ALU.add))
                best(lg2, 150, one2)
                signal(v.tensor_tensor(TINY[:, 68:70], TINY[:, 150:152], TINY[:, 148:150], ALU.subtract), "router_top")
                dve.wait_ge(sem("router_exp"), 1)
                step(v.tensor_scalar(TINY[:, 152:154], TINY[:, 70:72], 1.0, None, ALU.add))
                step(v.reciprocal(TINY[:, 154:156], TINY[:, 152:154]))
                step(v.tensor_tensor(TINY[:, 156:158], TINY[:, 70:72], TINY[:, 154:156], ALU.mult))
                for t in range(NT):
                    ins = v.tensor_scalar(comb[:, t, :], one1[:, t, :], TINY[:, 154 + t:155 + t], None, ALU.mult)
                step(ins)
                for t in range(NT):
                    ins = stt(comb[:, t, :], one2[:, t, :], TINY[:, 156 + t:157 + t], comb[:, t, :], ALU.mult, ALU.add)
                step(ins)
                v.memset(V2, 0.0).then_inc(sem("expert_taken"), 1)
                dve.wait_ge(sem("expert_taken"), 1)
                with dve.Fori(0, NEXP) as e:
                    for n in range(ET):
                        hidden(h0 + ET * e + n, n % 2, F[:, n:n + 1, :])
                    dve.wait_ge(sem("gemm_done"), JOB0["moe"] + EXP_JOBS * e + EXP_JOBS)
                    for t in range(NT):
                        for h in range(2):
                            hc = slice(h * 512, (h + 1) * 512)
                            stt(V2[:, t, hc], bank[2 + 2 * t + h][:, :], comb[:, t, bass.ds(e, 1)], V2[:, t, hc],
                                ALU.mult, ALU.add).then_inc(sem("expert_taken"), 1)
                    dve.wait_ge(sem("expert_taken"), 4 * e + 5)

            def head_norm(count, a0, need, tiles, gains, per_head):
                def square(i):
                    if need is not None:
                        dve.wait_ge(sem("proj_taken"), a0 + i + 1)
                    q = NQ[:, (i % 2) * 512:(i % 2 + 1) * 512].rearrange("p (e n) -> p e n", e=2)
                    signal(v.tensor_tensor(q, tiles(i), tiles(i), ALU.mult), "hn_square")

                square(0)
                for i in range(count):
                    if i + 1 < count:
                        square(i + 1)
                    dve.wait_ge(sem("hn_root"), made["hn_done"] + 1 if "hn_done" in made else 1)
                    w = 512 if per_head else S
                    r = NQ[:, (i % 2) * 512:(i % 2) * 512 + w]
                    step(v.reciprocal(r, r))
                    for e in range(2):
                        ins = stt(tiles(i)[:, e, :], tiles(i)[:, e, :], gains(i, e), r[:, e * S:(e + 1) * S] if per_head else r,
                                  ALU.mult, ALU.mult)
                    signal(ins, "hn_done")

            def ev():
                rms_norm("ev", X)
                dve.wait_ge(sem("gm_loaded"), 96)
                step(v.tensor_copy(SIN, POSI))
                step(v.tensor_scalar(COS, SIN, col("inv_freq"), None, ALU.mult))
                magic = 12582912.0
                step(v.tensor_scalar(SIN, COS, float(1.0 / (2.0 * np.pi)), magic, ALU.mult, ALU.add))
                step(v.tensor_scalar(SIN, SIN, -magic, None, ALU.add))
                c1 = 6.28125
                c2 = float(np.float32(np.round((2 * np.pi - c1) * 2 ** 21) / 2 ** 21))
                for c in (c1, c2, float(2 * np.pi - c1 - c2)):
                    step(stt(COS, SIN, -c, COS, ALU.mult, ALU.add))
                signal(v.tensor_scalar(COS, COS, 3.1415925, -3.1415925, ALU.min, ALU.max), "angle_ready")
                head_norm(4, ACT0["ev"], True, lambda i: F[:, 2 * i:2 * i + 2, :],
                          lambda i, e: col("q_gain" if i < 2 else "k_gain"), True)
                dve.wait_ge(sem("rope_table"), 1)
                both = lambda x: x.unsqueeze(1).to_broadcast([P, 2, S])
                for i in range(4):
                    q = NQ[:, (i % 2) * 512:(i % 2 + 1) * 512].rearrange("p (e n) -> p e n", e=2)
                    f = F[:, 2 * i:2 * i + 2, :]
                    dve.wait_ge(sem("rot_psum"), i + 1)
                    v.tensor_tensor(q, half(4 + i % 2), both(SIN), ALU.mult)
                    step(v.tensor_tensor(f, f, both(COS), ALU.mult))
                    signal(v.tensor_tensor(f, f, q, ALU.add), "rope_done")
                dve.wait_ge(sem("wst_psum"), 1)
                for b in range(2):
                    ins = v.tensor_tensor(WST[:, 4 * b:4 * b + 4, :], bank[6 + b][:, :].rearrange("p (i n) -> p i n", i=4),
                                          tril.unsqueeze(1).to_broadcast([P, 4, P]), ALU.mult)
                step(ins)
                dve.wait_ge(sem("proj_taken"), ACT0["ev"] + 10)
                stat = lambda c: TINY[:, c:c + 16].rearrange("p (t g o) -> p t g o", t=NT, g=8)
                for t in range(NT):
                    vg = V2[:, t, 512:1024].rearrange("p (g d) -> p g d", g=8)
                    sq = NQ[:, t * 512:(t + 1) * 512].rearrange("p (g d) -> p g d", g=8)
                    m = stat(80)[:, t, :, :].to_broadcast([P, 8, HD])
                    step(v.tensor_reduce(TINY[:, 80 + 8 * t:88 + 8 * t], vg, axis=AX, op=ALU.add))
                    step(stt(vg, m, -1.0 / HD, vg, ALU.mult, ALU.add))
                    step(v.tensor_tensor(sq, vg, vg, ALU.mult))
                    ins = v.tensor_reduce(TINY[:, 80 + 8 * t:88 + 8 * t], sq, axis=AX, op=ALU.add)
                    if t == 0:
                        step(ins)
                signal(ins, "gvar_ready")
                dve.wait_ge(sem("groot_ready"), 1)
                step(v.reciprocal(TINY[:, 80:96], TINY[:, 96:112]))
                for t in range(NT):
                    vg = V2[:, t, 512:1024].rearrange("p (g d) -> p g d", g=8)
                    step(v.tensor_tensor(vg, vg, stat(80)[:, t, :, :].to_broadcast([P, 8, HD]), ALU.mult))
                    step(v.tensor_tensor(V2[:, t, 512:1024], V2[:, t, 512:1024], GLN[:, 0, :], ALU.mult))
                    ins = v.tensor_tensor(V2[:, t, 512:1024], V2[:, t, 512:1024], GLN[:, 1, :], ALU.add)
                    if t == 0:
                        step(ins)
                signal(ins, "vn_ready")
                dve.wait_ge(sem("mixed_psum"), 1)
                for g in range(8):
                    hb = HD * (g % 2)
                    ins = v.tensor_tensor(OT[hb:hb + HD, 4 + g // 2, :].rearrange("p (t n) -> p t n", t=NT),
                                          half(6 + g // 4)[hb:hb + HD, (g // 2) % 2, :].rearrange("p (t n) -> p t n", t=NT),
                                          BS[hb:hb + HD, g, :].unsqueeze(1).to_broadcast([HD, NT, P]), ALU.add)
                step(ins)
                signal(v.tensor_tensor(OT[:, 4:8, :], OT[:, 4:8, :], F[:, 8:12, :], ALU.mult), "gmlp_done")
                attention("ev")

            def xa(L, before):
                step(residual(before))
                rms_norm(f"xq{L}", X)
                dve.wait_ge(sem("mem_loaded"), 16)
                rms_norm(f"xkv{L}", MEM)
                head_norm(8, ACT0[f"xa{L}"], True, lambda i: F[:, 2 * i:2 * i + 2, :],
                          lambda i, e: col(f"xq_gain{L}" if i < 4 else f"xk_gain{L}", e), False)
                attention(f"xa{L}")

            def gla():
                step(residual("ffn1"))
                rms_norm("gla", X)
                v.memset(flat(20, 24), 0.0)
                dve.wait_ge(sem("gl_ready"), 1)
                step(stt(GE, GB, 0.0, GE, ALU.min, ALU.subtract))
                step(v.tensor_scalar(GE, GE, 1.0 / 16.0, None, ALU.mult))
                signal(v.tensor_tensor_scan(GB, keep4, GE, 0.0, ALU.mult, ALU.add), "gscan_ready")
                dve.wait_ge(sem("gexp_ready"), 1)
                chunks = lambda x: x.rearrange("p (x n) -> p x n", n=CH)
                tiles4 = lambda x: x.rearrange("p (h n) -> p h n", h=4)
                v.tensor_copy(TINY[:, 80:96].rearrange("p (x o) -> p x o", o=1), chunks(GE)[:, :, CH - 1:CH])
                signal(stt(F[:, 0:4, :], F[:, 0:4, :], 128 ** -0.5, tiles4(GE), ALU.mult, ALU.mult), "gexp_used")
                signal(v.tensor_tensor(chunks(KS), chunks(GB)[:, :, CH - 1:CH].to_broadcast([P, 16, CH]), chunks(GB),
                                       ALU.subtract), "glast_ready")
                dve.wait_ge(sem("gexp_ready"), 3)
                step(v.tensor_tensor(tiles4(KS), tiles4(KS), F[:, 4:8, :], ALU.mult))
                signal(v.tensor_tensor(F[:, 4:8, :], F[:, 4:8, :], tiles4(GE), ALU.mult), "gla_factors")
                signal(v.memset(GS, 0.0), "gs_ready")
                dve.wait_ge(sem("att_psum"), 1)
                incl = strict_incl[:, P:2 * P].bitcast(i32).unsqueeze(1).to_broadcast([P, 4, P])
                att = flat(20, 24).rearrange("p (x n) -> p x n", n=P)
                for b in range(2):
                    ins = v.copy_predicated(att[:, 4 * b:4 * b + 4, :], incl,
                                            bank[4 + b][:, :].rearrange("p (x n) -> p x n", n=P))
                signal(ins, "att_ready")
                for c in range(NCH):
                    dve.wait_ge(sem("ds_psum"), c + 1)
                    for h in range(4):
                        ins = stt(GS[:, h, :], GS[:, h, :], TINY[:, 80 + 4 * h + c:81 + 4 * h + c],
                                  half(2 + h // 2)[:, h % 2, :], ALU.mult, ALU.add)
                    signal(ins, "gs_ready")
                dve.wait_ge(sem("go_taken"), NCH)
                head_norm(4, 0, None, lambda i: OT[:, 2 * i:2 * i + 2, :], lambda i, e: col("o_gain", 2 * i + e), False)
                dve.wait_ge(sem("proj_taken"), ACT0["gla"] + 12)
                signal(v.tensor_tensor(OT[:, 0:8, :], OT[:, 0:8, :], F[:, 8:16, :], ALU.mult), "gla_done")

            signal(v.memset(TINY[:, :], 0.0), "hidden_ready")
            mix(0)
            layer_norm(0, "mix0")
            ffn("ffn0")
            layer_norm(1, "ffn0")
            mix(1)
            layer_norm(2, "mix1")
            moe()
            layer_norm(3, "moe")
            ev()
            xa(0, "ev")
            step(residual("xa0"))
            rms_norm("ffn1", X)
            ffn("ffn1")
            gla()
            xa(1, "gla")
            step(residual("xa1"))
            rms_norm("ffn2", X)
            ffn("ffn2")
            residual("ffn2").then_inc(sem("x_final"), 1)


def kernel(**inputs):
    import concourse.bacc as _bacc
    from concourse import mybir as _mybir
    from concourse.bass_utils import run_bass_kernel_spmd as _run

    def tiles(v):
        return np.asarray(v).reshape(-1, P).T

    cols = np.zeros((P, NCOLS), np.float32)

    def put(name, block):
        cols[:, _AT[name]:_AT[name] + block.shape[1]] = block

    for L in range(DEPTH):
        for name, key in (("mu", "rwkv_mu"), ("w0", "rwkv_w0"), ("a0", "rwkv_a0"), ("k_k", "rwkv_k_k"), ("k_a", "rwkv_k_a"),
                          ("r_k", "rwkv_r_k"), ("gn_g", "rwkv_gn_g"), ("gn_b", "rwkv_gn_b"), ("gate", "gate_bias"),
                          ("norm_mix", "norm_mix_2"), ("norm_q", "norm_mem_q_2"), ("norm_kv", "norm_mem_kv_2"),
                          ("norm_ffn", "norm_ffn_2"), ("xq_gain", "xa_q_gain_2"), ("xk_gain", "xa_k_gain_2")):
            put(f"{name}{L}", tiles(inputs[key][L]))
    for name, key in (("q_gain", "ev_q_gain_2"), ("k_gain", "ev_k_gain_2")):
        put(name, tiles(np.concatenate([np.asarray(inputs[key][0])] * 2)))
    put("b_g", tiles(inputs["od_b_g_2"][0]))
    put("o_gain", tiles(inputs["od_o_gain_2"][0]))
    inv = np.zeros((P, 1), np.float32)
    for base in (0, HD):
        for i in range(8):
            inv[base + i] = inv[base + 8 + i] = np.float32(500000.0) ** np.float32(-i * 2.0 / 16)
    put("inv_freq", inv)
    for name, value in (("eps_ln", LN_EPS), ("eps_rms", RMS_EPS), ("eps_gn", GN_EPS), ("eps_kk", 1e-12),
                        ("half_pi", np.pi / 2)):
        put(name, np.full((P, 1), value, np.float32))

    arrays = {"x": np.asarray(inputs["x"])[0], "mem_2": np.asarray(inputs["mem_2"])[0], "cols": cols,
              "consts": shape_constants(),
              "srow": np.concatenate([np.asarray(inputs["swa_sinks"]).reshape(-1), np.asarray(inputs["fox_f_bias"]).reshape(-1),
                                      np.asarray(inputs["router_b"]).reshape(-1)])}
    for name in ("w_in", "rwkv_w_up", "rwkv_a_up", "rwkv_g_up", "w_branch", "w_out", "ln_g", "ln_b", "ffn_w1", "ffn_w3",
                 "ffn_w2", "router_w", "exp_w1", "exp_w3", "exp_w2", "positions_2", "ev_w_in_2", "ev_w_s_2", "ev_b_s_2",
                 "ev_ln_g_2", "ev_ln_b_2", "ev_w_out_2", "od_w_in_2", "od_w_g1_2", "od_w_g2_2", "od_w_out_2", "xa_w_q_2",
                 "xa_w_kv_2", "xa_w_out_2", "ffn_w_gu_2", "ffn_w_down_2"):
        arrays[name] = np.asarray(inputs[name])

    nc = _bacc.Bacc("TRN2", target_bir_lowering=False, num_devices=1)
    arrays = {f"in_{n}": np.ascontiguousarray(v) for n, v in arrays.items()}
    aps = {n[3:]: nc.dram_tensor(n, v.shape, _mybir.dt.from_np(v.dtype), kind="ExternalInput").ap()
           for n, v in arrays.items()}
    out = nc.dram_tensor("out_x", (S, D), _mybir.dt.float32, kind="ExternalOutput").ap()
    program(nc, aps, out)
    r = _run(nc, [arrays], core_ids=[0])
    return r.results[0]["out_x"].reshape(1, S, D)
```

```python
import numpy as np
import concourse.bass as bass
from concourse import mybir
from contextlib import ExitStack

P = 128
S = 256
NT = S // P
D = 1024
KT = D // P
HD = 64
DEPTH = 2
CH = 64
NCH = S // CH
DFF = 2816
FT = DFF // P
NEXP = 8
DFE = 1408
ET = DFE // P
ALPHA = float((2 * DEPTH) ** 0.25)
LN_EPS = 1e-5
RMS_EPS = 1e-6
GN_EPS = 64e-5
TOPK = min(256, S // 4)
NEG = -1e30
TAKEN = -3e38
UW = 2048
RING = 4
HALF = 2

TM_SWA_V, TM_FOX_V, TM_FOX_F, TM_DSA_V, TM_DSA_W, TM_COLS = 0, 128, 384, 388, 452, 456
F_SWA_Q, F_SWA_K, F_R, F_K, F_V, F_LO, F_FOX_Q, F_FOX_K, F_DSA_Q, F_DSA_K, F_IDX_Q, F_IDX_K, F_TILES = \
    0, 4, 6, 8, 10, 12, 14, 16, 18, 20, 21, 23, 24

_AT = {}
NCOLS = 0


def _columns(name, n):
    global NCOLS
    _AT[name] = NCOLS
    NCOLS += n


for _l in range(DEPTH):
    for _name, _n in (("mu", 8), ("w0", 2), ("a0", 2), ("k_k", 2), ("k_a", 2), ("r_k", 2), ("gn_g", 2), ("gn_b", 2),
                      ("gate", 32), ("norm_mix", 8), ("norm_q", 8), ("norm_kv", 8), ("norm_ffn", 8),
                      ("xq_gain", 2), ("xk_gain", 2)):
        _columns(f"{_name}{_l}", _n)
for _name, _n in (("q_gain", 1), ("k_gain", 1), ("b_g", 4), ("o_gain", 8), ("inv_freq", 1),
                  ("eps_ln", 1), ("eps_rms", 1), ("eps_gn", 1), ("eps_kk", 1), ("half_pi", 1)):
    _columns(_name, _n)

CONST_SPEC = [("ident", P), ("bones", P), ("ones", P), ("rot", P), ("causal", S * NT), ("window", S * NT),
              ("admit", S * NT), ("prefix", S * NT), ("strict_incl", 2 * P), ("levels", 6 * P),
              ("chunk_keep", S * 2), ("sel4", 4 * S), ("tril", P)]
CONST_AT = {}
NCONST = 0
for _name, _n in CONST_SPEC:
    CONST_AT[_name] = (NCONST, _n)
    NCONST += _n


def shape_constants():
    c = np.zeros((P, NCONST), np.float32)

    def put(name, a):
        at, n = CONST_AT[name]
        c[:a.shape[0], at:at + n] = a.reshape(a.shape[0], n)

    i = np.arange(P)
    s = np.arange(S)
    put("ident", np.eye(P))
    put("bones", (i[:, None] // HD == i[None, :] // HD).astype(np.float32))
    put("ones", np.ones((P, P)))
    rot = np.zeros((P, P))
    for base in (0, HD):
        for a in range(8):
            rot[base + 8 + a, base + a] = -1.0
            rot[base + a, base + 8 + a] = 1.0
    put("rot", rot)
    q = np.arange(NT)[None, :, None] * P + i[:, None, None]
    k = s[None, None, :]
    put("causal", np.where(k <= q, 0.0, NEG))
    put("window", np.where((k // CH <= q // CH) & (k // CH >= q // CH - 2), 0.0, NEG))
    put("admit", np.where(k // CH <= q // CH, 0.0, NEG))
    put("prefix", (q <= k).astype(np.float32))
    same = (i[:, None] // CH == i[None, :] // CH)
    put("strict_incl", np.stack([same & (i[:, None] < i[None, :]), same & (i[:, None] <= i[None, :])], 1).astype(np.float32))
    put("levels", np.stack([((i[:, None] // m) % 2 == 0) & (i[None, :] // m == i[:, None] // m + 1)
                            for m in (1, 2, 4, 8, 16, 32)], 1).astype(np.float32))
    put("chunk_keep", np.broadcast_to((np.arange(2 * S) % CH != 0).astype(np.float32), (P, 2 * S)))
    sel = np.zeros((4, 4, S))
    for h in range(4):
        sel[h, h, :P] = 1.0
        sel[h, h, P:] = -1.0
    put("sel4", sel)
    put("tril", (i[:, None] <= i[None, :]).astype(np.float32))
    return c


def cols_units(n, jobs=1):
    return [("cols", 256, jobs)] * n


OUT_UNITS = [("down", 2, 1)] * 4

MIX_PROJ = [(768, 256, [("feat", 0, F_R)]), (1024, 256, [("feat", 0, F_K)]),
            (1280, 256, [("feat", 0, F_V)]), (1536, 256, [("feat", 0, F_LO)]),
            (2564, 256, [("feat", 0, F_DSA_Q)]),
            (2820, 128, [("dup64", 0, F_DSA_K), ("tok", (64, 64), TM_DSA_V)]),
            (2948, 256, [("feat", 0, F_IDX_Q)]),
            (3204, 128, [("dup64", 0, F_IDX_K), ("tok", (64, 4), TM_DSA_W)]),
            (1792, 256, [("feat", 0, F_FOX_Q)]), (2048, 256, [("feat", 0, F_FOX_K)]),
            (2304, 256, [("tok", (0, 256), TM_FOX_V)]), (2560, 4, [("tok", (0, 4), TM_FOX_F)]),
            (0, 256, [("feat", 0, F_SWA_Q)]), (256, 256, [("feat", 0, F_SWA_Q + 2)]),
            (512, 256, [("dup128", 0, F_SWA_K), ("tok", (128, 128), TM_SWA_V)])]
GATE_COL0 = 3272
N_GATES = 16
BRANCHES = [(0, 4, [(0, 0, 4, 0)]), (4, 4, [(1, 0, 2, 4), (2, 2, 2, 6)]), (8, 2, [(3, 0, 2, 8)])]
MIX_UNITS = [("cols", w, len(jobs)) for _, w, jobs in MIX_PROJ] + cols_units(N_GATES) \
    + [("branch", kn, 2 * len(parts)) for _, kn, parts in BRANCHES for _ in range(2)] + OUT_UNITS
FFN_UNITS = [("up", 256, 1)] * FT + [("down", 2, 1)] * (FT // 2)
EXP_DOWN = [2, 2, 2, 2, 1, 1, 1]
EXP_UNITS = [("up", 256, 1)] * ET + [("down", kn, 1) for kn in EXP_DOWN] + [None] * 2
assert sum(EXP_DOWN) == ET and len(EXP_UNITS) % RING == 0
STAGES = [("mix0", MIX_UNITS), ("ffn0", FFN_UNITS), ("mix1", MIX_UNITS), ("moe", EXP_UNITS * NEXP),
          ("ev", cols_units(10) + OUT_UNITS), ("xa0", cols_units(12) + OUT_UNITS), ("ffn1", FFN_UNITS),
          ("gla", cols_units(12) + OUT_UNITS), ("xa1", cols_units(12) + OUT_UNITS), ("ffn2", FFN_UNITS)]
PLACES = []
U0 = {}
for _name, _units in STAGES:
    U0[_name] = len(PLACES)
    PLACES += _units
STAGE_END = {name: U0[name] + len(units) for name, units in STAGES}


def used_value(u):
    return sum(x[2] for x in PLACES[:u + 1] if x)


def loaded_value(u):
    return 32 * sum(1 for g in range(u % RING, u + 1, RING) if PLACES[g])


def split_value(u):
    return sum(1 for x in PLACES[:u + 1] if x)


def following(u):
    return next((g for g in range(u + 1, len(PLACES)) if PLACES[g]), None)


def before(u, ring):
    return next((g for g in range(u - ring, -1, -ring) if PLACES[g]), None)


JOB0 = {name: used_value(U0[name] - 1) if U0[name] else 0 for name, _ in STAGES}
EXP_JOBS = sum(x[2] for x in EXP_UNITS if x)
EXP_REAL = sum(1 for x in EXP_UNITS if x)


def attention_units():
    out = {}
    n = 0
    for stage, kinds in (("mix0", (("swa", 8), ("fox", 4), ("dsa", 4))), ("mix1", (("swa", 8), ("fox", 4), ("dsa", 4))),
                         ("ev", (("moba", 8),)), ("xa0", (("cross", 4),)), ("xa1", (("cross", 4),))):
        units = [(kind, h, t) for kind, heads in kinds for h in range(heads) for t in range(NT)]
        out[stage] = (n, units)
        n += len(units)
    return out


UNITS = attention_units()

N_PROJ = sum(len(jobs) for _, _, jobs in MIX_PROJ)
TAKEN_BY_ACT = {"mix0": N_PROJ + N_GATES, "ffn0": 0, "mix1": N_PROJ + N_GATES, "moe": 0, "ev": 10, "xa0": 12, "ffn1": 0,
                "gla": 12, "xa1": 12, "ffn2": 0}
ACT0 = {}
_n = 0
for _name, _ in STAGES:
    ACT0[_name] = _n
    _n += TAKEN_BY_ACT[_name]
OPEN = 2
OT0 = {"mix0": 0, "mix1": 2, "ev": 4, "xa0": 8, "gla": 12, "xa1": 16}
H0 = {"ffn0": 0, "moe": FT, "ffn1": FT + NEXP * ET, "ffn2": 2 * FT + NEXP * ET}
NORMS = ["mix0", "ffn0", "mix1", "moe", "ev", "xq0", "xkv0", "ffn1", "gla", "xq1", "xkv1", "ffn2"]
NORM_NO = {name: n for n, name in enumerate(NORMS)}



def program(nc, a, out):
    fp32, i32 = mybir.dt.float32, mybir.dt.int32
    ALU, ACT = mybir.AluOpType, mybir.ActivationFunctionType
    AX = mybir.AxisListType.X

    ctx = ExitStack()
    with ctx:
        def sb(name, shape, dt=fp32):
            return ctx.enter_context(nc.sbuf_tensor(name, shape, dt))

        sems = {}

        def sem(name):
            if name not in sems:
                sems[name] = ctx.enter_context(nc.semaphore(name))
            return sems[name]

        f32r = mybir.dt.float32r
        place = [-(-nc.sbuf_base // 32) * 32]
        at = {}

        def sb(name, shape, dt=fp32, over=None, skip=0):
            n = int(np.prod(shape[1:]))
            if over is None:
                at[name] = place[0]
                place[0] += 4 * n
            else:
                at[name] = at[over] + 4 * skip
            return nc.alloc_sbuf_tensor_at(name, shape, dt, offset=at[name])

        RAW = sb("RAW", [P, RING, UW])
        WL = sb("WL", [P, RING, UW], f32r, "RAW")
        WH = sb("WH", [P, HALF, UW], f32r)
        X = sb("X", [P, NT, D])
        XTH = sb("XTH", [P, KT, S], f32r)
        XTL = sb("XTL", [P, KT, S], f32r)
        CST = sb("CST", [P, NCONST])
        F = sb("F", [P, F_TILES, S])
        G = sb("G", [P, 32, S])
        HIDH = sb("HIDH", [P, FT, S], f32r, "F")
        HIDL = sb("HIDL", [P, FT, S], f32r, "G", 8 * S)
        OT = sb("OT", [P, 10, S])
        OTH = sb("OTH", [P, 10, S], f32r, "F")
        OTL = sb("OTL", [P, 10, S], f32r, "F", 10 * S)
        WK = sb("WK", [P, 7552])
        MTH = sb("MTH", [P, KT, S], f32r, "WK")
        MTL = sb("MTL", [P, KT, S], f32r, "WK", 2048)
        SMX = sb("SMX", [P, 4, S])
        PT = sb("PT", [P, 2, S])
        SEL = sb("SEL", [P, NT, S])
        LORA = sb("LORA", [P, 512])
        RW = sb("RW", [P, KT, NEXP])
        G1 = sb("G1", [P, KT, 16])
        TINY = sb("TINY", [P, 256])
        SROW = sb("SROW", [P, 32])
        TM = sb("TM", [P, NT, TM_COLS])
        COL = sb("COL", [P, NCOLS + (-NCOLS) % 8])
        assert place[0] <= nc.sbuf_usable_end

        def const(name):
            at, n = CONST_AT[name]
            return CST[:, at:at + n]

        def col(name, n=0):
            return COL[:, _AT[name] + n:_AT[name] + n + 1]

        ident = const("ident")
        bones = const("bones")
        ones = const("ones")
        rot = const("rot")
        causal = const("causal").rearrange("p (t k) -> p t k", t=NT)
        window = const("window").rearrange("p (t k) -> p t k", t=NT)
        admit = const("admit").rearrange("p (t k) -> p t k", t=NT)
        prefix = const("prefix").rearrange("p (t k) -> p t k", t=NT)
        strict_incl = const("strict_incl")
        levels = const("levels").rearrange("p (l k) -> p l k", l=6)
        keep = const("chunk_keep")
        sel4 = const("sel4").rearrange("p (h k) -> p h k", h=4)
        tril = const("tril")

        def wk(at, n):
            return WK[:, at:at + n]

        ROWS = wk(0, 2048)
        AR = wk(0, 1024).rearrange("p (f t a n) -> p f t a n", f=2, t=NT, a=2)
        ARF = wk(0, 1024).rearrange("p (f t x) -> p f t x", f=2, t=NT)
        BKT = wk(1024, 1024).rearrange("p (w f n) -> p w f n", w=2, f=2)
        TOK = wk(2048, 1536).rearrange("p (w t n) -> p w t n", w=3, t=NT)
        XI = wk(3584, 1024).rearrange("p (i n) -> p i n", i=8)
        XIT = wk(4608, 1024).rearrange("p (i n) -> p i n", i=8)
        LM = wk(5632, 1024).rearrange("p (i n) -> p i n", i=8)
        T1 = wk(1024, 1024).rearrange("p (i n) -> p i n", i=8)
        ST = wk(6656, 128).rearrange("p (f n) -> p f n", f=2)
        GG = wk(6784, 512).rearrange("p (f n) -> p f n", f=2)
        YT = wk(1024, 512).rearrange("p (f n) -> p f n", f=2)
        R1 = wk(1536, 256)
        SA = wk(1792, 256)
        MB = G[:, 16:24, :].rearrange("p i (w n) -> p i w n", w=2)
        MK = G[:, 24:32, :].rearrange("p i (w n) -> p i w n", w=2)
        DT = G[:, 16:24, :]
        smx = SMX[:, :, :].rearrange("p a b -> p (a b)")
        E = [wk(3584 + 512 * n, 512) for n in range(4)] + [smx[:, 0:512], smx[:, 512:1024]] \
            + [wk(5632 + 512 * n, 512) for n in range(2)]
        REL = OT[:, 0:4, :]
        SCORE = OT[:, 8:10, :]
        C8 = wk(7296, 256)

        XN = wk(4096, 2048).rearrange("p (t n) -> p t n", t=NT)
        MEM = G[:, 24:32, :].rearrange("p (t x) n -> p t (x n)", t=NT)
        BS = wk(0, 1024).rearrange("p (g i) -> p g i", g=8)
        GLN = wk(1024, 1024).rearrange("p (w n) -> p w n", w=2)
        WS = wk(2048, 1024).rearrange("p (g j) -> p g j", g=8)
        WST = F[:, 12:16, :].rearrange("p a b -> p (a b)").rearrange("p (g i) -> p g i", g=8)
        POSI = wk(3072, 256).bitcast(i32)
        COS, SIN = wk(3328, 256), wk(3584, 256)
        GL1 = wk(3840, 256)[0:16, :]
        NQ = wk(6144, 1024)
        SIL = wk(3072, 512).rearrange("p (b n) -> p b n", b=2)
        HT = wk(3584, 512).rearrange("p (b n) -> p b n", b=2)
        MRG = wk(2048, 2048).rearrange("p (k n) -> p k n", k=KT)
        flat = lambda lo, hi: G[:, lo:hi, :].rearrange("p a b -> p (a b)")
        GB, GE, KS = flat(8, 12), flat(12, 16), flat(16, 20)
        ATT = flat(20, 24).rearrange("p (h t n) -> p h t n", h=4, t=NT)
        KSM = flat(24, 28).rearrange("p (t n) -> p t n", t=NT)
        GS = flat(28, 32).rearrange("p (h n) -> p h n", h=4)

        bank = [ctx.enter_context(nc.psum_tensor(f"bank{n}", [P, 512], fp32)) for n in range(8)]

        def half(b):
            return bank[b][:, :].rearrange("p (h n) -> p h n", h=2)

        def part(t, u, ring):
            kind, n, _ = PLACES[u]
            flat = t[:, u % ring, :]
            if kind in ("cols", "up"):
                return flat.rearrange("p (k n) -> p k n", k=KT)[:, :, 0:n]
            return flat.rearrange("p (k n) -> p k n", n=D if kind == "down" else 512)[:, 0:n, :]

        def raw(u):
            return part(RAW, u, RING)

        def wlo(u):
            return part(WL, u, RING)

        def whi(u):
            return part(WH, u, HALF)

        V2 = G[:, 0:8, :].rearrange("p (t x) n -> p t (x n)", t=NT)

        def unit_at(kind, h, t):
            hb = HD * (h % 2)
            nk = NT if kind == "cross" or t > 0 else 1
            keys = slice(0, nk * P)
            tq = slice(t * P, (t + 1) * P)
            if kind == "cross":
                qk = [(F[:, 2 * h + e, tq], F[:, 8 + 2 * h + e, keys]) for e in range(2)]
                return nk, qk, [[V2[:, kt, h * S + e * P:h * S + (e + 1) * P] for e in range(2)] for kt in range(nk)], \
                    (slice(0, P), slice(2 * h, 2 * h + 2))
            fq, fk, v0, o0 = {"swa": (F_SWA_Q + h // 2, F_SWA_K + h // 4, TM_SWA_V + HD * (h // 4), h // 2),
                              "fox": (F_FOX_Q + h // 2, F_FOX_K + h // 2, TM_FOX_V + HD * h, 6 + h // 2),
                              "dsa": (F_DSA_Q + h // 2, F_DSA_K, TM_DSA_V, 8 + h // 2),
                              "moba": (h // 2, 4 + h // 2, HD * h, h // 2)}[kind]
            vv = V2 if kind == "moba" else TM
            return nk, [(F[hb:hb + HD, fq, tq], F[hb:hb + HD, fk, keys])], \
                [[vv[:, kt, v0:v0 + HD]] for kt in range(nk)], (slice(hb, hb + HD), slice(o0, o0 + 1))

        SCORE_SCALE = {"swa": HD ** -0.5, "fox": HD ** -0.5, "dsa": HD ** -0.5, "moba": HD ** -0.5, "cross": 256 ** -0.5}

        block = ctx.enter_context(nc.Block())

        @block.sync
        def _(sp):
            sp.dma_start(X[:, :, :], a["x"].rearrange("(t p) n -> p t n", p=P)).then_inc(sem("x_in"), 16)
            sp.dma_start(CST[:, :], a["consts"]).then_inc(sem("params_in"), 16)
            sp.dma_start(COL[:, :], a["cols"]).then_inc(sem("params_in"), 16)
            sp.dma_start(SROW[:, :], a["srow"].partition_broadcast(P)).then_inc(sem("params_in"), 16)
            sp.dma_start(RW[:, :, :], a["router_w"][0].rearrange("(k p) n -> p k n", p=P))\
                .then_inc(sem("params_in"), 16)
            sp.dma_start(G1[:, :, :], a["od_w_g1_2"][0].rearrange("(k p) n -> p k n", p=P))\
                .then_inc(sem("params_in"), 16)

            def free(u):
                if before(u, RING) is not None:
                    sp.wait_ge(sem("gemm_done"), used_value(before(u, RING)))

            def put(u, dst, src):
                sp.dma_start(dst, src).then_inc(sem(f"slot_loaded{u % RING}"), 16)

            def tiled(w):
                return w.rearrange("(k p) n -> p k n", p=P)

            def cols(u, w, c0):
                n = PLACES[u][1]
                for k in (0, KT // 2):
                    put(u, raw(u)[:, k:k + KT // 2, :], tiled(w)[:, k:k + KT // 2, c0:c0 + n])

            def up(u, w1, w3, c1, c3):
                put(u, raw(u)[:, :, 0:P], w1[:, :, c1])
                put(u, raw(u)[:, :, P:2 * P], w3[:, :, c3])

            def rows(u, w, r0, c0=0):
                kind, kn, _ = PLACES[u]
                n = D if kind == "down" else 512
                if kn == 1:
                    for c in (0, n // 2):
                        put(u, raw(u)[:, 0, c:c + n // 2], w[:, r0, c0 + c:c0 + c + n // 2])
                else:
                    for k in (0, kn // 2):
                        put(u, raw(u)[:, k:k + kn // 2, :], w[:, r0 + k:r0 + k + kn // 2, c0:c0 + n])

            def mix(L):
                u = U0[f"mix{L}"]
                for c0 in [c for c, _, _ in MIX_PROJ] + [GATE_COL0 + 256 * j for j in range(N_GATES)]:
                    free(u)
                    cols(u, a["w_in"][L], c0)
                    u += 1
                for r0, _, _ in BRANCHES:
                    for c0 in (0, 512):
                        free(u)
                        rows(u, tiled(a["w_branch"][L]), r0, c0)
                        u += 1
                for i in range(4):
                    free(u)
                    rows(u, tiled(a["w_out"][L]), 2 * i)
                    u += 1

            def ffn(stage, w1, c1, w3, c3, w2):
                u0 = U0[stage]
                for i in range(RING):
                    free(u0 + i)
                    up(u0 + i, tiled(w1), tiled(w3), slice(c1 + P * i, c1 + P * (i + 1)),
                       slice(c3 + P * i, c3 + P * (i + 1)))
                with sp.Fori(1, FT // RING) as r:
                    for i in range(RING):
                        sp.wait_ge(sem("gemm_done"), used_value(u0 + i) + RING * (r - 1))
                        c = P * RING * r + P * i
                        up(u0 + i, tiled(w1), tiled(w3), bass.ds(c + c1, P), bass.ds(c + c3, P))
                for i in range(FT // RING * RING, FT):
                    free(u0 + i)
                    up(u0 + i, tiled(w1), tiled(w3), slice(c1 + P * i, c1 + P * (i + 1)),
                       slice(c3 + P * i, c3 + P * (i + 1)))
                for i in range(FT // 2):
                    free(u0 + FT + i)
                    rows(u0 + FT + i, tiled(w2), 2 * i)

            def expert(e, first):
                u0 = U0["moe"]
                w1, w3, w2 = ([a[n][0, bass.ds(e, 1), :, :].rearrange("e (k p) n -> p (e k) n", p=P) for n in
                               ("exp_w1", "exp_w3", "exp_w2")])
                k0 = 0
                for i, place in enumerate(EXP_UNITS):
                    if place is None:
                        continue
                    if first:
                        free(u0 + i)
                    else:
                        sp.wait_ge(sem("gemm_done"), used_value(before(u0 + len(EXP_UNITS) + i, RING))
                                   + EXP_JOBS * (e - 1))
                    if place[0] == "up":
                        up(u0 + i, w1, w3, slice(P * i, P * (i + 1)), slice(P * i, P * (i + 1)))
                    else:
                        rows(u0 + i, w2, k0)
                        k0 += place[1]

            def simple(stage, parts, w_out):
                u = U0[stage]
                for w, n in parts:
                    for i in range(n):
                        free(u)
                        cols(u, w, 256 * i)
                        u += 1
                for i in range(4):
                    free(u)
                    rows(u, tiled(w_out), 2 * i)
                    u += 1

            mix(0)
            ffn("ffn0", a["ffn_w1"][0], 0, a["ffn_w3"][0], 0, a["ffn_w2"][0])
            mix(1)
            expert(0, True)
            with sp.Fori(1, NEXP) as e:
                expert(e, False)
            simple("ev", [(a["ev_w_in_2"][0], 10)], a["ev_w_out_2"][0])
            for L in range(DEPTH):
                if L == 1:
                    simple("gla", [(a["od_w_in_2"][0], 12)], a["od_w_out_2"][0])
                simple(f"xa{L}", [(a["xa_w_q_2"][L], 4), (a["xa_w_kv_2"][L], 8)], a["xa_w_out_2"][L])
                ffn(f"ffn{L + 1}", a["ffn_w_gu_2"][L], 0, a["ffn_w_gu_2"][L], DFF, a["ffn_w_down_2"][L])
            sp.wait_ge(sem("x_final"), 1)
            sp.dma_start(out.rearrange("(t p) n -> p t n", p=P), X[:, :, :]).then_inc(sem("x_out"), 16)
            sp.wait_ge(sem("x_out"), 16)

        @block.gpsimd
        def _(pool):

            def lora(L):
                if L:
                    pool.wait_ge(sem("lora_out"), 3 * L)
                pool.dma_start(LORA[0:64, 0:256], a["rwkv_w_up"][L]).then_inc(sem("lora_loaded"), 16)
                pool.dma_start(LORA[64:128, 0:256], a["rwkv_a_up"][L]).then_inc(sem("lora_loaded"), 16)
                pool.dma_start(LORA[:, 256:512], a["rwkv_g_up"][L]).then_inc(sem("lora_loaded"), 16)

            def rows(name, L, k):
                pool.dma_start(ROWS[:, 0:D], a["ln_g"][L, k:k + 1, :].rearrange("a n -> (a n)").partition_broadcast(P))\
                    .then_inc(sem("rows_loaded"), 16)
                pool.dma_start(ROWS[:, D:2 * D],
                               a["ln_b"][L, k:k + 1, :].rearrange("a n -> (a n)").partition_broadcast(P))\
                    .then_inc(sem("rows_loaded"), 16)

            for L in range(DEPTH):
                lora(L)
                pool.wait_ge(sem("shift_done"), L + 1)
                nc.gpsimd.memset(G[:, 16:32, :], 0.0).then_inc(sem("grams_cleared"), 1)
                pool.wait_ge(sem("rwkv_done"), L + 1)
                rows("mix", L, 0)
                pool.wait_ge(sem("ln_done"), 2 * L + 1)
                rows("ffn", L, 1)
            pool.wait_ge(sem("ln_done"), 4)
            for dst, src in ((ROWS[:, 0:1024], a["ev_b_s_2"][0]), (ROWS[:, 1024:1536], a["ev_ln_g_2"][0]),
                             (ROWS[:, 1536:2048], a["ev_ln_b_2"][0])):
                pool.dma_start(dst, src.rearrange("g n -> (g n)").partition_broadcast(P))\
                    .then_inc(sem("gm_loaded"), 16)
            pool.dma_start(wk(2048, 1024).rearrange("p (g j) -> p g j", g=8),
                           a["ev_w_s_2"][0].rearrange("g i j -> i g j")).then_inc(sem("gm_loaded"), 16)
            pool.dma_start(wk(3072, 256).bitcast(i32), a["positions_2"].rearrange("b n -> (b n)").partition_broadcast(P))\
                .then_inc(sem("gm_loaded"), 16)
            pool.dma_start(LORA[0:16, :], a["od_w_g2_2"][0]).then_inc(sem("gm_loaded"), 16)
            pool.dma_start(MEM[:, :, :], a["mem_2"].rearrange("(t p) n -> p t n", p=P)).then_inc(sem("mem_loaded"), 16)
            pool.wait_ge(sem("gla_done"), 1)
            pool.dma_start(MEM[:, :, :], a["mem_2"].rearrange("(t p) n -> p t n", p=P)).then_inc(sem("mem_loaded"), 16)

        @block.tensor
        def _(pe):
            mm = nc.tensor.matmul
            fences = [0]
            XT, MT, OTS, HID = (XTH, XTL), (MTH, MTL), (OTH, OTL), (HIDH, HIDL)

            def fence(ins):
                fences[0] += 1
                ins.then_inc(sem("row_tile_fence"), 1)
                pe.wait_ge(sem("row_tile_fence"), fences[0])

            def high_in(u, more=0):
                pe.wait_ge(sem("wh_ready"), split_value(u) + more)

            def low_in(u, more=0):
                pe.wait_ge(sem("wl_ready"), split_value(u) + more)

            def transposed(name, src):
                n = NORM_NO[name]
                for j in range(4):
                    for i in range(2):
                        for t in range(NT):
                            last = nc.tensor.transpose(half(2 + j)[:, i, t * P:(t + 1) * P],
                                                       src[:, t, (2 * j + i) * P:(2 * j + i + 1) * P], ident)
                    last.then_inc(sem("xt_psum"), 1)
                pe.wait_ge(sem("xt_ready"), 4 * n + 4)

            def bank_free(stage, i):
                if ACT0[stage] + i - 1 > 0:
                    pe.wait_ge(sem("proj_taken"), ACT0[stage] + i - 1)

            def columns(dst, u, ks, c, src, k0=0, more=0):
                wh, wl = whi(u), wlo(u)
                n = len(ks)
                for i, x in enumerate(src):
                    for j, k in enumerate(ks):
                        mm(dst, wh[:, k, c:c + P], x[:, k0 + j, :], start=(i == 0 and j == 0), stop=False)
                low_in(u, more)
                for j, k in enumerate(ks):
                    last = mm(dst, wl[:, k, c:c + P], src[0][:, k0 + j, :], start=False, stop=(j == n - 1))
                return last

            def feat(stage, u, i, tiles=2, src=XT):
                high_in(u)
                bank_free(stage, i)
                for t in range(tiles):
                    last = columns(half(i % 2)[:, t, :], u, range(KT), t * P, src)
                last.then_inc(sem("gemm_done"), 1)

            def tok(stage, u, i, c0=0, width=256, src=XT):
                high_in(u)
                bank_free(stage, i)
                wh, wl = whi(u)[:, :, c0:c0 + width], wlo(u)[:, :, c0:c0 + width]
                for t in range(NT):
                    dst = bank[i % 2][:, t * width:(t + 1) * width]
                    tt = slice(t * P, (t + 1) * P)
                    for n, x in enumerate(src):
                        for k in range(KT):
                            mm(dst, x[:, k, tt], wh[:, k, :], start=(n == 0 and k == 0), stop=False)
                    low_in(u)
                    for k in range(KT):
                        last = mm(dst, src[0][:, k, tt], wl[:, k, :], start=False, stop=(k == KT - 1))
                last.then_inc(sem("gemm_done"), 1)

            def down(u, src, k0, first, last_unit, more=0):
                kn = PLACES[u][1]
                high_in(u, more)
                for x in src:
                    for k in range(kn):
                        for t in range(NT):
                            for h in range(2):
                                mm(bank[2 + 2 * t + h][:, :], x[:, k0 + k, t * P:(t + 1) * P],
                                   whi(u)[:, k, h * 512:(h + 1) * 512],
                                   start=(first and x is src[0] and k == 0), stop=False)
                low_in(u, more)
                for k in range(kn):
                    for t in range(NT):
                        for h in range(2):
                            last = mm(bank[2 + 2 * t + h][:, :], src[0][:, k0 + k, t * P:(t + 1) * P],
                                      wlo(u)[:, k, h * 512:(h + 1) * 512], start=False,
                                      stop=(last_unit and k == kn - 1))
                last.then_inc(sem("gemm_done"), 1)

            def out_product(stage, u0):
                for i in range(4):
                    pe.wait_ge(sem("ot_low"), OT0[stage] + i + 1)
                    down(u0 + i, OTS, 2 * i, i == 0, i == 3)

            def scores(n, unit):
                kind, h, t = unit
                nk, qk, _, _ = unit_at(kind, h, t)
                if n >= 2:
                    pe.wait_ge(sem("scores_taken"), n - 1)
                dst = bank[2 + n % 2][:, 0:nk * P]
                for i, (lhsT, rhs) in enumerate(qk):
                    last = mm(dst, lhsT, rhs, start=(i == 0), stop=(i == len(qk) - 1 and kind != "fox"),
                              skip_group_check=kind == "fox")
                if kind == "fox":
                    mm(half(2 + n % 2)[:, 0, 0:P], C8[0:4, t * P:(t + 1) * P], sel4[0:4, h, 0:P],
                       start=False, stop=False, skip_group_check=True)
                    if nk == 2:
                        mm(half(2 + n % 2)[:, 0, P:2 * P], C8[0:4, t * P:(t + 1) * P], sel4[0:4, h, 0:P],
                           start=False, stop=False, skip_group_check=True)
                    last = mm(dst, sel4[0:4, h, P:2 * P], C8[0:4, 0:nk * P], start=False, stop=True,
                              skip_group_check=True)
                last.then_inc(sem("scores_ready"), 1)

            def turn(n, unit):
                kind, h, t = unit
                nk = unit_at(kind, h, t)[0]
                pe.wait_ge(sem("probs_ready"), n + 1)
                if n >= 2:
                    pe.wait_ge(sem("pt_ready"), n - 1)
                for kt in range(nk):
                    last = nc.tensor.transpose(half(4 + n % 2)[:, 0, kt * P:(kt + 1) * P],
                                               SMX[:, n % 4, kt * P:(kt + 1) * P], ident)
                last.then_inc(sem("pt_psum"), 1)

            def context(n, unit):
                kind, h, t = unit
                nk, _, vs, (parts, outs) = unit_at(kind, h, t)
                pe.wait_ge(sem("pt_ready"), n + 1)
                if n >= 2:
                    pe.wait_ge(sem("ctx_taken"), n - 1)
                for e in range(outs.stop - outs.start):
                    for kt in range(nk):
                        last = mm(bank[6 + n % 2][parts, e * P:(e + 1) * P], vs[kt][e], PT[:, n % 2, kt * P:(kt + 1) * P],
                                  start=(kt == 0), stop=(kt == nk - 1))
                last.then_inc(sem("ctx_psum"), 1)

            def attention(stage, filler=None):
                n0, units = UNITS[stage]
                for i in range(len(units) + 3):
                    if i < len(units):
                        scores(n0 + i, units[i])
                    if filler is not None:
                        filler(i)
                    if 2 <= i < len(units) + 2:
                        turn(n0 + i - 2, units[i - 2])
                    if i >= 3:
                        context(n0 + i - 3, units[i - 3])
                pe.wait_ge(sem("ctx_taken"), n0 + len(units))

            def mix(L):
                stage = f"mix{L}"
                u0 = U0[stage]
                if L == 0:
                    pe.wait_ge(sem("x_in"), 16)
                    pe.wait_ge(sem("params_in"), 80)
                else:
                    pe.wait_ge(sem("ln_done"), 2)
                transposed(stage, X)
                i = 0
                for n, (_, _, jobs) in enumerate(MIX_PROJ):
                    for kind, c, _ in jobs:
                        if kind == "tok":
                            tok(stage, u0 + n, i, c[0], c[1])
                        else:
                            feat(stage, u0 + n, i, 2 if kind == "feat" else 1)
                        i += 1

                def gate(j):
                    feat(stage, u0 + len(MIX_PROJ) + j, N_PROJ + j)

                pe.wait_ge(sem("lora_loaded"), 48 * (L + 1))
                pe.wait_ge(sem("lora_in"), L + 1)
                for m in range(2):
                    last = mm(half(2)[:, m, :], LORA[0:64, m * P:(m + 1) * P], F[0:64, F_LO, :], start=True, stop=True)
                last.then_inc(sem("lora_out"), 1)
                for m in range(2):
                    last = mm(half(3)[:, m, :], LORA[64:128, m * P:(m + 1) * P], F[64:128, F_LO, :],
                              start=True, stop=True)
                last.then_inc(sem("lora_out"), 1)
                for m in range(2):
                    last = mm(half(4)[:, m, :], LORA[:, 256 + m * P:256 + (m + 1) * P], F[:, F_LO + 1, :],
                              start=True, stop=True)
                last.then_inc(sem("lora_out"), 1)
                pe.wait_ge(sem("proj_taken"), ACT0[stage] + N_PROJ)
                for t in range(NT):
                    if t:
                        pe.wait_ge(sem("idx_relu"), 2 * L + 1)
                    for h in range(4):
                        hb = HD * (h % 2)
                        last = mm(half(6 + h % 2)[:, h // 2, :], F[hb:hb + HD, F_IDX_Q + h // 2, t * P:(t + 1) * P],
                                  F[hb:hb + HD, F_IDX_K, :], start=True, stop=True)
                    last.then_inc(sem("idx_scores"), 1)
                    gate(t)
                pe.wait_ge(sem("logf_ready"), L + 1)
                for t in range(NT):
                    last = mm(bank[5][0:4, 0:S], TM[:, t, TM_FOX_F:TM_FOX_F + 4], prefix[:, t, :],
                              start=(t == 0), stop=(t == NT - 1))
                last.then_inc(sem("foxc_psum"), 1)
                gate(2)
                pe.wait_ge(sem("kk_square"), L + 1)
                pe.wait_ge(sem("lora_taken"), 3 * (L + 1))
                mm(bank[2][:, :], bones, E[5], start=True, stop=True).then_inc(sem("kk_sum"), 1)
                gate(3)
                pe.wait_ge(sem("rkr_ready"), L + 1)
                mm(bank[3][:, :], bones, E[5], start=True, stop=True).then_inc(sem("rkr_sum"), 1)
                pe.wait_ge(sem("rwkv_factors"), L + 1)
                pe.wait_ge(sem("c8_ready"), L + 1)
                pe.wait_ge(sem("idx_relu"), 2 * L + 2)
                for w, src in enumerate((BKT[:, 0, :, :], BKT[:, 1, :, :], F[:, F_V:F_V + 2, :])):
                    for t in range(NT):
                        for f in range(2):
                            last = nc.tensor.transpose(half(4 + w)[:, t, f * P:(f + 1) * P],
                                                       src[:, f, t * P:(t + 1) * P], ident)
                    last.then_inc(sem("tok_psum"), 1)
                pe.wait_ge(sem("tok_ready"), 3 * (L + 1))
                pe.wait_ge(sem("bonus_taken"), L + 1)
                for w in range(2):
                    for i in range(8):
                        h, t = i // 2, i % 2
                        hb = HD * (h % 2)
                        if w and t == 0:
                            pe.wait_ge(sem("gram_taken"), 8 * L + i // 2 + 1)
                        last = mm(half(2 + i // 2)[:, t, :], BKT[hb:hb + HD, w, h // 2, t * P:(t + 1) * P],
                                  ARF[hb:hb + HD, h // 2, t, :], start=True, stop=True)
                        if t:
                            last.then_inc(sem("gram_psum"), 1)
                gate(4)
                pe.wait_ge(sem("gram_taken"), 8 * L + 8)
                for lv in range(6):
                    n = 6 * L + lv
                    pe.wait_ge(sem("lm_ready"), n + 1)
                    for i in range(8):
                        last = mm(bank[2 + i // 4][:, (i % 4) * P:(i % 4 + 1) * P], LM[:, i, :],
                                  ident if lv == 0 else XI[:, i, :], start=True, stop=True)
                    last.then_inc(sem("t1_psum"), 1)
                    if lv in (1, 3, 4):
                        gate(5 + (lv > 1) + (lv > 3))
                    if lv:
                        pe.wait_ge(sem("t1_ready"), 5 * L + lv)
                        if lv < 5:
                            for i in range(8):
                                last = mm(bank[4 + i // 4][:, (i % 4) * P:(i % 4 + 1) * P], XIT[:, i, :], T1[:, i, :],
                                          start=True, stop=True)
                        for i in range(8):
                            last = mm(bank[6 + i // 4][:, (i % 4) * P:(i % 4 + 1) * P], T1[:, i, :], XIT[:, i, :],
                                      start=True, stop=True)
                        last.then_inc(sem("xu_psum"), 1)
                pe.wait_ge(sem("inverse_ready"), L + 1)
                for c in range(NCH):
                    n = NCH * L + c
                    t, tb = c // 2, CH * (c % 2)
                    tc = slice(tb, tb + CH)
                    pe.wait_ge(sem("state_ready"), (NCH + 1) * L + c + 1)
                    other = 1 - c % 2
                    for h in (other, other + 2, 1 - other, 3 - other):
                        hb, f = HD * (h % 2), h // 2
                        hc = slice(h * HD, (h + 1) * HD)
                        last = mm(bank[2][tc, hc], AR[hb:hb + HD, f, t, 0, tc], ST[hb:hb + HD, f, :],
                                  start=(h == other), stop=False, skip_group_check=True)
                        if h == other + 2:
                            fence(last)
                    for h in range(4):
                        hc = slice(h * HD, (h + 1) * HD)
                        last = mm(bank[2][tc, hc], MK[tc, 2 * h + t, 0, tc], TOK[tc, 2, t, hc],
                                  start=False, stop=True, skip_group_check=True)
                    last.then_inc(sem("r1_psum"), 1)
                    pe.wait_ge(sem("r1_ready"), n + 1)
                    for h in range(4):
                        i = 2 * h + t
                        hc = slice(h * HD, (h + 1) * HD)
                        last = mm(bank[3][tc, hc], XIT[tc, i, tc], R1[tc, hc], start=True, stop=True)
                    last.then_inc(sem("sa_psum"), 1)
                    pe.wait_ge(sem("sa_ready"), n + 1)
                    if c:
                        pe.wait_ge(sem("y_taken"), n)
                    for h in range(4):
                        hb, f = HD * (h % 2), h // 2
                        i = 2 * h + t
                        hc = slice(h * HD, (h + 1) * HD)
                        dst = bank[5][hb:hb + HD, f * HD:(f + 1) * HD]
                        mm(dst, TOK[tc, 0, t, hc], SA[tc, hc], start=True, stop=False)
                        last = mm(dst, TOK[tc, 1, t, hc], TOK[tc, 2, t, hc], start=False, stop=True)
                    last.then_inc(sem("st_psum"), 1)
                    for h in (other, other + 2, 1 - other, 3 - other):
                        hb, f = HD * (h % 2), h // 2
                        last = mm(bank[4][hb:hb + HD, f * CH:(f + 1) * CH], ST[hb:hb + HD, f, :],
                                  AR[hb:hb + HD, f, t, 1, tc], start=(f == 0), stop=False, skip_group_check=True)
                        if h == other + 2:
                            fence(last)
                    for h in range(4):
                        hb, f = HD * (h % 2), h // 2
                        i = 2 * h + t
                        hc = slice(h * HD, (h + 1) * HD)
                        dst = bank[4][hb:hb + HD, f * CH:(f + 1) * CH]
                        mm(dst, SA[tc, hc], MB[tc, i, 1, tc], start=False, stop=False, skip_group_check=True)
                        last = mm(dst, TOK[tc, 2, t, hc], MK[tc, i, 1, tc], start=False, stop=True, skip_group_check=True)
                    last.then_inc(sem("y_psum"), 1)
                pe.wait_ge(sem("y_taken"), NCH * (L + 1))
                mm(bank[2][:, :], bones, YT.rearrange("p f n -> p (f n)"), start=True, stop=True)\
                    .then_inc(sem("gn_sum"), 1)
                pe.wait_ge(sem("gn_square"), L + 1)
                mm(bank[3][:, :], bones, E[0], start=True, stop=True).then_inc(sem("gn_var"), 1)
                gate(8)
                pe.wait_ge(sem("dsa_mask"), L + 1)
                pe.wait_ge(sem("rwkv_done"), L + 1)
                attention(stage, lambda i: gate(9 + i // 4) if i % 4 == 0 and i // 4 < 7 else None)
                pe.wait_ge(sem("proj_taken"), ACT0[stage] + N_PROJ + N_GATES)
                j = 16 * L
                u = u0 + len(MIX_PROJ) + N_GATES
                for n, (_, _, parts) in enumerate(BRANCHES):
                    pe.wait_ge(sem("ot_low"), 2 * L + min(n, 1) + 1)
                    for c in range(2):
                        high_in(u)
                        for _, k0, kn, o0 in parts:
                            for fp in range(2):
                                if j >= 2:
                                    pe.wait_ge(sem("merge_taken"), j - 1)
                                for e in range(2):
                                    last = columns(half(j % 2)[:, e, :], u, range(k0, k0 + kn), (2 * fp + e) * P, OTS, o0)
                                last.then_inc(sem("gemm_done"), 1)
                                j += 1
                        u += 1
                for i in range(4):
                    pe.wait_ge(sem("mrg_low"), 4 * L + i + 1)
                    down(u + i, XT, 2 * i, i == 0, i == 3)

            def up(u, bk, more=0):
                high_in(u, more)
                for e in range(2):
                    last = columns(half(bk)[:, e, :], u, range(KT), e * P, XT, 0, more)
                last.then_inc(sem("gemm_done"), 1)

            def ffn(stage):
                u0, h0 = U0[stage], H0[stage]
                with pe.Fori(0, FT // RING) as r:
                    for i in range(RING):
                        pe.wait_ge(sem("hidden_ready"), OPEN + h0 - 1 + i + RING * r)
                        up(u0 + i, i % 2, RING * r)
                for i in range(FT // RING * RING, FT):
                    pe.wait_ge(sem("hidden_ready"), OPEN + h0 - 1 + i)
                    up(u0 + i, i % 2)
                for i in range(FT // 2):
                    pe.wait_ge(sem("hidden_ready"), OPEN + h0 + 2 * i + 2)
                    down(u0 + FT + i, HID, 2 * i, i == 0, i == FT // 2 - 1)

            def moe():
                u0, h0 = U0["moe"], H0["moe"]
                for t in range(NT):
                    for n, x in enumerate(XT):
                        for k in range(KT):
                            last = mm(bank[6][:, t * NEXP:(t + 1) * NEXP], x[:, k, t * P:(t + 1) * P].bitcast(fp32),
                                      RW[:, k, :], start=(n == 0 and k == 0), stop=(n == 1 and k == KT - 1))
                last.then_inc(sem("router_psum"), 1)
                with pe.Fori(0, NEXP) as e:
                    for n in range(ET):
                        pe.wait_ge(sem("hidden_ready"), OPEN + h0 - 1 + max(n, 1) + ET * e)
                        up(u0 + n, n % 2, EXP_REAL * e)
                    pe.wait_ge(sem("expert_taken"), 4 * e + 1)
                    k0 = 0
                    for i, kn in enumerate(EXP_DOWN):
                        pe.wait_ge(sem("hidden_ready"), OPEN + h0 + k0 + kn + ET * e)
                        down(u0 + ET + i, HID, k0, i == 0, i == len(EXP_DOWN) - 1, EXP_REAL * e)
                        k0 += kn

            def head_norm(n0, groups, group):
                for i in groups:
                    pe.wait_ge(sem("hn_square"), n0 + i + 1)
                    if i >= 2:
                        pe.wait_ge(sem("hn_done"), n0 + i - 1)
                    if group == 1:
                        last = mm(bank[2 + i % 2][:, :], bones, NQ[:, (i % 2) * 512:(i % 2 + 1) * 512], start=True, stop=True)
                    else:
                        for e in range(2):
                            last = mm(bank[2 + i % 2][:, 0:S], ones, NQ[:, (i % 2) * 512 + e * S:(i % 2) * 512 + (e + 1) * S],
                                      start=(e == 0), stop=(e == 1))
                    last.then_inc(sem("hn_sum"), 1)

            def ev():
                u0 = U0["ev"]
                pe.wait_ge(sem("xn_ready"), NORM_NO["ev"] - 3)
                transposed("ev", XN)
                for i in range(4):
                    feat("ev", u0 + i, i)
                for i in range(2):
                    tok("ev", u0 + 4 + i, 4 + i)
                    head_norm(0, [i], 1)
                for i in range(2):
                    feat("ev", u0 + 6 + i, 6 + i)
                    head_norm(0, [2 + i], 1)
                for i in range(2):
                    tok("ev", u0 + 8 + i, 8 + i)
                for i in range(4):
                    pe.wait_ge(sem("hn_done"), i + 1)
                    if i >= 2:
                        pe.wait_ge(sem("rope_done"), i - 1)
                    mm(bank[4 + i % 2][:, :], rot, F[:, 2 * i:2 * i + 2, :], start=True, stop=True)\
                        .then_inc(sem("rot_psum"), 1)
                pe.wait_ge(sem("gm_loaded"), 96)
                for g in range(8):
                    last = nc.tensor.transpose(bank[6 + g // 4][:, (g % 4) * P:(g % 4 + 1) * P], WS[:, g, :], ident)
                last.then_inc(sem("wst_psum"), 1)
                pe.wait_ge(sem("rope_done"), 4)
                pe.wait_ge(sem("vn_ready"), 1)
                for g in range(8):
                    hb = HD * (g % 2)
                    for t in range(NT):
                        last = mm(half(6 + g // 4)[hb:hb + HD, (g // 2) % 2, t * P:(t + 1) * P],
                                  V2[:, t, 512 + g * HD:512 + (g + 1) * HD], WST[:, g, :], start=True, stop=True)
                last.then_inc(sem("mixed_psum"), 1)
                pe.wait_ge(sem("gmlp_done"), 1)
                attention("ev")
                out_product("ev", u0 + 10)

            def xa(L):
                stage = f"xa{L}"
                u0 = U0[stage]
                pe.wait_ge(sem("xn_ready"), NORM_NO[f"xq{L}"] - 3)
                transposed(f"xq{L}", XN)
                for i in range(2):
                    feat(stage, u0 + i, i)
                pe.wait_ge(sem("xn_ready"), NORM_NO[f"xkv{L}"] - 3)
                transposed(f"xkv{L}", XN)
                for i in range(2, 4):
                    feat(stage, u0 + i, i)
                for i in range(4, 8):
                    feat(stage, u0 + i, i, src=MT)
                for i in range(4):
                    tok(stage, u0 + 8 + i, 8 + i, src=MT)
                    head_norm(4 + 12 * L, [2 * i, 2 * i + 1], 2)
                pe.wait_ge(sem("hn_done"), 12 + 12 * L)
                pe.wait_ge(sem("proj_taken"), ACT0[stage] + 12)
                attention(stage)
                out_product(stage, u0 + 12)

            def gla():
                u0 = U0["gla"]
                pe.wait_ge(sem("xn_ready"), NORM_NO["gla"] - 3)
                transposed("gla", XN)
                for n, x in enumerate(XT):
                    for k in range(KT):
                        last = mm(bank[6][0:16, 0:S], G1[:, k, :], x[:, k, :].bitcast(fp32), start=(n == 0 and k == 0),
                                  stop=(n == 1 and k == KT - 1))
                last.then_inc(sem("g1_psum"), 1)
                for i in range(4):
                    feat("gla", u0 + i, i)
                pe.wait_ge(sem("g1_ready"), 1)
                for h in range(4):
                    last = mm(half(2 + h // 2)[:, h % 2, :], LORA[0:16, h * P:(h + 1) * P], GL1, start=True, stop=True)
                last.then_inc(sem("g2_psum"), 1)
                for i in range(4):
                    tok("gla", u0 + 4 + i, 4 + i)
                for i in range(4):
                    feat("gla", u0 + 8 + i, 8 + i)
                pe.wait_ge(sem("gla_factors"), 1)
                pe.wait_ge(sem("proj_taken"), ACT0["gla"] + 12)
                for t in range(NT):
                    for h in range(4):
                        last = nc.tensor.transpose(bank[2 + t][:, h * P:(h + 1) * P],
                                                   KS[:, h * S + t * P:h * S + (t + 1) * P], ident)
                last.then_inc(sem("ksm_psum"), 1)
                for h in range(4):
                    for t in range(NT):
                        last = mm(bank[4 + h // 2][:, ((h % 2) * 2 + t) * P:((h % 2) * 2 + t + 1) * P],
                                  F[:, 4 + h, t * P:(t + 1) * P], F[:, h, t * P:(t + 1) * P], start=True, stop=True)
                last.then_inc(sem("att_psum"), 1)
                pe.wait_ge(sem("ksm_ready"), 1)
                pe.wait_ge(sem("att_ready"), 1)
                for c in range(NCH):
                    t, tb = c // 2, CH * (c % 2)
                    tc = slice(tb, tb + CH)
                    pe.wait_ge(sem("gs_ready"), c + 1)
                    if c:
                        pe.wait_ge(sem("go_taken"), c)
                    for h in range(4):
                        for e in range(2):
                            dst = bank[6][:, (2 * h + e) * CH:(2 * h + e + 1) * CH]
                            vc = slice(h * S + e * P, h * S + (e + 1) * P)
                            mm(dst, V2[tc, t, vc], ATT[tc, h, t, tc], start=True, stop=False)
                            last = mm(dst, GS[:, h, e * P:(e + 1) * P], F[:, h, c * CH:(c + 1) * CH],
                                      start=False, stop=True)
                    last.then_inc(sem("go_psum"), 1)
                    for h in range(4):
                        last = mm(half(2 + h // 2)[:, h % 2, :], KSM[tc, t, h * P:(h + 1) * P],
                                  V2[tc, t, h * S:(h + 1) * S], start=True, stop=True)
                    last.then_inc(sem("ds_psum"), 1)
                pe.wait_ge(sem("gs_ready"), NCH + 1)
                head_norm(12, range(4), 2)
                pe.wait_ge(sem("gla_done"), 1)
                out_product("gla", u0 + 12)

            def normed(name, src):
                pe.wait_ge(sem("xn_ready"), NORM_NO[name] - 3)
                transposed(name, src)

            mix(0)
            pe.wait_ge(sem("ln_done"), 1)
            transposed("ffn0", X)
            ffn("ffn0")
            mix(1)
            pe.wait_ge(sem("ln_done"), 3)
            transposed("moe", X)
            moe()
            ev()
            xa(0)
            normed("ffn1", XN)
            ffn("ffn1")
            gla()
            xa(1)
            normed("ffn2", XN)
            ffn("ffn2")

        @block.scalar
        def _(act):
            av = nc.scalar.activation
            chain = [0]

            def step(ins):
                chain[0] += 1
                ins.then_inc(sem("act_step"), 1)
                act.wait_ge(sem("act_step"), chain[0])

            def xt_out(name, dst, gain=None):
                n = NORM_NO[name]
                for j in range(4):
                    act.wait_ge(sem("xt_psum"), 4 * n + j + 1)
                    if gain is None:
                        last = av(dst[:, 2 * j:2 * j + 2, :], half(2 + j), ACT.Copy)
                    else:
                        for i in range(2):
                            last = av(dst[:, 2 * j + i, :], half(2 + j)[:, i, :], ACT.Copy, scale=col(gain, 2 * j + i))
                    last.then_inc(sem("xth_ready"), 1)

            def split_high(u, loaded=0, jobs=0):
                act.wait_ge(sem(f"slot_loaded{u % RING}"), loaded_value(u) + loaded)
                if before(u, HALF) is not None:
                    act.wait_ge(sem("gemm_done"), used_value(before(u, HALF)) + jobs)
                av(whi(u), raw(u), ACT.Copy).then_inc(sem("wh_ready"), 1)

            def ahead(u, loaded=0, jobs=0):
                if following(u) is not None:
                    split_high(following(u), loaded, jobs)

            def ot_high(pieces, n_ctx=None):
                if n_ctx is not None:
                    act.wait_ge(sem("ctx_taken"), n_ctx)
                for lo, hi in pieces:
                    av(OTH[:, lo:hi, :], OT[:, lo:hi, :], ACT.Copy).then_inc(sem("ot_high"), 1)

            def out_product(u0):
                for i in range(4):
                    ahead(u0 + i)

            def proj(stage, i, outs):
                act.wait_ge(sem("gemm_done"), JOB0[stage] + i + 1)
                for dst, src, fn, bias in outs:
                    last = av(dst, src, fn) if bias is None else av(dst, src, fn, bias=bias)
                last.then_inc(sem("proj_taken"), 1)

            def feat_out(stage, i, dest, fn=ACT.Copy):
                proj(stage, i, [(F[:, dest:dest + 2, :], half(i % 2), fn, None)])

            def exps(n, unit):
                kind, h, t = unit
                nk = unit_at(kind, h, t)[0]
                c0 = 8 * (n % 4)
                act.wait_ge(sem("nmax_ready"), n + 1)
                if kind == "swa":
                    av(TINY[:, c0 + 2:c0 + 3], SROW[:, SINK[0] + h:SINK[0] + h + 1], ACT.Exp, bias=TINY[:, c0:c0 + 1])
                av(SMX[:, n % 4, 0:nk * P], SMX[:, n % 4, 0:nk * P], ACT.Exp, bias=TINY[:, c0:c0 + 1],
                   accum_out=TINY[:, c0 + 1:c0 + 2]).then_inc(sem("exp_done"), 1)

            def pt_out(n, unit):
                kind, h, t = unit
                nk = unit_at(kind, h, t)[0]
                act.wait_ge(sem("pt_psum"), n + 1)
                if n >= 2:
                    act.wait_ge(sem("ctx_psum"), n - 1)
                av(PT[:, n % 2, 0:nk * P], half(4 + n % 2)[:, 0, 0:nk * P], ACT.Copy).then_inc(sem("pt_ready"), 1)

            def ctx_out(n, unit):
                kind, h, t = unit
                _, _, _, (parts, outs) = unit_at(kind, h, t)
                ne = outs.stop - outs.start
                act.wait_ge(sem("ctx_psum"), n + 1)
                av(OT[parts, outs, t * P:(t + 1) * P],
                   bank[6 + n % 2][parts, 0:ne * P].rearrange("p (e n) -> p e n", e=ne), ACT.Copy)\
                    .then_inc(sem("ctx_taken"), 1)

            SINK = [0]
            PAIRS = [(2 * i, 2 * i + 2) for i in range(4)]

            def attention(stage, filler=None):
                n0, units = UNITS[stage]
                for i in range(len(units) + 3):
                    if i < len(units):
                        exps(n0 + i, units[i])
                    if filler is not None:
                        filler(i)
                    if 2 <= i < len(units) + 2:
                        pt_out(n0 + i - 2, units[i - 2])
                    if i >= 3:
                        ctx_out(n0 + i - 3, units[i - 3])

            def mix(L):
                stage = f"mix{L}"
                SINK[0] = 8 * L
                if L == 0:
                    act.wait_ge(sem("params_in"), 80)
                u0 = U0[stage]
                xt_out(stage, XTH)
                i = 0
                for n, (_, _, jobs) in enumerate(MIX_PROJ):
                    ahead(u0 + n)
                    for kind, c, dest in jobs:
                        b = bank[i % 2]
                        if kind == "feat":
                            feat_out(stage, i, dest)
                        elif kind == "dup64":
                            proj(stage, i, [(F[o:o + HD, dest, :], b[0:HD, 0:S], ACT.Copy, None) for o in (0, HD)])
                        elif kind == "dup128":
                            proj(stage, i, [(F[o:o + HD, dest + g, :], b[g * HD:(g + 1) * HD, 0:S], ACT.Copy, None)
                                            for g in range(2) for o in (0, HD)])
                        else:
                            w = c[1]
                            proj(stage, i, [(TM[:, :, dest:dest + w], b[:, 0:NT * w].rearrange("p (t n) -> p t n", t=NT),
                                             ACT.Copy, None)])
                        if i == 7:
                            act.wait_ge(sem("shift_done"), L + 1)
                            av(F[0:64, F_LO, :], F[0:64, F_LO, :], ACT.Tanh)
                            av(F[:, F_LO + 1, :], F[:, F_LO + 1, :], ACT.Sigmoid).then_inc(sem("lora_in"), 1)
                        i += 1

                def gate(j):
                    i = N_PROJ + j
                    ahead(u0 + len(MIX_PROJ) + j)
                    proj(stage, i, [(G[:, 2 * j + e, :], half(i % 2)[:, e, :], ACT.Sigmoid, col(f"gate{L}", 2 * j + e))
                                    for e in range(2)])

                act.wait_ge(sem("lora_out"), 3 * L + 1)
                for m in range(2):
                    last = av(E[0][:, m * S:(m + 1) * S], half(2)[:, m, :], ACT.Sigmoid, bias=col(f"w0{L}", m))
                last.then_inc(sem("lora_taken"), 1)
                act.wait_ge(sem("lora_out"), 3 * L + 2)
                for m in range(2):
                    last = av(E[2][:, m * S:(m + 1) * S], half(3)[:, m, :], ACT.Sigmoid, bias=col(f"a0{L}", m))
                last.then_inc(sem("lora_taken"), 1)
                act.wait_ge(sem("lora_out"), 3 * L + 3)
                av(GG, half(4), ACT.Copy).then_inc(sem("lora_taken"), 1)
                for t in range(NT):
                    act.wait_ge(sem("idx_scores"), 2 * L + t + 1)
                    if t:
                        act.wait_ge(sem("idx_acc"), 2 * L + 1)
                    av(REL[:, 0:2, :], half(6), ACT.Relu, scale=HD ** -0.5)
                    av(REL[:, 2:4, :], half(7), ACT.Relu, scale=HD ** -0.5).then_inc(sem("idx_relu"), 1)
                    gate(t)
                act.wait_ge(sem("foxz_ready"), L + 1)
                z = TINY[:, 40:48]
                step(av(TINY[:, 48:56], z, ACT.Abs))
                step(av(TINY[:, 48:56], TINY[:, 48:56], ACT.Exp, scale=-1.0))
                av(TINY[:, 48:56], TINY[:, 48:56], ACT.Ln, bias=1.0).then_inc(sem("foxl_ready"), 1)
                gate(2)
                act.wait_ge(sem("scan_ready"), L + 1)
                av(E[3], E[1], ACT.Exp)
                av(E[4], E[1], ACT.Exp, scale=-1.0)
                av(E[6], E[6], ACT.Exp).then_inc(sem("exps_ready"), 1)
                act.wait_ge(sem("kk_sum"), L + 1)
                av(E[5], bank[2][:, :], ACT.Sqrt, bias=col("eps_kk")).then_inc(sem("kk_root"), 1)
                gate(3)
                for w in range(3):
                    act.wait_ge(sem("tok_psum"), 3 * L + w + 1)
                    av(TOK[:, w, :, :], half(4 + w), ACT.Copy).then_inc(sem("tok_ready"), 1)
                gate(4)
                for lv in range(1, 6):
                    act.wait_ge(sem("t1_psum"), 6 * L + lv + 1)
                    if lv > 1:
                        act.wait_ge(sem("xu_psum"), 5 * L + lv - 1)
                    av(T1[:, 0:4, :], bank[2][:, :].rearrange("p (i n) -> p i n", i=4), ACT.Copy)
                    av(T1[:, 4:8, :], bank[3][:, :].rearrange("p (i n) -> p i n", i=4), ACT.Copy)\
                        .then_inc(sem("t1_ready"), 1)
                    if lv in (1, 3, 4):
                        gate(5 + (lv > 1) + (lv > 3))
                for c in range(NCH):
                    act.wait_ge(sem("y_psum"), NCH * L + c + 1)
                    av(YT[:, :, c * CH:(c + 1) * CH], bank[4][:, 0:2 * CH].rearrange("p (f n) -> p f n", f=2), ACT.Copy)\
                        .then_inc(sem("y_taken"), 1)
                act.wait_ge(sem("gn_var"), L + 1)
                av(E[1], bank[3][:, :], ACT.Sqrt, scale=1.0 / HD, bias=col("eps_gn")).then_inc(sem("gn_root"), 1)
                act.wait_ge(sem("rwkv_done"), L + 1)
                gate(8)
                n0 = UNITS[stage][0]

                def beside(i):
                    if i % 4 == 0 and i // 4 < 7:
                        gate(9 + i // 4)
                    if i == 22:
                        ot_high([(0, 4)], n0 + 16)

                attention(stage, beside)
                ot_high([(4, 10)], n0 + len(UNITS[stage][1]))
                u = u0 + len(MIX_PROJ) + N_GATES
                for n in range(6):
                    ahead(u + n)

                def mrg_high(fp):
                    act.wait_ge(sem("merged"), 4 * L + fp + 1)
                    av(XTH[:, 2 * fp:2 * fp + 2, :], MRG[:, 2 * fp:2 * fp + 2, :], ACT.Copy).then_inc(sem("mrg_high"), 1)

                mrg_high(0)
                mrg_high(1)
                ahead(u + 6)
                mrg_high(2)
                mrg_high(3)
                for n in range(7, 10):
                    ahead(u + n)

            def root(count, scale, eps):
                act.wait_ge(sem("ms_ready"), count)
                av(TINY[:, 66:68], TINY[:, 64:66], ACT.Sqrt, scale=scale, bias=col(eps)).then_inc(sem("root_ready"), 1)

            def silu(bk):
                av(SIL[:, bk, :], half(bk)[:, 0, :], ACT.Silu).then_inc(sem("silu_ready"), 1)

            def ffn(stage):
                u0, job = U0[stage], JOB0[stage]
                with act.Fori(0, FT // RING) as r:
                    for i in range(RING):
                        ahead(u0 + i, 2 * 16 * r, RING * r)
                        act.wait_ge(sem("gemm_done"), job + i + 1 + RING * r)
                        silu(i % 2)
                for i in range(FT // RING * RING, FT):
                    ahead(u0 + i)
                    act.wait_ge(sem("gemm_done"), job + i + 1)
                    silu(i % 2)
                for i in range(FT // 2):
                    ahead(u0 + FT + i)

            def moe():
                u0, job = U0["moe"], JOB0["moe"]
                act.wait_ge(sem("router_top"), 1)
                av(TINY[:, 70:72], TINY[:, 68:70], ACT.Exp).then_inc(sem("router_exp"), 1)

                def beside(u, e):
                    f = following(u)
                    ahead(u, (loaded_value(f + len(EXP_UNITS)) - loaded_value(f)) * e, EXP_JOBS * e)

                with act.Fori(0, NEXP) as e:
                    for n in range(ET):
                        beside(u0 + n, e)
                        act.wait_ge(sem("gemm_done"), job + n + 1 + EXP_JOBS * e)
                        silu(n % 2)
                    for i in range(len(EXP_DOWN)):
                        beside(u0 + ET + i, e)

            def head_root(n0, groups, width):
                for i in groups:
                    act.wait_ge(sem("hn_sum"), n0 + i + 1)
                    w = 512 if width == HD else S
                    av(NQ[:, (i % 2) * 512:(i % 2) * 512 + w], bank[2 + i % 2][:, 0:w], ACT.Sqrt, scale=1.0 / width,
                       bias=col("eps_rms")).then_inc(sem("hn_root"), 1)

            def tok_out(stage, i, c0, fn=ACT.Copy):
                proj(stage, i, [(V2[:, :, c0:c0 + 256], half(i % 2), fn, None)])

            def ev():
                root(5, 1.0 / D, "eps_rms")
                xt_out("ev", XTH, "norm_mix0")
                u0 = U0["ev"]
                for i in range(4):
                    ahead(u0 + i)
                    feat_out("ev", i, 2 * i)
                for i in range(2):
                    ahead(u0 + 4 + i)
                    tok_out("ev", 4 + i, 256 * i)
                    head_root(0, [i], HD)
                for i in range(2):
                    ahead(u0 + 6 + i)
                    feat_out("ev", 6 + i, 8 + 2 * i, ACT.Gelu)
                    head_root(0, [2 + i], HD)
                for i in range(2):
                    ahead(u0 + 8 + i)
                    tok_out("ev", 8 + i, 512 + 256 * i, ACT.Gelu)
                act.wait_ge(sem("angle_ready"), 1)
                av(SIN, COS, ACT.Sin)
                step(av(COS, COS, ACT.Abs))
                av(COS, COS, ACT.Sin, scale=-1.0, bias=col("half_pi")).then_inc(sem("rope_table"), 1)
                act.wait_ge(sem("gvar_ready"), 1)
                av(TINY[:, 96:112], TINY[:, 80:96], ACT.Sqrt, scale=1.0 / HD, bias=col("eps_rms"))\
                    .then_inc(sem("groot_ready"), 1)
                attention("ev")
                act.wait_ge(sem("gmlp_done"), 1)
                ot_high(PAIRS, UNITS["ev"][0] + len(UNITS["ev"][1]))
                out_product(u0 + 10)

            def xa(L):
                stage = f"xa{L}"
                u0 = U0[stage]
                root(6 + 4 * L, 1.0 / D, "eps_rms")
                xt_out(f"xq{L}", XTH, f"norm_q{L}")
                root(7 + 4 * L, 1.0 / D, "eps_rms")
                for i in range(8):
                    if i == 2:
                        xt_out(f"xkv{L}", MTH, f"norm_kv{L}")
                    ahead(u0 + i)
                    feat_out(stage, i, 2 * i)
                for i in range(4):
                    ahead(u0 + 8 + i)
                    tok_out(stage, 8 + i, 256 * i)
                    head_root(4 + 12 * L, [2 * i, 2 * i + 1], S)
                attention(stage)
                ot_high(PAIRS, UNITS[stage][0] + len(UNITS[stage][1]))
                out_product(u0 + 12)

            def gla():
                root(9, 1.0 / D, "eps_rms")
                xt_out("gla", XTH, "norm_mix1")
                u0 = U0["gla"]
                act.wait_ge(sem("g1_psum"), 1)
                av(GL1, bank[6][0:16, 0:S], ACT.Copy).then_inc(sem("g1_ready"), 1)
                for i in range(4):
                    ahead(u0 + i)
                    feat_out("gla", i, 2 * i)
                act.wait_ge(sem("g2_psum"), 1)
                for h in range(4):
                    last = av(GB[:, h * S:(h + 1) * S], half(2 + h // 2)[:, h % 2, :], ACT.Identity, bias=col("b_g", h))
                step(last)
                step(av(GE, GB, ACT.Abs))
                step(av(GE, GE, ACT.Exp, scale=-1.0))
                av(GE, GE, ACT.Ln, bias=1.0).then_inc(sem("gl_ready"), 1)
                for i in range(8):
                    ahead(u0 + 4 + i)
                    if i < 4:
                        tok_out("gla", 4 + i, 256 * i)
                    else:
                        feat_out("gla", 4 + i, 2 * i, ACT.Silu)
                    if i == 1:
                        act.wait_ge(sem("gscan_ready"), 1)
                        av(GE, GB, ACT.Exp).then_inc(sem("gexp_ready"), 1)
                    elif i == 2:
                        act.wait_ge(sem("gexp_used"), 1)
                        av(GE, GB, ACT.Exp, scale=-1.0).then_inc(sem("gexp_ready"), 1)
                    elif i == 3:
                        act.wait_ge(sem("glast_ready"), 1)
                        av(KS, KS, ACT.Exp).then_inc(sem("gexp_ready"), 1)
                act.wait_ge(sem("ksm_psum"), 1)
                for t in range(NT):
                    last = av(KSM[:, t, :], bank[2 + t][:, :], ACT.Copy)
                last.then_inc(sem("ksm_ready"), 1)
                for c in range(NCH):
                    act.wait_ge(sem("go_psum"), c + 1)
                    av(OT[:, 0:8, c * CH:(c + 1) * CH], bank[6][:, :].rearrange("p (e n) -> p e n", e=8), ACT.Copy)\
                        .then_inc(sem("go_taken"), 1)
                head_root(12, range(4), S)
                act.wait_ge(sem("gla_done"), 1)
                ot_high(PAIRS)
                out_product(u0 + 12)

            split_high(0)
            mix(0)
            root(1, 1.0, "eps_ln")
            xt_out("ffn0", XTH)
            ffn("ffn0")
            root(2, 1.0, "eps_ln")
            mix(1)
            root(3, 1.0, "eps_ln")
            xt_out("moe", XTH)
            moe()
            root(4, 1.0, "eps_ln")
            ev()
            xa(0)
            root(8, 1.0 / D, "eps_rms")
            xt_out("ffn1", XTH, "norm_ffn0")
            ffn("ffn1")
            gla()
            xa(1)
            root(12, 1.0 / D, "eps_rms")
            xt_out("ffn2", XTH, "norm_ffn1")
            ffn("ffn2")

        @block.vector
        def _(dve):
            v = nc.vector
            chain = [0]
            made = {}

            def step(ins):
                chain[0] += 1
                ins.then_inc(sem("dve_step"), 1)
                dve.wait_ge(sem("dve_step"), chain[0])

            def signal(ins, name):
                made[name] = made.get(name, 0) + 1
                ins.then_inc(sem(name), 1)
                dve.wait_ge(sem(name), made[name])

            def cols(t, lo, n):
                return t[:, lo:lo + n]

            def stt(out, in0, scalar, in1, op0, op1, **kw):
                return v.scalar_tensor_tensor(out=out, in0=in0, scalar=scalar, in1=in1, op0=op0, op1=op1, **kw)

            def low(u, more=0):
                dve.wait_ge(sem("wh_ready"), split_value(u) + more)
                v.tensor_tensor(wlo(u), raw(u), whi(u).bitcast(fp32), ALU.subtract).then_inc(sem("wl_ready"), 1)

            def xt_low(name, high, dst, gain=None):
                for j in range(4):
                    dve.wait_ge(sem("xth_ready"), 4 * NORM_NO[name] + j + 1)
                    pair = slice(2 * j, 2 * j + 2)
                    if gain is None:
                        last = v.tensor_tensor(dst[:, pair, :], half(2 + j), high[:, pair, :].bitcast(fp32), ALU.subtract)
                    else:
                        for i in range(2):
                            last = stt(dst[:, 2 * j + i, :], half(2 + j)[:, i, :], col(gain, 2 * j + i),
                                       high[:, 2 * j + i, :].bitcast(fp32), ALU.mult, ALU.subtract)
                    last.then_inc(sem("xt_ready"), 1)

            def ot_low(stage, n, pieces):
                for lo, hi in pieces:
                    n += 1
                    dve.wait_ge(sem("ot_high"), OT0[stage] + n)
                    v.tensor_tensor(OTL[:, lo:hi, :], OT[:, lo:hi, :], OTH[:, lo:hi, :].bitcast(fp32), ALU.subtract)\
                        .then_inc(sem("ot_low"), 1)

            PAIRS = [(2 * i, 2 * i + 2) for i in range(4)]

            def out_product(stage, u0):
                ot_low(stage, 0, PAIRS)
                for i in range(4):
                    low(following(u0 + i))

            MASK = {"swa": window, "fox": causal, "moba": causal, "dsa": SEL}
            LAYER = [0]

            def scaled(n, unit):
                kind, h, t = unit
                w = unit_at(kind, h, t)[0] * P
                c0 = 8 * (n % 4)
                dve.wait_ge(sem("scores_ready"), n + 1)
                if n >= 4:
                    dve.wait_ge(sem("pt_psum"), n - 3)
                src, dst = bank[2 + n % 2][:, 0:w], SMX[:, n % 4, 0:w]
                if kind == "cross":
                    signal(v.tensor_scalar(dst, src, SCORE_SCALE[kind], None, ALU.mult), "scores_taken")
                else:
                    signal(stt(dst, src, SCORE_SCALE[kind], MASK[kind][:, t, 0:w], ALU.mult, ALU.add), "scores_taken")
                nm = TINY[:, c0:c0 + 1]
                red = v.tensor_reduce(nm, dst, axis=AX, op=ALU.max, negate=True)
                if kind == "swa":
                    step(red)
                    s0 = 8 * LAYER[0] + h
                    red = stt(nm, SROW[:, s0:s0 + 1], -1.0, nm, ALU.mult, ALU.min)
                signal(red, "nmax_ready")

            def normalised(n, unit):
                kind, h, t = unit
                w = unit_at(kind, h, t)[0] * P
                c0 = 8 * (n % 4)
                dve.wait_ge(sem("exp_done"), n + 1)
                rs, es, ri = (TINY[:, c0 + e:c0 + e + 1] for e in (1, 2, 3))
                if kind == "swa":
                    step(v.tensor_tensor(rs, rs, es, ALU.add))
                step(v.reciprocal(ri, rs))
                signal(v.tensor_scalar(SMX[:, n % 4, 0:w], SMX[:, n % 4, 0:w], ri, None, ALU.mult), "probs_ready")

            def attention(stage, filler=None):
                n0, units = UNITS[stage]
                for i in range(len(units) + 1):
                    if i < len(units):
                        scaled(n0 + i, units[i])
                    if i:
                        normalised(n0 + i - 1, units[i - 1])
                    if filler is not None:
                        filler(i)

            def mix(L):
                stage = f"mix{L}"
                LAYER[0] = L
                a0 = ACT0[stage]
                if L == 0:
                    dve.wait_ge(sem("params_in"), 80)
                u0 = U0[stage]
                xt_low(stage, XTH, XTL)
                gates = u0 + len(MIX_PROJ)
                for n in range(1, 5):
                    low(u0 + n)
                dve.wait_ge(sem("proj_taken"), a0 + 4)
                R8 = F[:, F_R:F_R + 8, :]
                v.tensor_tensor(DT[:, :, 1:S], R8[:, :, 0:S - 1], R8[:, :, 1:S], ALU.subtract)
                step(v.tensor_scalar(DT[:, :, 0:1], R8[:, :, 0:1], -1.0, None, ALU.mult))
                for m in range(8):
                    last = stt(F[:, F_R + m, :], DT[:, m, :], col(f"mu{L}", m), F[:, F_R + m, :], ALU.mult, ALU.add)
                signal(last, "shift_done")
                for n in range(5, 8):
                    low(u0 + n)
                for m in range(2):
                    last = v.tensor_scalar(cols(E[7], m * S, S), F[:, F_K + m, :], col(f"k_k{L}", m), None, ALU.mult)
                step(last)
                signal(v.tensor_tensor(E[5], E[7], E[7], ALU.mult), "kk_square")
                for n in range(8, len(MIX_PROJ) + 1):
                    low(u0 + n)
                dve.wait_ge(sem("lora_taken"), 3 * L + 1)
                step(v.tensor_scalar(E[0], E[0], -float(np.exp(-0.5)), None, ALU.mult))
                step(v.tensor_tensor_scan(E[1], keep, E[0], 0.0, ALU.mult, ALU.add))
                signal(v.tensor_tensor(E[6], E[1], E[0], ALU.subtract), "scan_ready")
                dve.wait_ge(sem("idx_relu"), 2 * L + 1)
                iw = TINY[:, 56:64].rearrange("p (t h) -> p t h", t=NT)
                step(v.tensor_scalar(iw, TM[:, :, TM_DSA_W:TM_DSA_W + 4], 0.5, None, ALU.mult))
                for t in range(NT):
                    dve.wait_ge(sem("idx_relu"), 2 * L + t + 1)
                    step(v.tensor_scalar(SCORE[:, t, :], REL[:, 0, :], iw[:, t, 0:1], None, ALU.mult))
                    for h in range(1, 4):
                        ins = stt(SCORE[:, t, :], REL[:, 2 * (h % 2) + h // 2, :], iw[:, t, h:h + 1], SCORE[:, t, :], ALU.mult, ALU.add)
                        if h < 3:
                            step(ins)
                    signal(ins, "idx_acc")
                    low(gates + 1 + t)
                z = TINY[:, 40:48].rearrange("p (t h) -> p t h", t=NT)
                fb = SROW[:, 16 + 4 * L:20 + 4 * L].unsqueeze(1).to_broadcast([P, NT, 4])
                signal(v.tensor_tensor(z, TM[:, :, TM_FOX_F:TM_FOX_F + 4], fb, ALU.add), "foxz_ready")
                step(v.tensor_tensor(SCORE, SCORE, admit, ALU.add))
                dve.wait_ge(sem("foxl_ready"), L + 1)
                signal(stt(TM[:, :, TM_FOX_F:TM_FOX_F + 4], z, 0.0, TINY[:, 48:56].rearrange("p (t h) -> p t h", t=NT),
                           ALU.min, ALU.subtract), "logf_ready")
                dve.wait_ge(sem("lora_taken"), 3 * L + 2)
                for m in range(2):
                    last = v.tensor_scalar(cols(E[0], m * S, S), cols(E[2], m * S, S), -1.0, col(f"k_a{L}", m),
                                           ALU.add, ALU.mult)
                step(last)
                for m in range(2):
                    last = stt(F[:, F_K + m, :], cols(E[0], m * S, S), 1.0, F[:, F_K + m, :], ALU.add, ALU.mult)
                step(last)
                dve.wait_ge(sem("foxc_psum"), L + 1)
                signal(v.tensor_scalar(C8[0:4, :], bank[5][0:4, 0:S], 1.0 / SCORE_SCALE["fox"], None, ALU.mult), "c8_ready")
                low(gates + 3)
                dve.wait_ge(sem("kk_root"), L + 1)
                step(v.reciprocal(E[5], E[5]))
                step(v.tensor_tensor(E[7], E[7], E[5], ALU.mult))
                for m in range(2):
                    last = stt(cols(E[5], m * S, S), F[:, F_R + m, :], col(f"r_k{L}", m), F[:, F_K + m, :],
                               ALU.mult, ALU.mult)
                signal(last, "rkr_ready")
                dve.wait_ge(sem("exps_ready"), L + 1)

                def tiles(x):
                    return x.rearrange("p (t n) -> p t n", t=NT)

                for f in range(2):
                    stt(AR[:, f, :, 0, :], tiles(cols(E[7], f * S, S)), -1.0, tiles(cols(E[6], f * S, S)), ALU.mult, ALU.mult)
                    v.tensor_tensor(AR[:, f, :, 1, :], tiles(F[:, F_R + f, :]), tiles(cols(E[3], f * S, S)), ALU.mult)
                v.tensor_copy(TINY[:, 112:120].rearrange("p (x o) -> p x o", o=1),
                              E[3].rearrange("p (x n) -> p x n", n=CH)[:, :, CH - 1:CH])
                two = lambda x: x.rearrange("p (f n) -> p f n", f=2)
                v.tensor_tensor(BKT[:, 1, :, :], F[:, F_K:F_K + 2, :], two(E[4]), ALU.mult)
                step(v.tensor_tensor(E[1], E[7], E[2], ALU.mult))
                signal(v.tensor_tensor(BKT[:, 0, :, :], two(E[1]), two(E[4]), ALU.mult), "rwkv_factors")
                low(gates + 4)
                dve.wait_ge(sem("rkr_sum"), L + 1)
                signal(v.tensor_tensor(OT[:, 6:8, :], half(3), F[:, F_V:F_V + 2, :], ALU.mult), "bonus_taken")
                signal(v.memset(ST, 0.0), "state_ready")
                dve.wait_ge(sem("grams_cleared"), L + 1)
                mask = strict_incl.bitcast(i32).unsqueeze(1).to_broadcast([P, 2, 2 * P])
                for n in range(8):
                    dve.wait_ge(sem("gram_psum"), 8 * L + n + 1)
                    lo = 16 + 8 * (n // 4) + 2 * (n % 4)
                    signal(v.copy_predicated(G[:, lo:lo + 2, :], mask, half(2 + n % 4)), "gram_taken")

                def select(r):
                    t = r // (TOPK // 8)
                    best = TINY[:, 72:80]
                    step(v.max(out=best, in_=SCORE[:, t, :]))
                    step(v.match_replace(out=SCORE[:, t, :], in_to_replace=best, in_values=SCORE[:, t, :],
                                         imm_value=TAKEN))

                eight = lambda x: x.unsqueeze(1).to_broadcast([P, 8, P])
                four = lambda x: x.unsqueeze(1).to_broadcast([P, 4, P])
                quad = lambda b: bank[b][:, :].rearrange("p (i n) -> p i n", i=4)
                signal(v.tensor_tensor(LM, MB[:, :, 0, :], eight(levels[:, 0, :]), ALU.mult), "lm_ready")
                step(v.tensor_tensor(XIT, LM, eight(ident), ALU.add))
                low(gates + 5)
                dve.wait_ge(sem("t1_psum"), 6 * L + 1)
                v.tensor_tensor(XI[:, 0:4, :], quad(2), four(ident), ALU.add)
                step(v.tensor_tensor(XI[:, 4:8, :], quad(3), four(ident), ALU.add))
                for lv in range(1, 6):
                    dve.wait_ge(sem("t1_psum"), 6 * L + lv)
                    ins = v.tensor_tensor(LM, MB[:, :, 0, :], eight(levels[:, lv, :]), ALU.mult)
                    if lv > 1:
                        step(ins)
                        dve.wait_ge(sem("xu_psum"), 5 * L + lv - 1)
                        v.tensor_tensor(XI[:, 0:4, :], quad(4), XI[:, 0:4, :], ALU.add)
                        v.tensor_tensor(XI[:, 4:8, :], quad(5), XI[:, 4:8, :], ALU.add)
                        v.tensor_tensor(XIT[:, 0:4, :], quad(6), XIT[:, 0:4, :], ALU.add)
                        ins = v.tensor_tensor(XIT[:, 4:8, :], quad(7), XIT[:, 4:8, :], ALU.add)
                    signal(ins, "lm_ready")
                    if lv in (1, 3, 4):
                        low(gates + 6 + (lv > 1) + (lv > 3))
                    for r in range(2 * lv - 2, 2 * lv):
                        select(r)
                dve.wait_ge(sem("xu_psum"), 5 * L + 5)
                v.tensor_tensor(XIT[:, 0:4, :], quad(6), XIT[:, 0:4, :], ALU.add)
                signal(v.tensor_tensor(XIT[:, 4:8, :], quad(7), XIT[:, 4:8, :], ALU.add), "inverse_ready")
                for c in range(NCH):
                    n = NCH * L + c
                    tc = slice(CH * (c % 2), CH * (c % 2) + CH)
                    dve.wait_ge(sem("r1_psum"), n + 1)
                    signal(v.tensor_copy(R1[tc, :], bank[2][tc, 0:256]), "r1_ready")
                    dve.wait_ge(sem("sa_psum"), n + 1)
                    signal(v.tensor_copy(SA[tc, :], bank[3][tc, 0:256]), "sa_ready")
                    dve.wait_ge(sem("y_psum"), n + 1)
                    step(v.tensor_tensor(ST, bank[5][:, 0:2 * HD].rearrange("p (f n) -> p f n", f=2), ST, ALU.add))
                    for f in range(2):
                        last = v.tensor_scalar(ST[:, f, :], ST[:, f, :], TINY[:, 112 + 4 * f + c:113 + 4 * f + c],
                                               None, ALU.mult)
                    signal(last, "state_ready")
                    select(10 + c)
                dve.wait_ge(sem("gn_sum"), L + 1)
                dve.wait_ge(sem("y_taken"), NCH * (L + 1))
                yt = YT.rearrange("p f n -> p (f n)")
                step(stt(yt, bank[2][:, :], -1.0 / HD, yt, ALU.mult, ALU.add))
                signal(v.tensor_tensor(E[0], yt, yt, ALU.mult), "gn_square")
                for r in (14, 15):
                    select(r)
                signal(v.tensor_scalar(SEL[:, :, :], SCORE, -2e30, NEG, ALU.is_ge, ALU.mult), "dsa_mask")
                dve.wait_ge(sem("gn_root"), L + 1)
                step(v.reciprocal(E[1], E[1]))
                step(v.tensor_tensor(yt, yt, E[1], ALU.mult))
                for f in range(2):
                    last = v.tensor_scalar(YT[:, f, :], YT[:, f, :], col(f"gn_g{L}", f), col(f"gn_b{L}", f),
                                           ALU.mult, ALU.add)
                step(last)
                step(v.tensor_tensor(YT, YT, OT[:, 6:8, :], ALU.add))
                signal(v.tensor_tensor(OT[:, 4:6, :], YT, GG, ALU.mult), "rwkv_done")
                low(gates + 9)

                def beside(i):
                    if i % 4 == 0 and i // 4 < 7:
                        low(gates + 10 + i // 4)
                    if i == 22:
                        ot_low(stage, 0, [(0, 4)])

                attention(stage, beside)
                ot_low(stage, 1, [(4, 10)])
                tmp = wk(4096, 1024).rearrange("p (b h n) -> p b h n", b=2, h=2)
                u = gates + N_GATES
                j = 0

                def mrg_low(fp):
                    pair = slice(2 * fp, 2 * fp + 2)
                    dve.wait_ge(sem("mrg_high"), 4 * L + fp + 1)
                    v.tensor_tensor(XTL[:, pair, :], MRG[:, pair, :], XTH[:, pair, :].bitcast(fp32), ALU.subtract)\
                        .then_inc(sem("mrg_low"), 1)

                for _, _, parts in BRANCHES:
                    for c in range(2):
                        low(u + 1)
                        if u == gates + N_GATES + 5:
                            mrg_low(0)
                            mrg_low(1)
                        for br, _, _, _ in parts:
                            for fp in (2 * c, 2 * c + 1):
                                dve.wait_ge(sem("gemm_done"), used_value(gates + N_GATES - 1) + j + 1)
                                g = G[:, 8 * br + 2 * fp:8 * br + 2 * fp + 2, :]
                                acc = MRG[:, 2 * fp:2 * fp + 2, :]
                                if br == 0:
                                    signal(v.tensor_tensor(acc, g, half(j % 2), ALU.mult), "merge_taken")
                                else:
                                    signal(v.tensor_tensor(tmp[:, j % 2, :, :], g, half(j % 2), ALU.mult), "merge_taken")
                                    ins = v.tensor_tensor(acc, tmp[:, j % 2, :, :], acc, ALU.add)
                                    if br == 3:
                                        signal(ins, "merged")
                                    else:
                                        step(ins)
                                j += 1
                        u += 1
                low(u + 1)
                mrg_low(2)
                mrg_low(3)
                for i in range(1, 4):
                    low(following(u + i))

            def layer_norm(k, stage):
                if stage != "moe":
                    dve.wait_ge(sem("gemm_done"), used_value(STAGE_END[stage] - 1))
                for t in range(NT):
                    for h in range(2):
                        hc = slice(h * 512, (h + 1) * 512)
                        y = V2[:, t, hc] if stage == "moe" else bank[2 + 2 * t + h][:, :]
                        ins = stt(X[:, t, hc], X[:, t, hc], ALPHA, y, ALU.mult, ALU.add)
                step(ins)
                stats = TINY[:, 120:144].rearrange("p (t h n) -> p t h n", t=NT, h=2)
                for t in range(NT):
                    for h in range(2):
                        ins = v.bn_stats(stats[:, t, h, :], X[:, t, h * 512:(h + 1) * 512])
                step(ins)
                mv = TINY[:, 144:148].rearrange("p (t n) -> p t n", t=NT)
                for t in range(NT):
                    ins = v.bn_aggr(mv[:, t, :], stats[:, t, :, :])
                step(ins)
                signal(v.tensor_copy(TINY[:, 64:66].rearrange("p (t n) -> p t n", t=NT), mv[:, :, 1:2]), "ms_ready")
                dve.wait_ge(sem("root_ready"), made["ms_ready"])
                step(v.reciprocal(TINY[:, 68:70], TINY[:, 66:68]))
                dve.wait_ge(sem("rows_loaded"), 32 * (k + 1))
                for t in range(NT):
                    ins = stt(X[:, t, :], X[:, t, :], mv[:, t, 0:1], ROWS[:, 0:D], ALU.subtract, ALU.mult)
                step(ins)
                for t in range(NT):
                    ins = stt(X[:, t, :], X[:, t, :], TINY[:, 68 + t:69 + t], ROWS[:, D:2 * D], ALU.mult, ALU.add)
                signal(ins, "ln_done")

            def residual(stage):
                dve.wait_ge(sem("gemm_done"), used_value(STAGE_END[stage] - 1))
                for t in range(NT):
                    for h in range(2):
                        hc = slice(h * 512, (h + 1) * 512)
                        ins = v.tensor_tensor(X[:, t, hc], bank[2 + 2 * t + h][:, :], X[:, t, hc], ALU.add)
                return ins

            def rms_norm(name, src):
                dve.wait_ge(sem("xt_psum"), 4 * NORM_NO[name])
                for t in range(NT):
                    ins = stt(XN[:, t, :], src[:, t, :], 1.0, src[:, t, :], ALU.mult, ALU.mult,
                              accum_out=TINY[:, 64 + t:65 + t])
                signal(ins, "ms_ready")
                dve.wait_ge(sem("root_ready"), made["ms_ready"])
                step(v.reciprocal(TINY[:, 68:70], TINY[:, 66:68]))
                for t in range(NT):
                    ins = v.tensor_scalar(XN[:, t, :], src[:, t, :], TINY[:, 68 + t:69 + t], None, ALU.mult)
                signal(ins, "xn_ready")

            def hidden(n, bk, at, more=0):
                dve.wait_ge(sem("silu_ready"), n + 1 + more)
                sil, linear = SIL[:, bk, :].unsqueeze(1), half(bk)[:, 1:2, :]
                v.tensor_tensor(HT[:, bk:bk + 1, :], sil, linear, ALU.mult)
                v.tensor_tensor(HIDH[:, at, :], sil, linear, ALU.mult).then_inc(sem("hidden_high"), 1)
                dve.wait_ge(sem("hidden_high"), n + 1 + more)
                v.tensor_tensor(HIDL[:, at, :], HT[:, bk:bk + 1, :], HIDH[:, at, :].bitcast(fp32), ALU.subtract)\
                    .then_inc(sem("hidden_ready"), 1)

            def ffn(stage):
                u0, h0 = U0[stage], H0[stage]
                with dve.Fori(0, FT // RING) as r:
                    for i in range(RING):
                        low(u0 + i + 1, RING * r)
                        hidden(h0 + i, i % 2, bass.ds(RING * r + i, 1), RING * r)
                for i in range(FT // RING * RING, FT):
                    low(u0 + i + 1)
                    hidden(h0 + i, i % 2, slice(i, i + 1))
                for i in range(FT // 2):
                    if following(u0 + FT + i) is not None:
                        low(following(u0 + FT + i))

            def moe():
                h0 = H0["moe"]
                lg, eq, cum, lg2 = (TINY[:, c:c + 16].rearrange("p (t e) -> p t e", t=NT) for c in (128, 176, 192, 240))
                comb, one1, one2 = (TINY[:, c:c + 16].rearrange("p (t e) -> p t e", t=NT) for c in (160, 208, 224))
                dve.wait_ge(sem("router_psum"), 1)
                rb = SROW[:, 24:32].unsqueeze(1).to_broadcast([P, NT, NEXP])
                step(v.tensor_tensor(lg, bank[6][:, 0:16].rearrange("p (t e) -> p t e", t=NT), rb, ALU.add))

                def best(src, m, one):
                    mt = TINY[:, m:m + 2].rearrange("p (t n) -> p t n", t=NT)
                    step(v.tensor_reduce(TINY[:, m:m + 2], src, axis=AX, op=ALU.max))
                    step(v.tensor_tensor(eq, src, mt.to_broadcast([P, NT, NEXP]), ALU.is_equal))
                    for t in range(NT):
                        ins = v.tensor_tensor_scan(cum[:, t, :], ones[:, 0:NEXP], eq[:, t, :], 0.0, ALU.mult, ALU.add)
                    step(ins)
                    step(stt(one, cum, 1.0, eq, ALU.is_equal, ALU.mult))

                best(lg, 148, one1)
                step(stt(lg2, one1, TAKEN, lg, ALU.mult, ALU.add))
                best(lg2, 150, one2)
                signal(v.tensor_tensor(TINY[:, 68:70], TINY[:, 150:152], TINY[:, 148:150], ALU.subtract), "router_top")
                dve.wait_ge(sem("router_exp"), 1)
                step(v.tensor_scalar(TINY[:, 152:154], TINY[:, 70:72], 1.0, None, ALU.add))
                step(v.reciprocal(TINY[:, 154:156], TINY[:, 152:154]))
                step(v.tensor_tensor(TINY[:, 156:158], TINY[:, 70:72], TINY[:, 154:156], ALU.mult))
                for t in range(NT):
                    ins = v.tensor_scalar(comb[:, t, :], one1[:, t, :], TINY[:, 154 + t:155 + t], None, ALU.mult)
                step(ins)
                for t in range(NT):
                    ins = stt(comb[:, t, :], one2[:, t, :], TINY[:, 156 + t:157 + t], comb[:, t, :], ALU.mult, ALU.add)
                step(ins)
                v.memset(V2, 0.0).then_inc(sem("expert_taken"), 1)
                dve.wait_ge(sem("expert_taken"), 1)
                u0 = U0["moe"]
                with dve.Fori(0, NEXP) as e:
                    for n in range(ET):
                        low(u0 + n + 1, EXP_REAL * e)
                        hidden(h0 + n, n % 2, slice(n, n + 1), ET * e)
                    for i in range(len(EXP_DOWN)):
                        low(following(u0 + ET + i), EXP_REAL * e)
                    dve.wait_ge(sem("gemm_done"), JOB0["moe"] + EXP_JOBS * e + EXP_JOBS)
                    for t in range(NT):
                        for h in range(2):
                            hc = slice(h * 512, (h + 1) * 512)
                            stt(V2[:, t, hc], bank[2 + 2 * t + h][:, :], comb[:, t, bass.ds(e, 1)], V2[:, t, hc],
                                ALU.mult, ALU.add).then_inc(sem("expert_taken"), 1)
                    dve.wait_ge(sem("expert_taken"), 4 * e + 5)

            def head_norm(count, a0, need, tiles, gains, per_head, beside=lambda i: None):
                def square(i):
                    if need is not None:
                        dve.wait_ge(sem("proj_taken"), a0 + i + 1)
                    q = NQ[:, (i % 2) * 512:(i % 2 + 1) * 512].rearrange("p (e n) -> p e n", e=2)
                    signal(v.tensor_tensor(q, tiles(i), tiles(i), ALU.mult), "hn_square")

                square(0)
                for i in range(count):
                    beside(i)
                    if i + 1 < count:
                        square(i + 1)
                    dve.wait_ge(sem("hn_root"), made["hn_done"] + 1 if "hn_done" in made else 1)
                    w = 512 if per_head else S
                    r = NQ[:, (i % 2) * 512:(i % 2) * 512 + w]
                    step(v.reciprocal(r, r))
                    for e in range(2):
                        ins = stt(tiles(i)[:, e, :], tiles(i)[:, e, :], gains(i, e), r[:, e * S:(e + 1) * S] if per_head else r,
                                  ALU.mult, ALU.mult)
                    signal(ins, "hn_done")

            def ev():
                rms_norm("ev", X)
                u0 = U0["ev"]
                xt_low("ev", XTH, XTL, "norm_mix0")
                low(u0 + 1)
                dve.wait_ge(sem("gm_loaded"), 96)
                step(v.tensor_copy(SIN, POSI))
                step(v.tensor_scalar(COS, SIN, col("inv_freq"), None, ALU.mult))
                magic = 12582912.0
                step(v.tensor_scalar(SIN, COS, float(1.0 / (2.0 * np.pi)), magic, ALU.mult, ALU.add))
                step(v.tensor_scalar(SIN, SIN, -magic, None, ALU.add))
                c1 = 6.28125
                c2 = float(np.float32(np.round((2 * np.pi - c1) * 2 ** 21) / 2 ** 21))
                for c in (c1, c2, float(2 * np.pi - c1 - c2)):
                    step(stt(COS, SIN, -c, COS, ALU.mult, ALU.add))
                signal(v.tensor_scalar(COS, COS, 3.1415925, -3.1415925, ALU.min, ALU.max), "angle_ready")
                for i in range(2, 5):
                    low(u0 + i)
                head_norm(4, ACT0["ev"], True, lambda i: F[:, 2 * i:2 * i + 2, :],
                          lambda i, e: col("q_gain" if i < 2 else "k_gain"), True, lambda i: low(u0 + 5 + i))
                for i in range(9, 11):
                    low(u0 + i)
                dve.wait_ge(sem("rope_table"), 1)
                both = lambda x: x.unsqueeze(1).to_broadcast([P, 2, S])
                for i in range(4):
                    q = NQ[:, (i % 2) * 512:(i % 2 + 1) * 512].rearrange("p (e n) -> p e n", e=2)
                    f = F[:, 2 * i:2 * i + 2, :]
                    dve.wait_ge(sem("rot_psum"), i + 1)
                    v.tensor_tensor(q, half(4 + i % 2), both(SIN), ALU.mult)
                    step(v.tensor_tensor(f, f, both(COS), ALU.mult))
                    signal(v.tensor_tensor(f, f, q, ALU.add), "rope_done")
                dve.wait_ge(sem("wst_psum"), 1)
                for b in range(2):
                    ins = v.tensor_tensor(WST[:, 4 * b:4 * b + 4, :], bank[6 + b][:, :].rearrange("p (i n) -> p i n", i=4),
                                          tril.unsqueeze(1).to_broadcast([P, 4, P]), ALU.mult)
                step(ins)
                dve.wait_ge(sem("proj_taken"), ACT0["ev"] + 10)
                stat = lambda c: TINY[:, c:c + 16].rearrange("p (t g o) -> p t g o", t=NT, g=8)
                for t in range(NT):
                    vg = V2[:, t, 512:1024].rearrange("p (g d) -> p g d", g=8)
                    sq = NQ[:, t * 512:(t + 1) * 512].rearrange("p (g d) -> p g d", g=8)
                    m = stat(80)[:, t, :, :].to_broadcast([P, 8, HD])
                    step(v.tensor_reduce(TINY[:, 80 + 8 * t:88 + 8 * t], vg, axis=AX, op=ALU.add))
                    step(stt(vg, m, -1.0 / HD, vg, ALU.mult, ALU.add))
                    step(v.tensor_tensor(sq, vg, vg, ALU.mult))
                    ins = v.tensor_reduce(TINY[:, 80 + 8 * t:88 + 8 * t], sq, axis=AX, op=ALU.add)
                    if t == 0:
                        step(ins)
                signal(ins, "gvar_ready")
                dve.wait_ge(sem("groot_ready"), 1)
                step(v.reciprocal(TINY[:, 80:96], TINY[:, 96:112]))
                for t in range(NT):
                    vg = V2[:, t, 512:1024].rearrange("p (g d) -> p g d", g=8)
                    step(v.tensor_tensor(vg, vg, stat(80)[:, t, :, :].to_broadcast([P, 8, HD]), ALU.mult))
                    step(v.tensor_tensor(V2[:, t, 512:1024], V2[:, t, 512:1024], GLN[:, 0, :], ALU.mult))
                    ins = v.tensor_tensor(V2[:, t, 512:1024], V2[:, t, 512:1024], GLN[:, 1, :], ALU.add)
                    if t == 0:
                        step(ins)
                signal(ins, "vn_ready")
                dve.wait_ge(sem("mixed_psum"), 1)
                for g in range(8):
                    hb = HD * (g % 2)
                    ins = v.tensor_tensor(OT[hb:hb + HD, 4 + g // 2, :].rearrange("p (t n) -> p t n", t=NT),
                                          half(6 + g // 4)[hb:hb + HD, (g // 2) % 2, :].rearrange("p (t n) -> p t n", t=NT),
                                          BS[hb:hb + HD, g, :].unsqueeze(1).to_broadcast([HD, NT, P]), ALU.add)
                step(ins)
                signal(v.tensor_tensor(OT[:, 4:8, :], OT[:, 4:8, :], F[:, 8:12, :], ALU.mult), "gmlp_done")
                attention("ev")
                out_product("ev", u0 + 10)

            def xa(L, former):
                u0 = U0[f"xa{L}"]
                step(residual(former))
                rms_norm(f"xq{L}", X)
                xt_low(f"xq{L}", XTH, XTL, f"norm_q{L}")
                dve.wait_ge(sem("mem_loaded"), 16 * (L + 1))
                rms_norm(f"xkv{L}", MEM)
                low(u0 + 1)
                low(u0 + 2)
                xt_low(f"xkv{L}", MTH, MTL, f"norm_kv{L}")
                for i in range(3, 9):
                    low(u0 + i)
                head_norm(8, ACT0[f"xa{L}"], True, lambda i: F[:, 2 * i:2 * i + 2, :],
                          lambda i, e: col(f"xq_gain{L}" if i < 4 else f"xk_gain{L}", e), False,
                          lambda i: low(u0 + 9 + i // 2) if i % 2 == 0 else None)
                attention(f"xa{L}")
                out_product(f"xa{L}", u0 + 12)

            def gla():
                step(residual("ffn1"))
                rms_norm("gla", X)
                u0 = U0["gla"]
                xt_low("gla", XTH, XTL, "norm_mix1")
                v.memset(flat(20, 24), 0.0)
                for i in range(1, 6):
                    low(u0 + i)
                dve.wait_ge(sem("gl_ready"), 1)
                step(stt(GE, GB, 0.0, GE, ALU.min, ALU.subtract))
                step(v.tensor_scalar(GE, GE, 1.0 / 16.0, None, ALU.mult))
                for lo in (0, 512):
                    ins = v.tensor_tensor_scan(GB[:, lo:lo + 512], keep, GE[:, lo:lo + 512], 0.0, ALU.mult, ALU.add)
                signal(ins, "gscan_ready")
                low(u0 + 6)
                dve.wait_ge(sem("gexp_ready"), 1)
                chunks = lambda x: x.rearrange("p (x n) -> p x n", n=CH)
                tiles4 = lambda x: x.rearrange("p (h n) -> p h n", h=4)
                v.tensor_copy(TINY[:, 80:96].rearrange("p (x o) -> p x o", o=1), chunks(GE)[:, :, CH - 1:CH])
                signal(stt(F[:, 0:4, :], F[:, 0:4, :], 128 ** -0.5, tiles4(GE), ALU.mult, ALU.mult), "gexp_used")
                signal(v.tensor_tensor(chunks(KS), chunks(GB)[:, :, CH - 1:CH].to_broadcast([P, 16, CH]), chunks(GB),
                                       ALU.subtract), "glast_ready")
                low(u0 + 7)
                low(u0 + 8)
                dve.wait_ge(sem("gexp_ready"), 3)
                step(v.tensor_tensor(tiles4(KS), tiles4(KS), F[:, 4:8, :], ALU.mult))
                signal(v.tensor_tensor(F[:, 4:8, :], F[:, 4:8, :], tiles4(GE), ALU.mult), "gla_factors")
                signal(v.memset(GS, 0.0), "gs_ready")
                for i in range(9, 13):
                    low(u0 + i)
                dve.wait_ge(sem("att_psum"), 1)
                incl = strict_incl[:, P:2 * P].bitcast(i32).unsqueeze(1).to_broadcast([P, 4, P])
                att = flat(20, 24).rearrange("p (x n) -> p x n", n=P)
                for b in range(2):
                    ins = v.copy_predicated(att[:, 4 * b:4 * b + 4, :], incl,
                                            bank[4 + b][:, :].rearrange("p (x n) -> p x n", n=P))
                signal(ins, "att_ready")
                for c in range(NCH):
                    dve.wait_ge(sem("ds_psum"), c + 1)
                    for h in range(4):
                        ins = stt(GS[:, h, :], GS[:, h, :], TINY[:, 80 + 4 * h + c:81 + 4 * h + c],
                                  half(2 + h // 2)[:, h % 2, :], ALU.mult, ALU.add)
                    signal(ins, "gs_ready")
                dve.wait_ge(sem("go_taken"), NCH)
                head_norm(4, 0, None, lambda i: OT[:, 2 * i:2 * i + 2, :], lambda i, e: col("o_gain", 2 * i + e), False)
                dve.wait_ge(sem("proj_taken"), ACT0["gla"] + 12)
                signal(v.tensor_tensor(OT[:, 0:8, :], OT[:, 0:8, :], F[:, 8:16, :], ALU.mult), "gla_done")
                out_product("gla", u0 + 12)

            signal(v.memset(TINY[:, 0:128], 0.0), "hidden_ready")
            signal(v.memset(TINY[:, 128:256], 0.0), "hidden_ready")
            low(0)
            mix(0)
            layer_norm(0, "mix0")
            xt_low("ffn0", XTH, XTL)
            ffn("ffn0")
            layer_norm(1, "ffn0")
            mix(1)
            layer_norm(2, "mix1")
            xt_low("moe", XTH, XTL)
            moe()
            layer_norm(3, "moe")
            ev()
            xa(0, "ev")
            step(residual("xa0"))
            rms_norm("ffn1", X)
            xt_low("ffn1", XTH, XTL, "norm_ffn0")
            ffn("ffn1")
            gla()
            xa(1, "gla")
            step(residual("xa1"))
            rms_norm("ffn2", X)
            xt_low("ffn2", XTH, XTL, "norm_ffn1")
            ffn("ffn2")
            residual("ffn2").then_inc(sem("x_final"), 1)


def kernel(**inputs):
    import concourse.bacc as _bacc
    from concourse import mybir as _mybir
    from concourse.bass_utils import run_bass_kernel_spmd as _run

    def tiles(v):
        return np.asarray(v).reshape(-1, P).T

    cols = np.zeros((P, NCOLS), np.float32)

    def put(name, block):
        cols[:, _AT[name]:_AT[name] + block.shape[1]] = block

    for L in range(DEPTH):
        for name, key in (("mu", "rwkv_mu"), ("w0", "rwkv_w0"), ("a0", "rwkv_a0"), ("k_k", "rwkv_k_k"), ("k_a", "rwkv_k_a"),
                          ("r_k", "rwkv_r_k"), ("gn_g", "rwkv_gn_g"), ("gn_b", "rwkv_gn_b"), ("gate", "gate_bias"),
                          ("norm_mix", "norm_mix_2"), ("norm_q", "norm_mem_q_2"), ("norm_kv", "norm_mem_kv_2"),
                          ("norm_ffn", "norm_ffn_2"), ("xq_gain", "xa_q_gain_2"), ("xk_gain", "xa_k_gain_2")):
            put(f"{name}{L}", tiles(inputs[key][L]))
    for name, key in (("q_gain", "ev_q_gain_2"), ("k_gain", "ev_k_gain_2")):
        put(name, tiles(np.concatenate([np.asarray(inputs[key][0])] * 2)))
    put("b_g", tiles(inputs["od_b_g_2"][0]))
    put("o_gain", tiles(inputs["od_o_gain_2"][0]))
    inv = np.zeros((P, 1), np.float32)
    for base in (0, HD):
        for i in range(8):
            inv[base + i] = inv[base + 8 + i] = np.float32(500000.0) ** np.float32(-i * 2.0 / 16)
    put("inv_freq", inv)
    for name, value in (("eps_ln", LN_EPS), ("eps_rms", RMS_EPS), ("eps_gn", GN_EPS), ("eps_kk", 1e-12),
                        ("half_pi", np.pi / 2)):
        put(name, np.full((P, 1), value, np.float32))

    arrays = {"x": np.asarray(inputs["x"])[0], "mem_2": np.asarray(inputs["mem_2"])[0], "cols": cols,
              "consts": shape_constants(),
              "srow": np.concatenate([np.asarray(inputs["swa_sinks"]).reshape(-1), np.asarray(inputs["fox_f_bias"]).reshape(-1),
                                      np.asarray(inputs["router_b"]).reshape(-1)])}
    for name in ("w_in", "rwkv_w_up", "rwkv_a_up", "rwkv_g_up", "w_branch", "w_out", "ln_g", "ln_b", "ffn_w1", "ffn_w3",
                 "ffn_w2", "router_w", "exp_w1", "exp_w3", "exp_w2", "positions_2", "ev_w_in_2", "ev_w_s_2", "ev_b_s_2",
                 "ev_ln_g_2", "ev_ln_b_2", "ev_w_out_2", "od_w_in_2", "od_w_g1_2", "od_w_g2_2", "od_w_out_2", "xa_w_q_2",
                 "xa_w_kv_2", "xa_w_out_2", "ffn_w_gu_2", "ffn_w_down_2"):
        arrays[name] = np.asarray(inputs[name])

    nc = _bacc.Bacc("TRN2", target_bir_lowering=False, num_devices=1)
    arrays = {f"in_{n}": np.ascontiguousarray(v) for n, v in arrays.items()}
    aps = {n[3:]: nc.dram_tensor(n, v.shape, _mybir.dt.from_np(v.dtype), kind="ExternalInput").ap()
           for n, v in arrays.items()}
    out = nc.dram_tensor("out_x", (S, D), _mybir.dt.float32, kind="ExternalOutput").ap()
    program(nc, aps, out)
    r = _run(nc, [arrays], core_ids=[0])
    return r.results[0]["out_x"].reshape(1, S, D)
```
